# Optimizing a Trainium2 kernel written in Bass

```python
import jax
import jax.numpy as jnp
from jax import lax
import numpy as np
import jax, jax.numpy as jnp

D_MODEL = 1024
BATCH = 1
SEQ = 512
DEPTH = 2

N_META = 16
N_MIXERS = 3
CHUNK = 64
LEAD_PAD = (-N_META) % CHUNK
RMS_EPS = 1e-6
D_FF = 4 * D_MODEL

GDN_QK_HEADS = 8
GDN_V_HEADS = 16
GDN_HEAD_DIM = 128
GDN_CONV = 4
GDN_QK_DIM = GDN_QK_HEADS * GDN_HEAD_DIM
GDN_V_DIM = GDN_V_HEADS * GDN_HEAD_DIM
GDN_CONV_DIM = 2 * GDN_QK_DIM + GDN_V_DIM
GDN_IN = GDN_CONV_DIM + GDN_V_DIM + 2 * GDN_V_HEADS

MLSTM_HEADS = 8
MLSTM_QK_DIM = D_MODEL // 2
MLSTM_V_DIM = D_MODEL
MLSTM_DQK = MLSTM_QK_DIM // MLSTM_HEADS
MLSTM_DV = MLSTM_V_DIM // MLSTM_HEADS
MLSTM_IN = 2 * MLSTM_QK_DIM + 2 * MLSTM_V_DIM + 2 * MLSTM_HEADS
GATE_SOFTCAP = 15.0

MLA_HEADS = 16
MLA_NOPE = 64
MLA_ROPE = 32
MLA_QK = MLA_NOPE + MLA_ROPE
MLA_V = 64
MLA_Q_RANK = 384
MLA_KV_RANK = 256
MLA_IN = MLA_Q_RANK + MLA_KV_RANK + MLA_ROPE
ROPE_THETA = 10000.0
Q_BLOCK = 128

N_GDN_LAYERS = len(range(0, DEPTH, N_MIXERS))
N_MLSTM_LAYERS = len(range(1, DEPTH, N_MIXERS))
N_MLA_LAYERS = len(range(2, DEPTH, N_MIXERS))


def rms_norm(x, w):
    xf = x.astype(jnp.float32)
    y = xf * lax.rsqrt(jnp.mean(xf * xf, axis=-1, keepdims=True) + RMS_EPS)
    return (y * w.astype(jnp.float32)).astype(x.dtype)

def l2_norm(x):
    xf = x.astype(jnp.float32)
    return xf * lax.rsqrt(jnp.sum(xf * xf, axis=-1, keepdims=True) + RMS_EPS)

def to_chunks(x, pad_value=0.0):
    widths = [(0, 0), (LEAD_PAD, 0)] + [(0, 0)] * (x.ndim - 2)
    x = jnp.pad(x, widths, constant_values=pad_value)
    b, tp = x.shape[:2]
    x = x.reshape((b, tp // CHUNK, CHUNK) + x.shape[2:])
    return jnp.moveaxis(x, 3, 1)

def from_chunks(x):
    b, nh, n, c, d = x.shape
    x = jnp.moveaxis(x, 1, 3).reshape(b, n * c, nh, d)
    return x[:, LEAD_PAD:]

def causal_conv_silu(x, w):
    k, c = w.shape
    y = lax.conv_general_dilated(x, w[:, None, :].astype(x.dtype), window_strides=(1,),
                                 padding=[(k - 1, 0)], dimension_numbers=('NWC', 'WIO', 'NWC'),
                                 feature_group_count=c)
    return jax.nn.silu(y)

def chunk_gated_delta_rule(q, k, v, g, beta):
    q, k, v = to_chunks(q), to_chunks(k), to_chunks(v)
    g, beta = to_chunks(g), to_chunks(beta)
    dv = v.shape[-1]
    causal = jnp.tril(jnp.ones((CHUNK, CHUNK), dtype=bool))
    strict = jnp.tril(jnp.ones((CHUNK, CHUNK), dtype=bool), k=-1)
    cum = jnp.cumsum(g, axis=-1)
    decay = jnp.exp(jnp.where(causal, cum[..., :, None] - cum[..., None, :], -jnp.inf))
    k_beta = k * beta[..., None]
    a = jnp.where(strict, jnp.einsum('bhnid,bhnjd->bhnij', k_beta, k) * decay, 0.0)
    eye = jnp.eye(CHUNK, dtype=a.dtype)
    rhs = jnp.concatenate([v * beta[..., None], k_beta * jnp.exp(cum)[..., None]], axis=-1)
    sol = lax.linalg.triangular_solve(a + eye, rhs, left_side=True, lower=True, unit_diagonal=True)
    u, w = sol[..., :dv], sol[..., dv:]
    attn = jnp.einsum('bhnid,bhnjd->bhnij', q, k) * decay
    q_dec = q * jnp.exp(cum)[..., None]
    k_dec = k * jnp.exp(cum[..., -1:] - cum)[..., None]
    last = jnp.exp(cum[..., -1])

    def step(state, xs):
        u_c, w_c, q_c, k_c, attn_c, last_c = xs
        v_new = u_c - jnp.einsum('bhck,bhkv->bhcv', w_c, state)
        o = jnp.einsum('bhck,bhkv->bhcv', q_c, state) + jnp.einsum('bhij,bhjv->bhiv', attn_c, v_new)
        state = state * last_c[..., None, None] + jnp.einsum('bhck,bhcv->bhkv', k_c, v_new)
        return state, o

    xs = tuple(jnp.moveaxis(t, 2, 0) for t in (u, w, q_dec, k_dec, attn, last))
    b, nh = q.shape[:2]
    state0 = jnp.zeros((b, nh, q.shape[-1], dv), jnp.float32)
    _, o = lax.scan(step, state0, xs)
    return from_chunks(jnp.moveaxis(o, 0, 2))

def gated_deltanet(h, w_in, w_conv, a_log, dt_bias, w_norm, w_out):
    b, t, _ = h.shape
    proj = h @ w_in
    qkv, z, beta_pre, a_pre = jnp.split(
        proj, [GDN_CONV_DIM, GDN_CONV_DIM + GDN_V_DIM, GDN_CONV_DIM + GDN_V_DIM + GDN_V_HEADS], axis=-1)
    qkv = causal_conv_silu(qkv, w_conv)
    q, k, v = jnp.split(qkv, [GDN_QK_DIM, 2 * GDN_QK_DIM], axis=-1)
    rep = GDN_V_HEADS // GDN_QK_HEADS
    q = l2_norm(q.reshape(b, t, GDN_QK_HEADS, GDN_HEAD_DIM)) * (GDN_HEAD_DIM ** -0.5)
    k = l2_norm(k.reshape(b, t, GDN_QK_HEADS, GDN_HEAD_DIM))
    q = jnp.repeat(q, rep, axis=2)
    k = jnp.repeat(k, rep, axis=2)
    v = v.reshape(b, t, GDN_V_HEADS, GDN_HEAD_DIM).astype(jnp.float32)
    beta = jax.nn.sigmoid(beta_pre.astype(jnp.float32))
    g = -jnp.exp(a_log.astype(jnp.float32)) * jax.nn.softplus(a_pre.astype(jnp.float32) + dt_bias.astype(jnp.float32))
    o = chunk_gated_delta_rule(q, k, v, g, beta)
    o = rms_norm(o, w_norm) * jax.nn.silu(z.reshape(b, t, GDN_V_HEADS, GDN_HEAD_DIM).astype(jnp.float32))
    return o.reshape(b, t, GDN_V_DIM).astype(h.dtype) @ w_out

def chunk_mlstm(q, k, v, i_pre, log_f):
    q, k, v = to_chunks(q), to_chunks(k), to_chunks(v)
    i_pre = to_chunks(i_pre, -jnp.inf)
    log_f = to_chunks(log_f)
    causal = jnp.tril(jnp.ones((CHUNK, CHUNK), dtype=bool))
    cum = jnp.cumsum(log_f, axis=-1)
    log_w = jnp.where(causal, cum[..., :, None] - cum[..., None, :] + i_pre[..., None, :], -jnp.inf)
    log_w_end = cum[..., -1:] - cum + i_pre
    qk = jnp.einsum('bhnid,bhnjd->bhnij', q, k)

    def step(carry, xs):
        c_mat, n_vec, m = carry
        q_c, k_c, v_c, cum_c, lw_c, lwe_c, qk_c = xs
        log_inter = cum_c + m[..., None]
        m_row = jnp.maximum(log_inter, jnp.max(lw_c, axis=-1))
        s_inter = jnp.exp(log_inter - m_row)
        w_intra = jnp.exp(lw_c - m_row[..., None]) * qk_c
        num = s_inter[..., None] * jnp.einsum('bhck,bhkv->bhcv', q_c, c_mat) \
            + jnp.einsum('bhij,bhjv->bhiv', w_intra, v_c)
        den = s_inter * jnp.einsum('bhck,bhk->bhc', q_c, n_vec) + jnp.sum(w_intra, axis=-1)
        h_c = num / jnp.maximum(jnp.abs(den), jnp.exp(-m_row))[..., None]
        log_keep = cum_c[..., -1] + m
        m_new = jnp.maximum(log_keep, jnp.max(lwe_c, axis=-1))
        s_keep = jnp.exp(log_keep - m_new)
        w_end = jnp.exp(lwe_c - m_new[..., None])
        c_mat = s_keep[..., None, None] * c_mat + jnp.einsum('bhc,bhck,bhcv->bhkv', w_end, k_c, v_c)
        n_vec = s_keep[..., None] * n_vec + jnp.einsum('bhc,bhck->bhk', w_end, k_c)
        return (c_mat, n_vec, m_new), h_c

    xs = tuple(jnp.moveaxis(t, 2, 0) for t in (q, k, v, cum, log_w, log_w_end, qk))
    b, nh, _, _, dk = q.shape
    dv = v.shape[-1]
    carry0 = (jnp.zeros((b, nh, dk, dv), jnp.float32), jnp.zeros((b, nh, dk), jnp.float32),
              jnp.zeros((b, nh), jnp.float32))
    _, hs = lax.scan(step, carry0, xs)
    return from_chunks(jnp.moveaxis(hs, 0, 2))

def mlstm(h, w_in, gate_bias, w_norm, w_out):
    b, t, _ = h.shape
    q, k, v, o, gates = jnp.split(
        h @ w_in, [MLSTM_QK_DIM, 2 * MLSTM_QK_DIM, 2 * MLSTM_QK_DIM + MLSTM_V_DIM,
                   2 * MLSTM_QK_DIM + 2 * MLSTM_V_DIM], axis=-1)
    q = q.reshape(b, t, MLSTM_HEADS, MLSTM_DQK).astype(jnp.float32)
    k = k.reshape(b, t, MLSTM_HEADS, MLSTM_DQK).astype(jnp.float32) * (MLSTM_DQK ** -0.5)
    v = v.reshape(b, t, MLSTM_HEADS, MLSTM_DV).astype(jnp.float32)
    gates = gates.astype(jnp.float32) + gate_bias.astype(jnp.float32)
    gates = GATE_SOFTCAP * jnp.tanh(gates / GATE_SOFTCAP)
    i_pre, f_pre = gates[..., :MLSTM_HEADS], gates[..., MLSTM_HEADS:]
    hs = chunk_mlstm(q, k, v, i_pre, jax.nn.log_sigmoid(f_pre))
    hs = rms_norm(hs, w_norm.reshape(MLSTM_HEADS, MLSTM_DV)) \
        * jax.nn.sigmoid(o.reshape(b, t, MLSTM_HEADS, MLSTM_DV).astype(jnp.float32))
    return hs.reshape(b, t, MLSTM_V_DIM).astype(h.dtype) @ w_out

def rope_tables(t):
    pos = jnp.arange(t, dtype=jnp.float32)
    inv_freq = ROPE_THETA ** (-jnp.arange(0, MLA_ROPE, 2, dtype=jnp.float32) / MLA_ROPE)
    ang = pos[:, None] * inv_freq[None, :]
    return jnp.cos(ang), jnp.sin(ang)

def apply_rope(x, cos, sin):
    x_pass, x_rot = x[..., :MLA_NOPE], x[..., MLA_NOPE:]
    x1, x2 = x_rot[..., :MLA_ROPE // 2], x_rot[..., MLA_ROPE // 2:]
    c = cos[None, :, None, :].astype(x.dtype)
    s = sin[None, :, None, :].astype(x.dtype)
    return jnp.concatenate([x_pass, x1 * c - x2 * s, x2 * c + x1 * s], axis=-1)

def causal_block_attention(q, k, v):
    b, t, nh, dq = q.shape
    dv = v.shape[-1]
    n_blk = -(-t // Q_BLOCK)
    qp = jnp.pad(q, ((0, 0), (0, n_blk * Q_BLOCK - t), (0, 0), (0, 0)))
    scale = dq ** -0.5
    k_pos = jnp.arange(t)

    def one_block(i):
        start = i * Q_BLOCK
        qb = lax.dynamic_slice_in_dim(qp, start, Q_BLOCK, axis=1)
        s = jnp.einsum('bqhd,bkhd->bhqk', qb, k).astype(jnp.float32) * scale
        q_pos = start + jnp.arange(Q_BLOCK)
        s = jnp.where(k_pos[None, :] <= q_pos[:, None], s, -jnp.inf)
        p = jax.nn.softmax(s, axis=-1).astype(v.dtype)
        return jnp.einsum('bhqk,bkhd->bqhd', p, v)

    o = lax.map(one_block, jnp.arange(n_blk))
    return jnp.moveaxis(o, 0, 1).reshape(b, n_blk * Q_BLOCK, nh, dv)[:, :t]

def mla(h, w_in, q_norm, w_uq, kv_norm, w_ukv, q_head_norm, k_head_norm, w_out):
    b, t, _ = h.shape
    c_q, c_kv, k_rope = jnp.split(h @ w_in, [MLA_Q_RANK, MLA_Q_RANK + MLA_KV_RANK], axis=-1)
    q = (rms_norm(c_q, q_norm) @ w_uq).reshape(b, t, MLA_HEADS, MLA_QK)
    kv = (rms_norm(c_kv, kv_norm) @ w_ukv).reshape(b, t, MLA_HEADS, MLA_NOPE + MLA_V)
    k_nope, v = kv[..., :MLA_NOPE], kv[..., MLA_NOPE:]
    k_rope = jnp.broadcast_to(k_rope[:, :, None, :], (b, t, MLA_HEADS, MLA_ROPE))
    k = jnp.concatenate([k_nope, k_rope], axis=-1)
    cos, sin = rope_tables(t)
    q = apply_rope(rms_norm(q, q_head_norm), cos, sin)
    k = apply_rope(rms_norm(k, k_head_norm), cos, sin)
    o = causal_block_attention(q, k, v)
    return o.reshape(b, t, MLA_HEADS * MLA_V) @ w_out

def squared_relu_mlp(h, w_up, w_down):
    a = jax.nn.relu(h @ w_up)
    return (a * a) @ w_down

def first_inputs(seed: int = 0) -> dict:
    key = jax.random.key(seed)
    keys = iter(jax.random.split(key, 40))
    f32 = jnp.float32

    def dense(shape, fan_in):
        return jax.random.normal(next(keys), shape, f32) * (fan_in ** -0.5)

    def gain(shape):
        return 1.0 + 0.02 * jax.random.normal(next(keys), shape, f32)

    x = jax.random.normal(next(keys), (BATCH, SEQ, D_MODEL), f32)
    meta_tokens = jax.random.normal(next(keys), (N_META, D_MODEL), f32)
    attn_norm = gain((DEPTH, D_MODEL))
    ffn_norm = gain((DEPTH, D_MODEL))
    ff_up = dense((DEPTH, D_MODEL, D_FF), D_MODEL)
    ff_down = dense((DEPTH, D_FF, D_MODEL), D_FF)
    gdn_in = dense((N_GDN_LAYERS, D_MODEL, GDN_IN), D_MODEL)
    gdn_conv = dense((N_GDN_LAYERS, GDN_CONV, GDN_CONV_DIM), GDN_CONV)
    gdn_a_log = jnp.log(jax.random.uniform(next(keys), (N_GDN_LAYERS, GDN_V_HEADS), f32, 1.0, 16.0))
    dt = jnp.exp(jax.random.uniform(next(keys), (N_GDN_LAYERS, GDN_V_HEADS), f32,
                                    np.float32(np.log(1e-3)), np.float32(np.log(1e-1))))
    gdn_dt_bias = dt + jnp.log(-jnp.expm1(-dt))
    gdn_norm = gain((N_GDN_LAYERS, GDN_HEAD_DIM))
    gdn_out = dense((N_GDN_LAYERS, GDN_V_DIM, D_MODEL), GDN_V_DIM)
    mlstm_in = dense((N_MLSTM_LAYERS, D_MODEL, MLSTM_IN), D_MODEL)
    ig_bias = 0.1 * jax.random.normal(next(keys), (N_MLSTM_LAYERS, MLSTM_HEADS), f32)
    fg_bias = jnp.linspace(3.0, 6.0, MLSTM_HEADS, dtype=f32)[None, :] \
        + 0.1 * jax.random.normal(next(keys), (N_MLSTM_LAYERS, MLSTM_HEADS), f32)
    mlstm_gate_bias = jnp.concatenate([ig_bias, fg_bias], axis=-1)
    mlstm_norm = gain((N_MLSTM_LAYERS, MLSTM_V_DIM))
    mlstm_out = dense((N_MLSTM_LAYERS, MLSTM_V_DIM, D_MODEL), MLSTM_V_DIM)
    mla_in = dense((N_MLA_LAYERS, D_MODEL, MLA_IN), D_MODEL)
    mla_q_norm = gain((N_MLA_LAYERS, MLA_Q_RANK))
    mla_uq = dense((N_MLA_LAYERS, MLA_Q_RANK, MLA_HEADS * MLA_QK), MLA_Q_RANK)
    mla_kv_norm = gain((N_MLA_LAYERS, MLA_KV_RANK))
    mla_ukv = dense((N_MLA_LAYERS, MLA_KV_RANK, MLA_HEADS * (MLA_NOPE + MLA_V)), MLA_KV_RANK)
    mla_q_head_norm = gain((N_MLA_LAYERS, MLA_QK))
    mla_k_head_norm = gain((N_MLA_LAYERS, MLA_QK))
    mla_out = dense((N_MLA_LAYERS, MLA_HEADS * MLA_V, D_MODEL), MLA_HEADS * MLA_V)
    return {'x': x, 'meta_tokens': meta_tokens, 'attn_norm': attn_norm, 'ffn_norm': ffn_norm,
            'ff_up': ff_up, 'ff_down': ff_down,
            'gdn_in': gdn_in, 'gdn_conv': gdn_conv, 'gdn_a_log': gdn_a_log, 'gdn_dt_bias': gdn_dt_bias,
            'gdn_norm': gdn_norm, 'gdn_out': gdn_out,
            'mlstm_in': mlstm_in, 'mlstm_gate_bias': mlstm_gate_bias, 'mlstm_norm': mlstm_norm,
            'mlstm_out': mlstm_out,
            'mla_in': mla_in, 'mla_q_norm': mla_q_norm, 'mla_uq': mla_uq, 'mla_kv_norm': mla_kv_norm,
            'mla_ukv': mla_ukv, 'mla_q_head_norm': mla_q_head_norm, 'mla_k_head_norm': mla_k_head_norm,
            'mla_out': mla_out}

def first_block(x, meta_tokens, attn_norm, ffn_norm, ff_up, ff_down,
              gdn_in, gdn_conv, gdn_a_log, gdn_dt_bias, gdn_norm, gdn_out,
              mlstm_in, mlstm_gate_bias, mlstm_norm, mlstm_out,
              mla_in, mla_q_norm, mla_uq, mla_kv_norm, mla_ukv, mla_q_head_norm, mla_k_head_norm,
              mla_out):
    b = x.shape[0]
    meta = jnp.broadcast_to(meta_tokens[None].astype(x.dtype), (b, N_META, x.shape[-1]))
    h = jnp.concatenate([meta, x], axis=1)
    for layer in range(DEPTH):
        kind, j = layer % N_MIXERS, layer // N_MIXERS
        hn = rms_norm(h, attn_norm[layer])
        if kind == 0:
            mix = gated_deltanet(hn, gdn_in[j], gdn_conv[j], gdn_a_log[j], gdn_dt_bias[j],
                                 gdn_norm[j], gdn_out[j])
        elif kind == 1:
            mix = mlstm(hn, mlstm_in[j], mlstm_gate_bias[j], mlstm_norm[j], mlstm_out[j])
        else:
            mix = mla(hn, mla_in[j], mla_q_norm[j], mla_uq[j], mla_kv_norm[j], mla_ukv[j],
                      mla_q_head_norm[j], mla_k_head_norm[j], mla_out[j])
        h = h + mix
        h = h + squared_relu_mlp(rms_norm(h, ffn_norm[layer]), ff_up[layer], ff_down[layer])
    return h[:, N_META:]


DEPTH_2 = 1

NORM_EPS = 1e-6
MASK_VALUE = -1e30
TINY = 1e-30

MIX_WIDTH = D_MODEL
HGRN_HEADS = 4
HGRN_WIDTH = MIX_WIDTH // 4
HGRN_KEY_DIM = HGRN_WIDTH // HGRN_HEADS
HGRN_VAL_DIM = HGRN_WIDTH // HGRN_HEADS
POOL_WINDOWS = (2, 4, 8, 16)
POOL_GROUPS = len(POOL_WINDOWS)
POOL_WIDTH = MIX_WIDTH // 4
POOL_GROUP_DIM = POOL_WIDTH // POOL_GROUPS
FOX_HEADS = 8
FOX_WIDTH = MIX_WIDTH // 2
FOX_HEAD_DIM = FOX_WIDTH // FOX_HEADS

IN_WIDTHS = (HGRN_WIDTH, HGRN_WIDTH, HGRN_WIDTH, HGRN_WIDTH,
             POOL_WIDTH, POOL_WIDTH,
             FOX_WIDTH, FOX_WIDTH, FOX_WIDTH, FOX_WIDTH, FOX_HEADS)
IN_WIDTH = int(sum(IN_WIDTHS))
IN_SPLIT_POINTS = tuple(int(v) for v in np.cumsum(IN_WIDTHS)[:-1])


def _rmsnorm(x, g):
    xf = x.astype(jnp.float32)
    y = xf * lax.rsqrt(jnp.mean(xf * xf, axis=-1, keepdims=True) + NORM_EPS)
    return (y * g.astype(jnp.float32)).astype(x.dtype)

def _hgrn2_chunkwise(q, k, v, log_f):
    B, T, H, dk = q.shape
    dv = v.shape[-1]
    n = T // CHUNK

    def to_chunks(a):
        return a.astype(jnp.float32).reshape(B, n, CHUNK, H, a.shape[-1]).transpose(1, 0, 3, 2, 4)

    qc, kc, vc, gc = to_chunks(q), to_chunks(k), to_chunks(v), to_chunks(log_f)
    pos = jnp.arange(CHUNK)
    causal = (pos[:, None] >= pos[None, :])[:, :, None]
    causal_f = causal.astype(jnp.float32)

    def step(S, inp):
        qi, ki, vi, gi = inp
        b = jnp.cumsum(gi, axis=2)
        diff = b[:, :, :, None, :] - b[:, :, None, :, :]
        decay = jnp.exp(jnp.where(causal, diff, 0.0)) * causal_f
        attn = jnp.einsum('bhtd,bhsd,bhtsd->bhts', qi, ki, decay)
        o = (jnp.einsum('bhts,bhsv->bhtv', attn, vi)
             + jnp.einsum('bhtd,bhdv->bhtv', qi * jnp.exp(b), S))
        b_last = b[:, :, -1, :]
        S = (jnp.exp(b_last)[..., None] * S
             + jnp.einsum('bhsd,bhsv->bhdv', ki * jnp.exp(b_last[:, :, None, :] - b), vi))
        return S, o

    S0 = jnp.zeros((B, H, dk, dv), jnp.float32)
    _, o = lax.scan(step, S0, (qc, kc, vc, gc))
    return o.transpose(1, 0, 3, 2, 4).reshape(B, T, H, dv)

def _multiscale_pool(u):
    B, T, _ = u.shape
    uf = u.astype(jnp.float32).reshape(B, T, POOL_GROUPS, POOL_GROUP_DIM)
    cs = jnp.pad(jnp.cumsum(uf, axis=1), ((0, 0), (1, 0), (0, 0), (0, 0)))
    t = jnp.arange(T, dtype=jnp.float32)
    outs = []
    for g, w in enumerate(POOL_WINDOWS):
        c = cs[:, :, g]
        upper = c[:, 1:]
        lower = jnp.pad(c[:, :T + 1 - w], ((0, 0), (w - 1, 0), (0, 0)))
        count = jnp.minimum(t + 1.0, float(w))[None, :, None]
        outs.append((upper - lower) / count - uf[:, :, g])
    return jnp.stack(outs, axis=2)

def _forgetting_attention(q, k, v, log_f):
    B, T, H, D = q.shape
    c = jnp.cumsum(log_f, axis=1).transpose(0, 2, 1)
    scale = D ** -0.5
    outs = []
    for i in range(T // Q_BLOCK):
        q0, q1 = i * Q_BLOCK, (i + 1) * Q_BLOCK
        s = jnp.einsum('bqhd,bkhd->bhqk', q[:, q0:q1], k[:, :q1]).astype(jnp.float32) * scale
        mask = (q0 + jnp.arange(Q_BLOCK))[:, None] >= jnp.arange(q1)[None, :]
        bias = jnp.where(mask, c[:, :, q0:q1, None] - c[:, :, None, :q1], 0.0)
        p = jax.nn.softmax(jnp.where(mask, s + bias, MASK_VALUE), axis=-1)
        outs.append(jnp.einsum('bhqk,bkhd->bqhd', p.astype(v.dtype), v[:, :q1]))
    return jnp.concatenate(outs, axis=1)

def second_inputs(seed: int = 0) -> dict:
    key = jax.random.key(seed)
    ks = jax.random.split(key, 11)
    f32 = jnp.float32
    x = jax.random.normal(ks[0], (BATCH, SEQ, D_MODEL), f32)
    lower_bounds = jax.random.normal(ks[1], (DEPTH_2, HGRN_WIDTH), f32)
    pre_norm_g = 1.0 + 0.05 * jax.random.normal(ks[2], (DEPTH_2, D_MODEL), f32)
    w_in = jax.random.normal(ks[3], (DEPTH_2, D_MODEL, IN_WIDTH), f32) * D_MODEL ** -0.5
    hgrn_norm_g = 1.0 + 0.05 * jax.random.normal(ks[4], (DEPTH_2, HGRN_WIDTH), f32)
    fox_f_bias = jax.random.uniform(ks[5], (DEPTH_2, FOX_HEADS), f32, minval=1.0, maxval=4.0)
    pool_w = jax.random.normal(ks[6], (DEPTH_2, POOL_GROUPS, POOL_GROUP_DIM, POOL_GROUP_DIM), f32) * POOL_GROUP_DIM ** -0.5
    pool_scale = jax.random.uniform(ks[7], (DEPTH_2, POOL_WIDTH), f32, minval=0.5, maxval=1.5)
    w_out = jax.random.normal(ks[8], (DEPTH_2, MIX_WIDTH, D_MODEL), f32) * MIX_WIDTH ** -0.5
    post_norm_g = 1.0 + 0.05 * jax.random.normal(ks[9], (DEPTH_2, D_MODEL), f32)
    return {"x": x, "lower_bounds": lower_bounds, "pre_norm_g": pre_norm_g, "w_in": w_in,
            "hgrn_norm_g": hgrn_norm_g, "fox_f_bias": fox_f_bias, "pool_w": pool_w,
            "pool_scale": pool_scale, "w_out": w_out, "post_norm_g": post_norm_g}

def second_block(x, lower_bounds, pre_norm_g, w_in, hgrn_norm_g, fox_f_bias, pool_w, pool_scale, w_out, post_norm_g):
    B, T, _ = x.shape
    p = jax.nn.softmax(lower_bounds.astype(jnp.float32), axis=0)
    lbs = jnp.cumsum(p, axis=0) - p[0]
    for l in range(DEPTH_2):
        h = _rmsnorm(x, pre_norm_g[l])
        proj = jnp.einsum('btd,de->bte', h, w_in[l])
        q_a, f_a, i_a, g_a, u_b, g_b, q_c, k_c, v_c, g_c, f_c = jnp.split(proj, IN_SPLIT_POINTS, axis=-1)

        lb = lbs[l]
        z = f_a.astype(jnp.float32)
        f_gate = lb + (1.0 - lb) * jax.nn.sigmoid(z)
        log_f_a = jnp.log(jnp.maximum(f_gate, TINY))
        k_a = (1.0 - lb) * jax.nn.sigmoid(-z)
        hshape = (B, T, HGRN_HEADS, HGRN_KEY_DIM)
        o_a = _hgrn2_chunkwise(jax.nn.silu(q_a).reshape(hshape), k_a.reshape(hshape),
                               i_a.reshape(B, T, HGRN_HEADS, HGRN_VAL_DIM), log_f_a.reshape(hshape))
        o_a = _rmsnorm(o_a, hgrn_norm_g[l].reshape(HGRN_HEADS, HGRN_VAL_DIM)).reshape(B, T, HGRN_WIDTH)
        o_a = o_a.astype(x.dtype) * jax.nn.silu(g_a)

        pooled = _multiscale_pool(u_b)
        o_b = jnp.einsum('btgc,gcd->btgd', pooled, pool_w[l].astype(jnp.float32)).reshape(B, T, POOL_WIDTH)
        o_b = (o_b * pool_scale[l].astype(jnp.float32)).astype(x.dtype) * jax.nn.silu(g_b)

        log_f_c = jax.nn.log_sigmoid((f_c + fox_f_bias[l]).astype(jnp.float32))
        fshape = (B, T, FOX_HEADS, FOX_HEAD_DIM)
        o_c = _forgetting_attention(q_c.reshape(fshape), k_c.reshape(fshape), v_c.reshape(fshape), log_f_c)
        o_c = o_c.reshape(B, T, FOX_WIDTH).astype(x.dtype) * jax.nn.silu(g_c)

        mixed = jnp.concatenate([o_a, o_b, o_c], axis=-1)
        y = jnp.einsum('bte,ed->btd', mixed, w_out[l])
        x = x + _rmsnorm(y, post_norm_g[l])
    return x


def setup_inputs(seed=0):
    out = dict(first_inputs(seed))
    for name, value in second_inputs(seed + 1).items():
        if name != "x":
            out[name + "_2"] = value
    return out


def reference(
    x, meta_tokens, attn_norm, ffn_norm, ff_up, ff_down, gdn_in, gdn_conv, gdn_a_log,
    gdn_dt_bias, gdn_norm, gdn_out, mlstm_in, mlstm_gate_bias, mlstm_norm, mlstm_out, mla_in,
    mla_q_norm, mla_uq, mla_kv_norm, mla_ukv, mla_q_head_norm, mla_k_head_norm, mla_out,
    lower_bounds_2, pre_norm_g_2, w_in_2, hgrn_norm_g_2, fox_f_bias_2, pool_w_2, pool_scale_2,
    w_out_2, post_norm_g_2,
):
    x = first_block(
        x, meta_tokens, attn_norm, ffn_norm, ff_up, ff_down, gdn_in, gdn_conv, gdn_a_log,
        gdn_dt_bias, gdn_norm, gdn_out, mlstm_in, mlstm_gate_bias, mlstm_norm, mlstm_out,
        mla_in, mla_q_norm, mla_uq, mla_kv_norm, mla_ukv, mla_q_head_norm, mla_k_head_norm,
        mla_out,
    )
    return second_block(
        x, lower_bounds_2, pre_norm_g_2, w_in_2, hgrn_norm_g_2, fox_f_bias_2, pool_w_2,
        pool_scale_2, w_out_2, post_norm_g_2,
    )


_drawn_inputs = setup_inputs


def setup_inputs(seed=0):
    import zlib

    import numpy as np

    out = dict(_drawn_inputs(seed))
    spreads = {}
    factors = {'gdn_norm': 3.483,
     'mlstm_norm': 80.244,
     'hgrn_norm_g_2': 129.092,
     'ffn_norm': 2.74,
     'pre_norm_g_2': 4.117,
     'fox_f_bias_2': 4.411,
     'pool_scale_2': 5.191,
     'post_norm_g_2': 21.794}
    for name, (base, spread) in spreads.items():
        noise = np.random.default_rng([zlib.crc32(name.encode()), seed]).standard_normal(out[name].shape)
        drawn = base * np.exp(spread * noise) if base else spread * noise
        out[name] = jnp.asarray(drawn.astype(out[name].dtype))
    for name, factor in factors.items():
        out[name] = (out[name] * factor).astype(out[name].dtype)
    return out
```

```python
from contextlib import ExitStack, contextmanager

import concourse.bass as bass
from concourse import mybir

F32 = mybir.dt.float32
F32R = mybir.dt.float32r
U32 = mybir.dt.uint32
ALU = mybir.AluOpType
ACT = mybir.ActivationFunctionType
AX = mybir.AxisListType

P = 128
D = 1024
KD = D // P
META = 16
SEQ = 512
T = META + SEQ
HT = T // 2
CH = 128
NCH = SEQ // CH
EPS = 1e-6

RAW_SLOTS = 4
SPLIT_SLOTS = 2
UNIT = 2048
HALVES = (slice(0, HT), slice(HT, T))


class Named(dict):
    __getattr__ = dict.__getitem__


def chunks():
    return [(0, META)] + [(META + CH * c, CH) for c in range(NCH)]


def persistent(nc, ctx):
    k = Named(nc=nc)
    sb = lambda name, shape, dt=F32: ctx.enter_context(nc.sbuf_tensor(name, shape, dt))
    sem = lambda name: ctx.enter_context(nc.semaphore(name))
    k.stage_sems, k.last_sems, k.uncleared = ExitStack(), ExitStack(), []
    k.opened = []

    def stage_sem(name):
        k.opened.append(k.stage_sems.enter_context(nc.semaphore(name)))
        return k.opened[-1]
    k.sem = stage_sem
    k.h = sb("h", [P, KD, T])
    k.raw = sb("raw", [P, RAW_SLOTS, UNIT])
    k.ones = sb("ones", [P, P])
    k.ident = sb("ident", [P, P])
    k.eps = sb("eps", [P, 1])
    k.ps = [ctx.enter_context(nc.psum_tensor(f"ps{i}", [P, 2, 512], F32)) for i in range(4)]
    k.raw_landed = [sem(f"raw_landed{i}") for i in range(RAW_SLOTS)]
    k.hi_done = sem("hi_done")
    k.lo_done = sem("lo_done")
    k.tile_full = sem("tile_full")
    k.unit = 0
    k.tile = 0
    k.loaded = 0
    return k


@contextmanager
def stage(k):
    with k.nc.Block() as block:
        if k.uncleared:
            nums = sorted(x.num for x in k.uncleared)

            @block.sync
            def _(sp):
                first = prev = nums[0]
                for x in nums[1:] + [None]:
                    if x != prev + 1:
                        sp.sem_clear(range(first, prev + 1))
                        first = x
                    prev = x
        yield block
    k.last_sems.close()
    k.last_sems, k.stage_sems = k.stage_sems, ExitStack()
    k.uncleared, k.opened = k.opened, []



def tall(w, c0):
    return w.rearrange("(k p) n -> p k n", p=P)[:, :, bass.ds(c0, 256)]


def wide(w, r0, c0):
    return w[bass.ds(r0, 512), c0:c0 + 512].rearrange("(k p) n -> p k n", p=P)


def load_unit(k, sp, u, src, slot):
    if not (isinstance(u, int) and u < RAW_SLOTS):
        sp.wait_ge(k.lo_done, u - RAW_SLOTS + 1)
    kt = src.shape[1]
    dst = k.raw[:, slot, :].rearrange("p (k n) -> p k n", k=kt)
    sp.dma_start(dst, src).then_inc(k.raw_landed[slot], 16)


def load_ahead(k, sp, u0, srcs):
    for j, src in enumerate(srcs):
        load_unit(k, sp, u0 + j, src, (u0 + j) % RAW_SLOTS)
    k.loaded = len(srcs)


def landed_value(u, slot):
    return (u - slot) * (16 // RAW_SLOTS) + 16


def split_hi(k, act, u, slot, used):
    act.wait_ge(k.raw_landed[slot], landed_value(u, slot))
    if used is not None:
        act.wait_ge(k.tile_full, used)
    k.nc.scalar.copy(k.whi[:, slot % SPLIT_SLOTS, :], k.raw[:, slot, :]).then_inc(k.hi_done, 1)


def split_lo(k, eng, u, slot):
    eng.wait_ge(k.hi_done, u + 1)
    s = slot % SPLIT_SLOTS
    eng.tensor_tensor(k.wlo[:, s, :], k.raw[:, slot, :], k.whi[:, s, :].bitcast(F32),
                      ALU.subtract).then_inc(k.lo_done, 1)


def product(pe, ps, whi, wlo, xhi, xlo, first, last):
    for n, (w, x) in enumerate(((whi, xhi), (whi, xlo), (wlo, xhi))):
        for b, half in enumerate(HALVES):
            mm = pe.matmul(ps[:, b, 0:HT], w, x[:, half], start=first and n == 0, stop=last and n == 2)
    return mm


def halves(ps, n=P):
    return ps[0:n, :, 0:HT]


def two(ap):
    return ap.rearrange("p (b t) -> p b t", b=2)


def unit_tiles(k, pe, u, slot, kts, xhi, xlo, first_slot, tile_free, x_ready=None):
    pe.wait_ge(k.lo_done, u + 1)
    s = slot % SPLIT_SLOTS
    whi = k.whi[:, s, :].rearrange("p (k n) -> p k n", k=kts)
    wlo = k.wlo[:, s, :].rearrange("p (k n) -> p k n", k=kts)
    def one(m, kt):
        cols = slice(m * P, (m + 1) * P)
        return product(pe, k.ps[first_slot + m], whi[:, kt, cols], wlo[:, kt, cols], xhi[:, kt, :],
                       xlo[:, kt, :], kt == 0, kt == kts - 1)
    tiles = range(UNIT // kts // P)
    if x_ready is not None:
        for kt in range(kts):
            x_ready(kt)
            for m in tiles:
                mm = one(m, kt)
                if kt == kts - 1:
                    mm.then_inc(k.tile_full, 1)
        return
    for m in tiles:
        tile_free(m)
        for kt in range(kts):
            mm = one(m, kt)
        mm.then_inc(k.tile_full, 1)



def steps(eng, n, step, first, last):
    first()
    step(0, 0)
    loops = (n - 2) // 2 if n > 4 else 0
    if loops:
        with eng.Fori(0, loops) as i:
            step(i * 2 + 1, 1)
            step(i * 2 + 2, 0)
    for g in range(1 + 2 * loops, n - 1):
        step(g, g % 2)
    last()


def first_units(up_cols):
    return [up_cols(0, 0), up_cols(0, 1), up_cols(1, 0), up_cols(1, 1)]


def up_down(k, name, n, up_cols, w_down, activate, acc, acc_new, norm=None, then=()):
    nc = k.nc
    u0, t0, loaded = k.unit, k.tile, k.loaded
    norm = norm or NoNorm()
    with ExitStack() as ctx:
        sb = lambda nm, shape, dt=F32: ctx.enter_context(nc.sbuf_tensor(f"{name}_{nm}", shape, dt))
        ahi, alo = sb("ahi", [P, 2, 4, T], F32R), sb("alo", [P, 2, 4, T], F32R)
        k.a = sb("a", [P, 2, T])
        k.b = sb("b", [P, 2, T])
        s = Named(
            up_free=k.sem(f"{name}_up_free"), a_ready=k.sem(f"{name}_a_ready"),
            hi=k.sem(f"{name}_hi"), lo=k.sem(f"{name}_lo"), down_free=k.sem(f"{name}_down_free"))
        step_unit = lambda g: u0 + 2 + 4 * g
        step_tile = lambda g: t0 + 4 + 12 * g
        slot = lambda j: (u0 + 2 + j) % RAW_SLOTS
        up_tile = lambda g: t0 if isinstance(g, int) and g == 0 else step_tile(g - 1)
        def down_tile(g):
            return t0 + 12 * g + (4 if isinstance(g, int) and g == n - 1 else 8)
        norm.open(k, ctx)

        block = ctx.enter_context(stage(k))

        @block.sync
        def _(sp):
            def down(g, j):
                return wide(w_down, g * 512, 512 * j)
            norm.sync(k, sp)
            def first():
                for j in range(loaded, 2):
                    load_unit(k, sp, u0 + j, up_cols(0, j), (u0 + j) % RAW_SLOTS)
            def step(g, par):
                for j in range(2):
                    if not (isinstance(g, int) and g == 0 and 2 + j < loaded):
                        load_unit(k, sp, step_unit(g) + j, up_cols(g + 1, j), slot(j))
                for j in range(2):
                    load_unit(k, sp, step_unit(g) + 2 + j, down(g, j), slot(2 + j))
            def last():
                for j in range(2):
                    load_unit(k, sp, step_unit(n - 1) + j, down(n - 1, j), slot(j))
            steps(sp, n, step, first, last)
            load_ahead(k, sp, u0 + 4 * n, then)

        @block.scalar
        def _(act):
            def hi_tile(g, m, par):
                act.wait_ge(s.a_ready, 4 * g + m + 1)
                if not (isinstance(g, int) and g < 2):
                    if m == 0:
                        act.wait_ge(k.tile_full, down_tile_end(g - 2))
                nc.scalar.copy(ahi[:, par, m, :], k.a[:, m % 2, :]).then_inc(s.hi, 1)
            def down_tile_end(g):
                return t0 + 12 * g + 16
            def ups(g, par, tiles):
                for m in tiles:
                    if not (isinstance(g, int) and g == 0 and m < 2):
                        act.wait_ge(s.lo, 4 * g + m - 1)
                    act.wait_ge(k.tile_full, up_tile(g) + m + 1)
                    activate.act(k, act, s, g, m, k.ps[m])
                    hi_tile(g, m, par)
            def first():
                norm.act_sum(k, act)
                split_hi(k, act, u0, u0 % RAW_SLOTS, t0 if u0 else None)
                norm.act(k, act)
                split_hi(k, act, u0 + 1, (u0 + 1) % RAW_SLOTS, t0 if u0 else None)
                split_hi(k, act, u0 + 2, (u0 + 2) % RAW_SLOTS, t0 + 2)
                ups(0, 0, (0, 1))
                split_hi(k, act, u0 + 3, (u0 + 3) % RAW_SLOTS, t0 + 4)
                ups(0, 0, (2, 3))
            def step(g, par):
                split_hi(k, act, step_unit(g) + 2, slot(2), step_tile(g) + 2)
                ups(g + 1, 1 - par, (0, 1))
                split_hi(k, act, step_unit(g) + 3, slot(3), step_tile(g) + 4)
                ups(g + 1, 1 - par, (2, 3))
                split_hi(k, act, step_unit(g) + 4, slot(0), step_tile(g) + 8)
                split_hi(k, act, step_unit(g) + 5, slot(1), step_tile(g) + 12)
            def last():
                pass
            steps(act, n, step, first, last)

        @block.vector
        def _(dve):
            def lo_tile(g, m, par):
                dve.wait_ge(s.hi, 4 * g + m + 1)
                dve.tensor_tensor(alo[:, par, m, :], k.a[:, m % 2, :], ahi[:, par, m, :].bitcast(F32),
                                  ALU.subtract).then_inc(s.lo, 1)
            def ups(g, par, tiles):
                for m in tiles:
                    activate.dve(k, dve, s, g, m, k.ps[m])
                    lo_tile(g, m, par)
            def one_down(g, j):
                dve.wait_ge(k.tile_full, down_tile(g) + j + 1)
                if acc_new and isinstance(g, int) and g == 0:
                    dve.tensor_copy(two(acc[:, j, :]), halves(k.ps[j % 4])).then_inc(s.down_free, 1)
                    return
                if not (isinstance(g, int) and g == 0):
                    dve.wait_ge(s.down_free, 8 * g - 8 + j + 1)
                dve.tensor_tensor(two(acc[:, j, :]), two(acc[:, j, :]), halves(k.ps[j % 4]),
                                  ALU.add).then_inc(s.down_free, 1)
            def downs(g, tiles):
                for j in tiles:
                    one_down(g, j)
            def first():
                norm.dve_sum(k, dve)
                split_lo(k, dve, u0, u0 % RAW_SLOTS)
                norm.dve(k, dve)
                for j in range(1, 3):
                    split_lo(k, dve, u0 + j, (u0 + j) % RAW_SLOTS)
                ups(0, 0, (0, 1))
                split_lo(k, dve, u0 + 3, (u0 + 3) % RAW_SLOTS)
                ups(0, 0, (2, 3))
            def step(g, par):
                split_lo(k, dve, step_unit(g) + 2, slot(2))
                ups(g + 1, 1 - par, (0, 1))
                split_lo(k, dve, step_unit(g) + 3, slot(3))
                ups(g + 1, 1 - par, (2, 3))
                downs(g, range(4))
                split_lo(k, dve, step_unit(g) + 4, slot(0))
                downs(g, range(4, 8))
                split_lo(k, dve, step_unit(g) + 5, slot(1))
            def last():
                downs(n - 1, range(8))
            steps(dve, n, step, first, last)

        @block.tensor
        def _(pe):
            def up(g, ub, us, par, prev):
                for j in range(2):
                    def free(m, j=j):
                        if prev is not None:
                            prev(2 * j + m)
                    unit_tiles(k, pe, ub + j, us[j], 8, k.xhi, k.xlo, 2 * j, free,
                               norm.x_ready(k, pe) if prev is None and j == 0 else None)
            def down(g, ub, us, par, prev):
                pe.wait_ge(s.lo, 4 * g + 4)
                for j in range(2):
                    def free(m, j=j):
                        if j == 0:
                            prev(m)
                        else:
                            pe.wait_ge(s.down_free, 8 * g + m + 1)
                    unit_tiles(k, pe, ub + j, us[j], 4, ahi[:, par], alo[:, par], 0, free)
            def first():
                norm.pe(k, pe)
                up(0, u0, [(u0 + j) % RAW_SLOTS for j in range(2)], 0, None)
            def step(g, par):
                if isinstance(g, int) and g == 0:
                    freed = lambda m: pe.wait_ge(s.up_free, m + 1)
                else:
                    freed = lambda m: pe.wait_ge(s.down_free, 8 * g - 4 + m + 1)
                up(g + 1, step_unit(g), (slot(0), slot(1)), 1 - par, freed)
                down(g, step_unit(g) + 2, (slot(2), slot(3)), par,
                     lambda m: pe.wait_ge(s.up_free, 4 * g + 4 + m + 1))
            def last():
                down(n - 1, step_unit(n - 1), (slot(0), slot(1)), (n - 1) % 2,
                     lambda m: pe.wait_ge(s.down_free, 8 * n - 16 + 4 + m + 1))
            steps(pe, n, step, first, last)
    k.unit += 4 * n
    k.tile += 12 * n


class SquaredRelu:

    def act(self, k, act, s, g, m, ps):
        k.nc.scalar.activation(two(k.b[:, m % 2, :]), halves(ps), ACT.Relu).then_inc(s.up_free, 1)
        act.wait_ge(s.up_free, 4 * g + m + 1)
        k.nc.scalar.square(k.a[:, m % 2, :], k.b[:, m % 2, :]).then_inc(s.a_ready, 1)

    def dve(self, k, dve, s, g, m, ps):
        pass



class NoNorm:

    def open(self, k, ctx):
        pass

    def sync(self, k, sp):
        pass

    act_sum = act = dve_sum = dve = pe = sync

    def x_ready(self, k, pe):
        return None


class RmsNorm:

    def __init__(self, name, src, gain_row):
        self.name, self.src, self.gain_row = name, src, gain_row

    def open(self, k, ctx):
        sb = lambda nm, shape: ctx.enter_context(k.nc.sbuf_tensor(f"{self.name}_{nm}", shape, F32))
        self.sq, self.gain, self.rinv, self.y = sb("sq", [P, 4, T]), sb("gain", [P, KD]), sb("rinv", [P, T]), None
        sem = lambda nm: k.sem(f"{self.name}_{nm}")
        self.gain_in, self.squared, self.paired, self.summed = (sem(x) for x in ("gain", "squared", "paired", "summed"))
        self.log, self.inv, self.scaled, self.hi, self.lo = (sem(x) for x in ("log", "inv", "scaled", "hi", "lo"))
        self.y = self.sq

    def sync(self, k, sp):
        with k.nc.allow_non_contiguous_dma(reason="1024 gains, feature on partitions"):
            sp.dma_start(self.gain[:, :], self.gain_row.rearrange("(k p) -> p k", p=P)).then_inc(self.gain_in, 16)

    def act_sum(self, k, act):
        k.nc.scalar.preload_act_table_set("natural_log_exp_and_others")
        for t in range(KD):
            if t >= 4:
                act.wait_ge(self.summed, t // 2 - 1)
            k.nc.scalar.square(self.sq[:, t % 4, :], self.src[:, t, :]).then_inc(self.squared, 1)

    def dve_sum(self, k, dve):
        for n in range(KD // 2):
            t = 2 * n
            dve.wait_ge(self.squared, t + 2)
            dve.tensor_tensor(self.sq[:, t % 4, :], self.sq[:, t % 4, :], self.sq[:, t % 4 + 1, :], ALU.add)\
                .then_inc(self.paired, 1)

    def pe(self, k, pe):
        for n in range(KD // 2):
            pe.wait_ge(self.paired, n + 1)
            for b, half in enumerate(HALVES):
                mm = pe.matmul(k.ps[3][:, b, 0:HT], k.ones[:, :], self.sq[:, 2 * n % 4, half], start=n == 0,
                               stop=n == KD // 2 - 1)
            mm.then_inc(self.summed, 1)

    def act(self, k, act):
        act.wait_ge(self.summed, KD // 2)
        k.nc.scalar.activation(two(self.rinv[:, :]), halves(k.ps[3]), ACT.Ln, scale=1.0 / D, bias=k.eps[:, :])\
            .then_inc(self.log, 1)
        act.wait_ge(self.log, 1)
        k.nc.scalar.activation(self.rinv[:, :], self.rinv[:, :], ACT.Exp, scale=-0.5).then_inc(self.inv, 1)
        for t in range(KD):
            act.wait_ge(self.scaled, t + 1)
            k.nc.scalar.copy(k.xhi[:, t, :], self.y[:, t % 4, :]).then_inc(self.hi, 1)

    def dve(self, k, dve):
        dve.wait_ge(self.gain_in, 16)
        dve.wait_ge(self.inv, 1)
        def take_lo(t):
            dve.wait_ge(self.hi, t + 1)
            dve.tensor_tensor(k.xlo[:, t, :], self.y[:, t % 4, :], k.xhi[:, t, :].bitcast(F32), ALU.subtract)\
                .then_inc(self.lo, 1)
        for t in range(KD):
            if t >= 4:
                dve.wait_ge(self.lo, t - 3)
            dve.scalar_tensor_tensor(out=self.y[:, t % 4, :], in0=self.src[:, t, :], scalar=self.gain[:, t:t + 1],
                                     in1=self.rinv[:, :], op0=ALU.mult, op1=ALU.mult).then_inc(self.scaled, 1)
            if t >= 1:
                take_lo(t - 1)
        take_lo(KD - 1)

    def x_ready(self, k, pe):
        return lambda kt: pe.wait_ge(self.lo, kt + 1)


def load_tokens(k, x, meta):
    nc = k.nc
    with ExitStack() as ctx:
        tok = ctx.enter_context(nc.sbuf_tensor("tok", [P, 1 + NCH, D], F32))
        ident_made, zeroed = k.sem("ident_made"), k.sem("ident_zeroed")
        landed = [k.sem(f"tok_landed{c}") for c in range(1 + NCH)]
        turned = k.sem("tok_turned")
        stored = [k.sem("tok_stored_dve"), k.sem("tok_stored_act")]
        block = ctx.enter_context(stage(k))

        @block.sync
        def _(sp):
            for c, (t0, n) in enumerate(chunks()):
                src = meta if c == 0 else x[0, t0 - META:t0 - META + n, :]
                sp.dma_start(tok[0:n, c, :], src).then_inc(landed[c], 16)

        @block.gpsimd
        def _(pool):
            pool.memset(k.eps[:, :], EPS).then_inc(zeroed, 1)
            pool.memset(k.ones[:, :], 1.0).then_inc(zeroed, 1)
            pool.wait_ge(zeroed, 2)
            nc.gpsimd.affine_select(out=k.ident[:, :], in_=k.ones[:, :], compare_op=ALU.is_equal, fill=0.0, base=0,
                                    pattern=[[-1, P]], channel_multiplier=1).then_inc(ident_made, 1)

        @block.tensor
        def _(pe):
            pe.wait_ge(ident_made, 1)
            for c, (t0, n) in enumerate(chunks()):
                pe.wait_ge(landed[c], 16)
                if c >= 2:
                    for st in stored:
                        pe.wait_ge(st, c - 1)
                for t in range(KD):
                    mm = pe.transpose(k.ps[2 * (c % 2) + t // 4][:, t % 4 // 2, t % 2 * P:t % 2 * P + n],
                                      tok[0:n, c, t * P:(t + 1) * P], k.ident[0:n, 0:n])
                    if t % 4 == 3:
                        mm.then_inc(turned, 1)

        def store(eng, copy, half):
            for c, (t0, n) in enumerate(chunks()):
                eng.wait_ge(turned, 2 * c + half + 1)
                src = k.ps[2 * (c % 2) + half][:, :, 0:2 * P].rearrange("p b (t n) -> p b t n", t=2)[:, :, :, 0:n]
                dst = k.h[:, 4 * half:4 * half + 4, t0:t0 + n].rearrange("p (b t) n -> p b t n", b=2)
                copy(dst, src).then_inc(stored[half], 1)

        @block.vector
        def _(dve):
            store(dve, nc.vector.tensor_copy, 0)

        @block.scalar
        def _(act):
            nc.scalar.preload_act_table_set("natural_log_exp_and_others")
            store(act, nc.scalar.copy, 1)


def store_tokens(k, src, out):
    nc = k.nc
    with ExitStack() as ctx:
        tok = ctx.enter_context(nc.sbuf_tensor("tok_out", [P, NCH, D], F32))
        turned, written = k.sem("out_turned"), k.sem("out_written")
        stored = [k.sem("out_stored_dve"), k.sem("out_stored_act")]
        block = ctx.enter_context(stage(k))

        @block.tensor
        def _(pe):
            for c in range(NCH):
                t0 = META + CH * c
                if c >= 2:
                    for st in stored:
                        pe.wait_ge(st, c - 1)
                for t in range(KD):
                    mm = pe.transpose(k.ps[2 * (c % 2) + t // 4][:, t % 4 // 2, t % 2 * P:(t % 2 + 1) * P],
                                      src[:, t, t0:t0 + CH], k.ident[:, :])
                    if t % 4 == 3:
                        mm.then_inc(turned, 1)

        def store(eng, copy, half):
            for c in range(NCH):
                eng.wait_ge(turned, 2 * c + half + 1)
                dst = tok[:, c, 512 * half:512 * half + 512].rearrange("p (b n) -> p b n", b=2)
                copy(dst, k.ps[2 * (c % 2) + half][:, :, 0:2 * P]).then_inc(stored[half], 1)

        @block.vector
        def _(dve):
            store(dve, nc.vector.tensor_copy, 0)

        @block.scalar
        def _(act):
            store(act, nc.scalar.copy, 1)

        @block.sync
        def _(sp):
            for c in range(NCH):
                for st in stored:
                    sp.wait_ge(st, c + 1)
                sp.dma_start(out[0, CH * c:CH * (c + 1), :], tok[:, c, :]).then_inc(written, 16)
            sp.wait_ge(written, 16 * NCH)


def rounds(eng, n, body, period=2):
    for j in range(min(period, n)):
        body(j, j % period)
    loops = (n - 2 * period) // period
    if loops > 1:
        with eng.Fori(0, loops) as i:
            for r in range(period):
                body(i * period + period + r, r)
    else:
        loops = 0
    for j in range(period + period * loops, n):
        body(j, j % period)


def split_rings(k, name, ctx):
    sb = lambda nm, shape, dt: ctx.enter_context(k.nc.sbuf_tensor(f"{name}_{nm}", shape, dt))
    k.xhi, k.xlo = sb("xhi", [P, KD, T], F32R), sb("xlo", [P, KD, T], F32R)


def weight_ring(k, name, ctx):
    sb = lambda nm, shape, dt: ctx.enter_context(k.nc.sbuf_tensor(f"{name}_{nm}", shape, dt))
    k.whi, k.wlo = sb("whi", [P, SPLIT_SLOTS, UNIT], F32R), sb("wlo", [P, SPLIT_SLOTS, UNIT], F32R)



def project(k, name, n, cols, leave, norm=None, then=()):
    u0, t0, loaded = k.unit, k.tile, k.loaded
    norm = norm or NoNorm()
    body = 4
    with ExitStack() as ctx:
        leave.open(k, name, ctx)
        free = leave.free
        norm.open(k, ctx)
        block = ctx.enter_context(stage(k))

        def walk(eng, one):
            loops = n // body - 1
            for u in range(min(n, body)):
                one(u, u)
            if loops > 1:
                with eng.Fori(0, loops) as i:
                    for r in range(body):
                        one(i * body + body + r, r)
            else:
                loops = 0
            for u in range(body * (1 + loops), n):
                one(u, u % body)

        def walk_split(eng, one):
            loops = n // body - 2
            for u in range(min(n, body)):
                one(u, u)
            if loops > 1:
                with eng.Fori(0, loops) as i:
                    for r in range(body):
                        one(i * body + body + r, r)
            else:
                loops = 0
            for u in range(body * (1 + loops), n):
                one(u, u % body)

        ring = lambda r: (u0 + r) % RAW_SLOTS

        @block.sync
        def _(sp):
            norm.sync(k, sp)
            def one(u, r):
                if not (isinstance(u, int) and u < loaded):
                    load_unit(k, sp, u0 + u, cols(u), ring(r))
                if isinstance(u, int) and u == 1:
                    leave.sync(k, sp)
            walk(sp, one)
            load_ahead(k, sp, u0 + n, then)

        @block.scalar
        def _(act):
            norm.act_sum(k, act)
            split_hi(k, act, u0, ring(0), t0 if u0 else None)
            norm.act(k, act)
            split_hi(k, act, u0 + 1, ring(1), t0 if u0 else None)

            def one(u, r):
                for m in range(2):
                    leave.act(k, act, 2 * u + m, (2 * r + m) % 4, t0)
                if not (isinstance(u, int) and u + 2 >= n):
                    split_hi(k, act, u0 + u + 2, ring(r + 2), t0 + 2 * u + 2)
            walk_split(act, one)
            leave.act_end(k, act, 2 * n, t0)

        @block.vector
        def _(dve):
            leave.dve_start(k, dve)
            norm.dve_sum(k, dve)
            split_lo(k, dve, u0, ring(0))
            norm.dve(k, dve)
            split_lo(k, dve, u0 + 1, ring(1))

            def one(u, r):
                for m in range(2):
                    leave.dve(k, dve, 2 * u + m, (2 * r + m) % 4, t0)
                if not (isinstance(u, int) and u + 2 >= n):
                    split_lo(k, dve, u0 + u + 2, ring(r + 2))
            walk_split(dve, one)
            leave.dve_end(k, dve, 2 * n, t0)

        @block.tensor
        def _(pe):
            norm.pe(k, pe)
            def one(u, r):
                def tile_free(m):
                    if not (isinstance(u, int) and u < 2):
                        free(pe, 2 * u + m - 4)
                unit_tiles(k, pe, u0 + u, ring(r), KD, k.xhi, k.xlo, 2 * (r % 2), tile_free,
                           norm.x_ready(k, pe) if isinstance(u, int) and u == 0 else None)
            walk(pe, one)
    k.unit += n
    k.tile += 2 * n


class ConvSilu:

    def __init__(self, dst, conv, c0):
        self.dst, self.conv = dst, conv[:, c0:c0 + dst.shape[1] * P]

    def open(self, k, name, ctx):
        nc = k.nc
        sb = lambda nm, shape: ctx.enter_context(nc.sbuf_tensor(f"{name}_{nm}", shape, F32))
        self.taps = self.conv.shape[0]
        self.tiles = self.conv.shape[1] // P
        self.w = sb("convw", [P, self.taps, self.tiles])
        self.pre = sb("pre", [P, 2, T + self.taps - 1])
        self.y = sb("y", [P, 2, T])
        self.w_in, self.zeroed = k.sem(f"{name}_convw_in"), k.sem(f"{name}_zeroed")
        self.out = k.sem(f"{name}_left")
        self.tapped = k.sem(f"{name}_tapped")
        self.done = k.sem(f"{name}_silu")

    def free(self, pe, j):
        pe.wait_ge(self.out, 2 * j + 2)

    def sync(self, k, sp):
        with k.nc.allow_non_contiguous_dma(reason="small table, feature on partitions"):
            for i in range(self.taps):
                sp.dma_start(self.w[:, i, :], self.conv[i].rearrange("(t p) -> p t", p=P)).then_inc(self.w_in, 16)

    def dve_start(self, k, dve):
        dve.memset(self.pre[:, :, 0:self.taps - 1], 0.0).then_inc(self.zeroed, 1)

    def act(self, k, act, j, r, t0):
        b, last = r % 2, self.taps - 1
        if isinstance(j, int) and j == 0:
            act.wait_ge(self.w_in, 16 * self.taps)
        act.wait_ge(k.tile_full, t0 + j + 1)
        if not (isinstance(j, int) and j < 2):
            act.wait_ge(self.tapped, last * (j - 1))
            act.wait_ge(self.done, j - 1)
        k.nc.scalar.copy(two(self.pre[:, b, last:last + T]), halves(k.ps[r])).then_inc(self.out, 1)
        k.nc.scalar.activation(two(self.y[:, b, :]), halves(k.ps[r]), ACT.Copy,
                               scale=self.w[:, last, bass.ds(j, 1)]).then_inc(self.out, 1)
        if not (isinstance(j, int) and j == 0):
            self.silu(k, act, j - 1, 1 - b)

    def silu(self, k, act, j, b):
        act.wait_ge(self.tapped, (self.taps - 1) * (j + 1))
        k.nc.scalar.activation(self.dst[:, bass.ds(j, 1), :].rearrange("p o t -> p (o t)"), self.y[:, b, :],
                               ACT.Silu).then_inc(self.done, 1)

    def act_end(self, k, act, n, t0):
        self.silu(k, act, n - 1, (n - 1) % 2)

    def dve(self, k, dve, j, r, t0):
        b = r % 2
        if isinstance(j, int) and j == 0:
            dve.wait_ge(self.w_in, 16 * self.taps)
            dve.wait_ge(self.zeroed, 1)
        for i in range(self.taps - 1):
            if i == 0:
                dve.wait_ge(self.out, 2 * j + 2)
            else:
                dve.wait_ge(self.tapped, (self.taps - 1) * j + i)
            dve.scalar_tensor_tensor(out=self.y[:, b, :], in0=self.pre[:, b, i:i + T],
                                     scalar=self.w[:, i, bass.ds(j, 1)], in1=self.y[:, b, :],
                                     op0=ALU.mult, op1=ALU.add).then_inc(self.tapped, 1)

    def dve_end(self, k, dve, n, t0):
        pass


def head_norm(k, name, n, tile, ones, scale, gain, gain_src=None, then=()):
    nc = k.nc
    with ExitStack() as ctx:
        sb = lambda nm, shape: ctx.enter_context(nc.sbuf_tensor(f"{name}_{nm}", shape, F32))
        sq, rinv = sb("sq", [P, 4, T]), sb("rinv", [P, 4, T])
        g = sb("g", [P, n]) if gain_src is not None else None
        sem = lambda nm: k.sem(f"{name}_{nm}")
        gain_in, squared, summed, log, inv, done = (sem(x) for x in (
            "gain_in", "squared", "summed", "log", "inv", "done"))
        past4 = lambda j: not (isinstance(j, int) and j < 4)
        block = ctx.enter_context(stage(k))

        @block.sync
        def _(sp):
            if gain_src is not None:
                with nc.allow_non_contiguous_dma(reason="gains, feature on partitions"):
                    sp.dma_start(g[:, 0:gain_src.shape[1]], gain_src).then_inc(gain_in, 16)
            if then:
                load_ahead(k, sp, k.unit, then)

        @block.gpsimd
        def _(pool):
            def square(j, b):
                if past4(j):
                    pool.wait_ge(summed, j - 3)
                pool.tensor_tensor(sq[:, b, :], tile(j), tile(j), ALU.mult).then_inc(squared, 1)
            rounds(pool, n, square, 4)

        @block.tensor
        def _(pe):
            def one(j, b):
                pe.wait_ge(squared, j + 1)
                if past4(j):
                    pe.wait_ge(log, j - 3)
                for hf, half in enumerate(HALVES):
                    mm = pe.matmul(k.ps[b][:, hf, 0:HT], ones, sq[:, b, half], start=True, stop=True)
                mm.then_inc(summed, 1)
            rounds(pe, n, one, 4)

        @block.scalar
        def _(act):
            def logarithm(j, b):
                act.wait_ge(summed, j + 1)
                if past4(j):
                    act.wait_ge(done, j - 3)
                nc.scalar.activation(two(rinv[:, b, :]), halves(k.ps[b]), ACT.Ln, scale=scale, bias=k.eps[:, :])\
                    .then_inc(log, 1)
            def one(j, b):
                if not (isinstance(j, int) and j == n - 1):
                    logarithm(j + 1, (b + 1) % 4)
                act.wait_ge(log, j + 1)
                nc.scalar.activation(rinv[:, b, :], rinv[:, b, :], ACT.Exp, scale=-0.5).then_inc(inv, 1)
            nc.scalar.preload_act_table_set("natural_log_exp_and_others")
            logarithm(0, 0)
            rounds(act, n, one, 4)

        @block.vector
        def _(dve):
            if gain_src is not None:
                dve.wait_ge(gain_in, 16)
            def one(j, b):
                dve.wait_ge(inv, j + 1)
                dve.scalar_tensor_tensor(out=tile(j), in0=tile(j), scalar=gain(g, j), in1=rinv[:, b, :],
                                         op0=ALU.mult, op1=ALU.mult).then_inc(done, 1)
            rounds(dve, n, one, 4)



GV, GQ = 16, 8
GRP = 4
NG = GV // GRP


def gate_rows(k, name, ctx, w_cols, rows):
    sb = lambda nm, shape, dt=F32: ctx.enter_context(k.nc.sbuf_tensor(f"{name}_{nm}", shape, dt))
    s = Named(rows=rows, w_cols=w_cols)
    s.raw = sb("gw", [P, KD, rows])
    s.hi, s.lo = sb("gwhi", [P, KD, rows], F32R), sb("gwlo", [P, KD, rows], F32R)
    s.cleared, s.landed = k.sem(f"{name}_gw_cleared"), k.sem(f"{name}_gw_landed")
    s.hi_done, s.lo_done, s.ready = (k.sem(f"{name}_{x}") for x in ("gw_hi", "gw_lo", "gate_ready"))
    return s


def gate_load(k, sp, s):
    sp.wait_ge(s.cleared, 1)
    for w, r in s.w_cols:
        sp.dma_start(s.raw[:, :, r:r + w.shape[1]], w.rearrange("(k p) n -> p k n", p=P)).then_inc(s.landed, 16)


def gate_hi(k, act, s):
    act.wait_ge(s.landed, 16 * len(s.w_cols))
    k.nc.scalar.copy(s.hi[:, :, :], s.raw[:, :, :]).then_inc(s.hi_done, 1)


def gate_clear(k, dve, s):
    dve.memset(s.raw[:, :, :], 0.0).then_inc(s.cleared, 1)


def gate_lo(k, dve, s):
    dve.wait_ge(s.hi_done, 1)
    dve.tensor_tensor(s.lo[:, :, :], s.raw[:, :, :], s.hi[:, :, :].bitcast(F32), ALU.subtract).then_inc(s.lo_done, 1)


def gate_product(k, pe, s, ps):
    pe.wait_ge(s.lo_done, 1)
    for kt in range(KD):
        for n, (w, x) in enumerate(((s.hi, k.xhi), (s.hi, k.xlo), (s.lo, k.xhi))):
            for b, half in enumerate(HALVES):
                mm = pe.matmul(ps[0:s.rows, b, 0:HT], w[:, kt, :], x[:, kt, half],
                               start=kt == 0 and n == 0, stop=kt == KD - 1 and n == 2)
    mm.then_inc(s.ready, 1)


def chunk_scan_mask(dve, mask, made):
    dve.memset(mask, 1.0).then_inc(made, 1)
    dve.wait_ge(made, 1)
    for n, (t, _) in enumerate(chunks()):
        ins = dve.memset(mask[:, t:t + 1], 0.0).then_inc(made, 1)


def gdn_gates(k, g, w_in, a_log, dt_bias):
    nc = k.nc
    c0 = 2 * GQ * P + 2 * GV * P
    with ExitStack() as ctx:
        sb = lambda nm, shape: ctx.enter_context(nc.sbuf_tensor(f"gdng_{nm}", shape, F32))
        s = gate_rows(k, "gdng", ctx, [(w_in[:, c0 + GV:c0 + 2 * GV], 0), (w_in[:, c0:c0 + GV], 32)], 48)
        par = sb("par", [GV, 3])
        y, e, mask = sb("y", [GV, T]), sb("e", [GV, T]), sb("mask", [GV, T])
        beta = sb("beta", [48, T])
        par_in, act_step, dve_step, made = (k.sem(f"gdng_{x}") for x in ("par_in", "act", "dve", "mask_made"))
        turned, tok_done = k.sem("gdng_turned"), k.sem("gdng_tok")
        block = ctx.enter_context(stage(k))

        @block.sync
        def _(sp):
            with nc.allow_non_contiguous_dma(reason="a few gate weights and parameters"):
                sp.dma_start(par[:, 0:1], a_log.rearrange("(h o) -> h o", o=1)).then_inc(par_in, 16)
                sp.dma_start(par[:, 1:2], dt_bias.rearrange("(h o) -> h o", o=1)).then_inc(par_in, 16)
                gate_load(k, sp, s)

        @block.tensor
        def _(pe):
            gate_product(k, pe, s, k.ps[0])
            pe.wait_ge(dve_step, 6)
            for c, (t, n) in enumerate(chunks()):
                pe.transpose(k.ps[1][0:n, 0, 32 * c:32 * c + GV], g.cum[0:GV, t:t + n], k.ident[0:GV, 0:GV])
                mm = pe.transpose(k.ps[1][0:n, 1, 32 * c:32 * c + GV], beta[32:48, t:t + n],
                                  k.ident[32:48, 32:48])
            mm.then_inc(turned, 1)

        @block.scalar
        def _(act):
            gate_hi(k, act, s)
            act.wait_ge(par_in, 32)
            nc.scalar.activation(par[:, 2:3], par[:, 0:1], ACT.Exp).then_inc(act_step, 1)
            act.wait_ge(s.ready, 1)
            nc.scalar.activation(two(beta[32:48, :]), k.ps[0][32:48, :, 0:HT], ACT.Exp, scale=-1.0)\
                .then_inc(act_step, 1)
            nc.scalar.activation(two(e[:, :]), k.ps[0][0:GV, :, 0:HT], ACT.Abs, bias=par[:, 1:2]).then_inc(act_step, 1)
            act.wait_ge(act_step, 3)
            nc.scalar.activation(e[:, :], e[:, :], ACT.Exp, scale=-1.0).then_inc(act_step, 1)
            act.wait_ge(act_step, 4)
            nc.scalar.activation(e[:, :], e[:, :], ACT.Ln, bias=k.ones[0:GV, 0:1]).then_inc(act_step, 1)
            act.wait_ge(tok_done, 3)
            nc.scalar.activation(g.tok[:, :, 2, :], g.tok[:, :, 0, :], ACT.Exp).then_inc(act_step, 1)

        @block.vector
        def _(dve):
            gate_clear(k, dve, s)
            chunk_scan_mask(dve, mask[:, :], made)
            gate_lo(k, dve, s)
            dve.wait_ge(act_step, 4)
            dve.tensor_scalar(two(y[:, :]), k.ps[0][0:GV, :, 0:HT], par[:, 1:2], 0.0, ALU.add, ALU.max)\
                .then_inc(dve_step, 1)
            dve.tensor_scalar(beta[32:48, :], beta[32:48, :], 1.0, None, ALU.add).then_inc(dve_step, 1)
            dve.wait_ge(act_step, 5)
            dve.wait_ge(dve_step, 2)
            dve.tensor_tensor(y[:, :], y[:, :], e[:, :], ALU.add).then_inc(dve_step, 1)
            dve.reciprocal(beta[32:48, :], beta[32:48, :]).then_inc(dve_step, 1)
            dve.wait_ge(dve_step, 4)
            dve.tensor_scalar(y[:, :], y[:, :], par[:, 2:3], -1.0, ALU.mult, ALU.mult).then_inc(dve_step, 1)
            dve.wait_ge(dve_step, 5)
            dve.wait_ge(made, 1 + len(chunks()))
            dve.tensor_tensor_scan(g.cum[:, :], mask[:, :], y[:, :], 0.0, ALU.mult, ALU.add).then_inc(dve_step, 1)
            dve.memset(g.tok[:, :, :, :], 0.0).then_inc(tok_done, 1)
            dve.wait_ge(turned, 1)
            dve.wait_ge(tok_done, 1)
            cols = lambda b, c0, c1: k.ps[1][:, b, 32 * c0:32 * c1].rearrange("p (c x) -> p c x", x=32)[:, :, 0:GV]
            done = 1
            for c0, c1, n in ((0, 1, META), (1, 1 + NCH, CH)):
                dve.tensor_copy(g.tok[0:n, c0:c1, 0, :], cols(0, c0, c1)[0:n]).then_inc(tok_done, 1)
                done += 1
            for c0, c1, n in ((0, 1, META), (1, 1 + NCH, CH)):
                dve.tensor_copy(g.beta[0:n, c0:c1, :], cols(1, c0, c1)[0:n]).then_inc(tok_done, 1)
            dve.wait_ge(tok_done, 5)
            for c0, c1, n in ((0, 1, META), (1, 1 + NCH, CH)):
                dve.tensor_scalar(g.tok[0:n, c0:c1, 1, :], g.beta[0:n, c0:c1, :], -1.0, None, ALU.mult)\
                    .then_inc(tok_done, 1)
            dve.wait_ge(tok_done, 7)
            dve.wait_ge(act_step, 6)
            dve.tensor_tensor(g.tok[:, :, 2, :], g.tok[:, :, 2, :], g.tok[:, :, 1, :], ALU.mult).then_inc(tok_done, 1)


LEVELS = 7
SHORT = 4


def gdn_recurrence(k, g, qkv, vf):
    nc = k.nc
    with ExitStack() as ctx:
        sb = lambda nm, shape: ctx.enter_context(nc.sbuf_tensor(f"gdn_{nm}", shape, F32))
        raw = k.raw[:, :, :].rearrange("p s (g h n) -> p s g h n", g=NG, h=GRP)
        an, yt, xp = raw[:, 0], raw[:, 1], raw[:, 2]
        st = raw[:, 3]
        vc = xp
        new, new_dec = an, xp
        dt = sb("dt", [P, NG, GRP, CH])
        eq = sb("eq", [P, NG, GRP, CH])
        z = sb("z", [P, NG, 2 * CH])
        kt = z[:, :, :].rearrange("p g (h n) -> p g h n", h=2)
        vt = sb("vt", [P, NG, GRP, CH])
        kc = sb("kc", [P, GQ, CH])
        dl = sb("dl", [P, 2, GRP, CH])
        cc = sb("cc", [GV, CH])
        go = sb("go", [P, NG * LEVELS])
        kd, el = sb("kd", [P, GV]), sb("el", [P, GV])
        below, strict = sb("below", [P, CH]), sb("strict", [P, CH])
        lev = sb("lev", [P, LEVELS, CH // 2])
        names = ("masks", "k_staged", "v_staged", "y_staged", "bcast", "diffed", "clamped", "eq_exp", "d_exp", "gram", "small", "an_done",
                 "attn_done", "qd_done", "v_turned", "v_done", "z_ready", "z_done", "yz_ready", "y_done", "x_ready",
                 "x_done", "ks_ready", "r_done", "new_ready", "new_done", "dec_done", "o_ready", "o_done",
                 "kt_ready", "kt_done", "su_ready", "s_done", "s_zero", "cum_in")
        s = Named(**{x: k.sem(f"gdn_{x}") for x in names})
        bank_a = [k.ps[i][:, 0, :].rearrange("p (h n) -> p h n", h=GRP) for i in range(NG)]
        bank_b = [k.ps[i][:, 1, :].rearrange("p (h n) -> p h n", h=GRP) for i in range(NG)]
        zb = [k.ps[i][:, 0, 0:2 * CH] for i in range(NG)]
        yzb = [k.ps[i][:, 1, 0:2 * CH] for i in range(NG)]
        is0 = lambda c: isinstance(c, int) and c == 0
        levels = lambda c: SHORT if is0(c) else LEVELS
        first_token = lambda c: 0 if is0(c) else c * CH + (META - CH)
        q = lambda c, i: 4 * c + i
        lv = lambda c, l, i: 4 * l + i if is0(c) else c * (4 * LEVELS) + (4 * SHORT - 4 * LEVELS) + 4 * l + i

        part = lambda c, l, i: 4 * l + i if is0(c) else (c * (4 * (LEVELS - 1)) + 4 * (SHORT - LEVELS) + 4 * l + i)
        xr = part
        yr = lambda c, l, i: part(c, l - 1, i)

        def walk(eng, body):
            body(0, META)
            with eng.Fori(0, NCH) as i:
                body(i + 1, CH)

        block = ctx.enter_context(stage(k))

        @block.gpsimd
        def _(pool):
            pool.memset(below[:, :], 0.0).then_inc(s.masks, 1)
            pool.memset(strict[:, :], 0.0).then_inc(s.masks, 1)
            pool.memset(lev[:, :, :], 1.0).then_inc(s.masks, 1)
            pool.wait_ge(s.masks, 3)
            nc.gpsimd.affine_select(out=below[:, :], in_=below[:, :], compare_op=ALU.is_ge, fill=-1e30, base=0,
                                    pattern=[[1, CH]], channel_multiplier=-1).then_inc(s.masks, 1)
            nc.gpsimd.affine_select(out=strict[:, :], in_=strict[:, :], compare_op=ALU.is_ge, fill=1e30, base=-1,
                                    pattern=[[-1, CH]], channel_multiplier=1).then_inc(s.masks, 1)
            n = 5
            for l in range(LEVELS):
                hf, b = 1 << l, 2 << l
                for sign, base in ((1, 0), (-1, hf - 1)):
                    v = lev[:, l, :].rearrange("p (b w) -> p b w", w=hf)
                    nc.gpsimd.affine_select(out=v, in_=v, compare_op=ALU.is_ge, fill=0.0, base=base,
                                            pattern=[[-b * sign, CH // b], [0, hf]], channel_multiplier=sign)\
                        .then_inc(s.masks, 1)
                    n += 1
                    pool.wait_ge(s.masks, n)
            def body(c, n):
                t = first_token(c)
                if not is0(c):
                    pool.wait_ge(s.bcast, q(c - 1, NG - 1) + 1)
                pool.tensor_copy(cc[:, 0:n], g.cum[0:GV, bass.ds(t, n)]).then_inc(s.cum_in, 1)
                for i in range(NG):
                    if not is0(c):
                        pool.wait_ge(s.kt_ready, q(c - 1, i) + 1)
                    pool.tensor_copy(kc[:, 2 * i:2 * i + 2, 0:n],
                                     qkv[:, GQ + 2 * i:GQ + 2 * i + 2, bass.ds(t, n)]).then_inc(s.k_staged, 1)
                    pool.tensor_copy(yt[:, i, :, :], k.ident[:, :].unsqueeze(1).to_broadcast([P, GRP, CH]))\
                        .then_inc(s.y_staged, 1)
                for i in range(NG):
                    if not is0(c):
                        pool.wait_ge(s.su_ready, q(c - 1, i) + 1)
                    pool.tensor_copy(vc[:, i, :, 0:n],
                                     vf[:, GRP * i:GRP * (i + 1), bass.ds(t, n)]).then_inc(s.v_staged, 1)
                for i in range(NG):
                    pool.wait_ge(s.eq_exp, q(c, i) + 1)
                    e4 = eq[:, i, :, 0:n].rearrange("p (q o) n -> p q o n", o=2)
                    qs = qkv[:, 2 * i:2 * i + 2, bass.ds(t, n)]
                    pool.tensor_tensor(e4, e4, qs.unsqueeze(2).to_broadcast([P, 2, 2, n]), ALU.mult)\
                        .then_inc(s.qd_done, 1)
            walk(pool, body)

        @block.tensor
        def _(pe):
            def body(c, n):
                t = first_token(c)
                for i in range(NG):
                    pe.wait_ge(s.cum_in, c + 1)
                    if not is0(c):
                        pe.wait_ge(s.s_done, q(c - 1, i) + 1)
                    for h in range(GRP):
                        hd = GRP * i + h
                        mm = pe.matmul(bank_a[i][:, h, 0:n], k.ident[0:GV, hd:hd + 1].to_broadcast([GV, P]),
                                       cc[:, 0:n], start=True, stop=True)
                    mm.then_inc(s.bcast, 1)
                for i in range(NG):
                    pe.wait_ge(s.k_staged, q(c, i) + 1)
                    if not is0(c):
                        pe.wait_ge(s.kt_done, q(c - 1, i) + 1)
                    for h in range(2):
                        kk = kc[:, 2 * i + h, 0:n]
                        pe.matmul(bank_b[i][0:n, h, 0:n], kk, kk, start=True, stop=True)
                        mm = pe.matmul(bank_b[i][0:n, 2 + h, 0:n], kk, qkv[:, 2 * i + h, bass.ds(t, n)],
                                       start=True, stop=True)
                    mm.then_inc(s.gram, 1)
                for i in range(NG):
                    pe.wait_ge(s.v_staged, q(c, i) + 1)
                    pe.wait_ge(s.eq_exp, q(c, i) + 1)
                    for h in range(GRP):
                        mm = pe.transpose(bank_a[i][0:n, h, :], vc[:, i, h, 0:n], k.ident[:, :])
                    mm.then_inc(s.v_turned, 1)
                for l in range(levels(c)):
                    hf, b = 1 << l, 2 << l
                    second = lambda ap: ap.rearrange("p (b w) -> p b w", w=b)[:, :, hf:b]
                    for i in range(NG):
                        if l == 0:
                            pe.wait_ge(s.an_done, GRP * q(c, i) + GRP)
                            pe.wait_ge(s.v_done, q(c, i) + 1)
                        else:
                            pe.wait_ge(s.x_done, xr(c, l - 1, i) + 1)
                        for h in range(GRP):
                            y = k.ident[0:n, 0:n] if l == 0 else yt[0:n, i, h, 0:n]
                            mm = pe.matmul(zb[i][0:n, h * (n // 2):(h + 1) * (n // 2)], an[0:n, i, h, 0:n],
                                           second(y), start=True, stop=True)
                        mm.then_inc(s.z_ready, 1)
                    if l > 0:
                        for i in range(NG):
                            pe.wait_ge(s.z_done, yr(c, l, i) + 1)
                            if l == 1:
                                pe.wait_ge(s.attn_done, q(c, i) + 1)
                            for h in range(GRP):
                                mm = pe.matmul(yzb[i][0:n, h * (n // 2):(h + 1) * (n // 2)], xp[0:n, i, h, 0:n],
                                               z[0:n, i, h * (n // 2):(h + 1) * (n // 2)], start=True, stop=True)
                            mm.then_inc(s.yz_ready, 1)
                    if l < levels(c) - 1:
                        for i in range(NG):
                            pe.wait_ge(s.y_done, lv(c, l, i) + 1)
                            for h in range(GRP):
                                mm = pe.transpose(bank_a[i][0:n, h, 0:n], yt[0:n, i, h, 0:n], k.ident[0:n, 0:n])
                            mm.then_inc(s.x_ready, 1)
                for i in range(NG):
                    if is0(c):
                        pe.wait_ge(s.s_zero, 1)
                    for h in range(GRP):
                        mm = pe.matmul(bank_a[i][0:n, h, :], kc[:, 2 * i + h // 2, 0:n], st[:, i, h, :],
                                       start=True, stop=True)
                    mm.then_inc(s.ks_ready, 1)
                for i in range(NG):
                    pe.wait_ge(s.y_done, lv(c, levels(c) - 1, i) + 1)
                    pe.wait_ge(s.r_done, GRP * q(c, i) + GRP)
                    for h in range(GRP):
                        mm = pe.matmul(bank_b[i][0:n, h, :], yt[0:n, i, h, 0:n], vt[0:n, i, h, :],
                                       start=True, stop=True)
                    mm.then_inc(s.new_ready, 1)
                for i in range(NG):
                    pe.wait_ge(s.new_done, q(c, i) + 1)
                    pe.wait_ge(s.qd_done, q(c, i) + 1)
                    for h in range(GRP):
                        pe.matmul(bank_a[i][:, h, 0:n], st[:, i, h, :], eq[:, i, h, 0:n], start=True, stop=False)
                        mm = pe.matmul(bank_a[i][:, h, 0:n], new[0:n, i, h, :], dt[0:n, i, h, 0:n],
                                       start=False, stop=True)
                    mm.then_inc(s.o_ready, 1)
                for i in range(NG):
                    pe.wait_ge(s.dec_done, q(c, i) + 1)
                    for h in range(2):
                        mm = pe.transpose(bank_b[i][0:n, h, :], kc[:, 2 * i + h, 0:n], k.ident[:, :])
                    mm.then_inc(s.kt_ready, 1)
                for i in range(NG):
                    pe.wait_ge(s.kt_done, q(c, i) + 1)
                    pe.wait_ge(s.o_done, q(c, i) + 1)
                    for h in range(GRP):
                        mm = pe.matmul(bank_a[i][:, h, :], kt[0:n, i, h // 2, :], new_dec[0:n, i, h, :],
                                       start=True, stop=True)
                    mm.then_inc(s.su_ready, 1)
            walk(pe, body)

        @block.scalar
        def _(act):
            out = qkv[:, 0:2 * GQ, :].rearrange("p (o q) t -> p o q t", o=2)
            def body(c, n):
                t = first_token(c)
                for i in range(NG):
                    act.wait_ge(s.diffed, q(c, i) + 1)
                    nc.scalar.activation(eq[:, i, :, 0:n], bank_a[i][:, :, 0:n], ACT.Exp)
                    nc.scalar.activation(el[:, GRP * i:GRP * (i + 1)].unsqueeze(2), bank_a[i][:, :, n - 1:n],
                                         ACT.Exp).then_inc(s.eq_exp, 1)
                    act.wait_ge(s.clamped, 2 * q(c, i) + 1)
                    nc.scalar.activation(dl[0:n, i % 2, :, 0:n], dl[0:n, i % 2, :, 0:n], ACT.Exp, scale=-1.0)\
                        .then_inc(s.d_exp, 1)
                    act.wait_ge(s.clamped, 2 * q(c, i) + 2)
                    nc.scalar.activation(dt[0:n, i, :, 0:n], dt[0:n, i, :, 0:n], ACT.Exp).then_inc(s.d_exp, 1)
                for i in range(NG):
                    act.wait_ge(s.v_turned, q(c, i) + 1)
                    for h in range(GRP):
                        hd = GRP * i + h
                        ins = nc.scalar.activation(vt[0:n, i, h, :], bank_a[i][0:n, h, :], ACT.Copy,
                                                   scale=g.beta[0:n, bass.ds(c, 1), hd:hd + 1].rearrange(
                                                       "p o h -> p (o h)"))
                    ins.then_inc(s.v_done, 1)
                for l in range(levels(c)):
                    if l > 0:
                        for i in range(NG):
                            act.wait_ge(s.z_ready, lv(c, l, i) + 1)
                            nc.scalar.copy(z[0:n, i, 0:2 * n], zb[i][0:n, 0:2 * n]).then_inc(s.z_done, 1)
                    if l < levels(c) - 1:
                        for i in range(NG):
                            act.wait_ge(s.x_ready, xr(c, l, i) + 1)
                            nc.scalar.copy(xp[0:n, i, :, 0:n], bank_a[i][0:n, :, 0:n]).then_inc(s.x_done, 1)
                for i in range(NG):
                    act.wait_ge(s.new_ready, q(c, i) + 1)
                    nc.scalar.copy(new[0:n, i, :, :], bank_b[i][0:n, :, :]).then_inc(s.new_done, 1)
                for i in range(NG):
                    act.wait_ge(s.o_ready, q(c, i) + 1)
                    nc.scalar.copy(out[:, :, 2 * i:2 * i + 2, bass.ds(t, n)],
                                   bank_a[i][:, :, 0:n].rearrange("p (q o) n -> p o q n", o=2)).then_inc(s.o_done, 1)
                for i in range(NG):
                    act.wait_ge(s.kt_ready, q(c, i) + 1)
                    nc.scalar.copy(kt[0:n, i, :, :], bank_b[i][0:n, 0:2, :]).then_inc(s.kt_done, 1)
            walk(act, body)

        @block.vector
        def _(dve):
            dve.memset(k.raw[:, 3, :], 0.0).then_inc(s.s_zero, 1)
            def body(c, n):
                t = first_token(c)
                head = lambda i: slice(GRP * i, GRP * (i + 1))
                def decay(i):
                    b = i % 2
                    dve.wait_ge(s.bcast, q(c, i) + 1)
                    cum = g.tok[0:n, bass.ds(c, 1), 0, head(i)].rearrange("p o h -> p (o h)")
                    dve.tensor_tensor(dt[0:n, i, :, 0:n], bank_a[i][0:n, :, 0:n],
                                      cum.unsqueeze(2).to_broadcast([n, GRP, n]), ALU.subtract).then_inc(s.diffed, 1)
                    dve.wait_ge(s.diffed, q(c, i) + 1)
                    mask = lambda m: m[0:n, 0:n].unsqueeze(1).to_broadcast([n, GRP, n])
                    dve.scalar_tensor_tensor(out=dl[0:n, b, :, 0:n], in0=dt[0:n, i, :, 0:n], scalar=0.0,
                                             in1=mask(strict), op0=ALU.max, op1=ALU.add).then_inc(s.clamped, 1)
                    dve.scalar_tensor_tensor(out=dt[0:n, i, :, 0:n], in0=dt[0:n, i, :, 0:n], scalar=0.0,
                                             in1=mask(below), op0=ALU.min, op1=ALU.add).then_inc(s.clamped, 1)
                def scores(i):
                    b = i % 2
                    dve.wait_ge(s.gram, q(c, i) + 1)
                    dve.wait_ge(s.d_exp, 2 * q(c, i) + 1)
                    for h in range(GRP):
                        hd = GRP * i + h
                        dve.scalar_tensor_tensor(out=an[0:n, i, h, 0:n], in0=bank_b[i][0:n, h // 2, 0:n],
                                                 scalar=g.tok[0:n, bass.ds(c, 1), 1, hd:hd + 1].rearrange(
                                                     "p o h -> p (o h)"),
                                                 in1=dl[0:n, b, h, 0:n], op0=ALU.mult, op1=ALU.mult)\
                            .then_inc(s.an_done, 1)
                    dve.wait_ge(s.d_exp, 2 * q(c, i) + 2)
                    dve.tensor_copy(kd[0:n, head(i)].unsqueeze(2), dt[0:n, i, :, n - 1:n]).then_inc(s.small, 1)
                    dve.wait_ge(s.small, q(c, i) + 1)
                    d4 = dt[0:n, i, :, 0:n].rearrange("p (q o) n -> p q o n", o=2)
                    dve.tensor_tensor(d4, d4, bank_b[i][0:n, 2:4, 0:n].unsqueeze(2).to_broadcast([n, 2, 2, n]),
                                      ALU.mult).then_inc(s.attn_done, 1)
                if is0(c):
                    dve.wait_ge(s.masks, 5 + 2 * LEVELS)
                decay(0)
                for i in range(NG):
                    if i < NG - 1:
                        if i >= 1:
                            dve.wait_ge(s.an_done, GRP * q(c, i - 1) + GRP)
                        decay(i + 1)
                    scores(i)
                for l in range(levels(c)):
                    hf, b = 1 << l, 2 << l
                    for i in range(NG):
                        if l == 0:
                            dve.wait_ge(s.z_ready, lv(c, 0, i) + 1)
                            dve.wait_ge(s.y_staged, q(c, i) + 1)
                            src = zb
                        else:
                            dve.wait_ge(s.yz_ready, yr(c, l, i) + 1)
                            src = yzb
                        dve.memset(go[:, NG * l + i:NG * l + i + 1], 0.0)
                        y = yt[0:n, i, :, 0:n].rearrange("p h (b w) -> p h b w", w=b)[:, :, :, hf:b]
                        m = lev[0:n, l, 0:n // 2].rearrange("p (b w) -> p b w", w=hf).bitcast(U32)
                        dve.copy_predicated(
                            y, m.unsqueeze(1).to_broadcast([n, GRP, n // b, hf]),
                            src[i][0:n, 0:2 * n].rearrange("p (h b w) -> p h b w", h=GRP, w=hf)).then_inc(s.y_done, 1)
                for i in range(NG):
                    dve.wait_ge(s.ks_ready, q(c, i) + 1)
                    for h in range(GRP):
                        hd = GRP * i + h
                        dve.scalar_tensor_tensor(out=vt[0:n, i, h, :], in0=bank_a[i][0:n, h, :],
                                                 scalar=g.tok[0:n, bass.ds(c, 1), 2, hd:hd + 1].rearrange(
                                                     "p o h -> p (o h)"),
                                                 in1=vt[0:n, i, h, :], op0=ALU.mult, op1=ALU.add)\
                            .then_inc(s.r_done, 1)
                for i in range(NG):
                    dve.wait_ge(s.new_done, q(c, i) + 1)
                    dve.tensor_tensor(new_dec[0:n, i, :, :], bank_b[i][0:n, :, :],
                                      kd[0:n, head(i)].unsqueeze(2).to_broadcast([n, GRP, CH]), ALU.mult)\
                        .then_inc(s.dec_done, 1)
                for i in range(NG):
                    dve.wait_ge(s.su_ready, q(c, i) + 1)
                    for h in range(GRP):
                        hd = GRP * i + h
                        ins = dve.scalar_tensor_tensor(out=st[:, i, h, :], in0=st[:, i, h, :],
                                                       scalar=el[:, hd:hd + 1], in1=bank_a[i][:, h, :],
                                                       op0=ALU.mult, op1=ALU.add)
                    ins.then_inc(s.s_done, 1)
            walk(dve, body)


class SiluTimes:

    def __init__(self, other):
        self.other = other

    def act(self, k, act, s, g, m, ps):
        k.nc.scalar.activation(two(k.b[:, m % 2, :]), halves(ps), ACT.Silu).then_inc(s.up_free, 1)

    def dve(self, k, dve, s, g, m, ps):
        dve.wait_ge(s.up_free, 4 * g + m + 1)
        dve.tensor_tensor(k.a[:, m % 2, :], k.b[:, m % 2, :], self.other(g, m), ALU.mult).then_inc(s.a_ready, 1)


def gdn(k, ins, then=()):
    nc = k.nc
    w, conv = ins["gdn_in"][0], ins["gdn_conv"][0]
    with ExitStack() as c:
        sb = lambda nm, shape: c.enter_context(nc.sbuf_tensor(f"gdn_{nm}", shape, F32))
        split_rings(k, "gdn", c)
        norm = RmsNorm("gdn_in_norm", k.h, ins["attn_norm"][0])
        g = Named(cum=sb("cum", [GV, T]), tok=sb("tok", [P, 1 + NCH, 3, GV]), beta=sb("beta", [P, 1 + NCH, GV]))
        qk = sb("qk", [P, 2 * GQ, T])
        qk_unit = lambda u: tall(w, u * 256)
        v_unit = lambda u: tall(w, u * 256 + 2 * GQ * P)
        z_unit = lambda g, j: tall(w, g * 512 + 256 * j + 2 * GQ * P + GV * P)
        with ExitStack() as c3:
            weight_ring(k, "gdnqk", c3)
            project(k, "gdn_qk", 8, qk_unit, ConvSilu(qk, conv, 0), norm, [v_unit(u) for u in range(4)])
        with ExitStack() as c2:
            v = c2.enter_context(nc.sbuf_tensor("gdn_v", [P, GV, T], F32))
            with ExitStack() as c3:
                weight_ring(k, "gdnv", c3)
                project(k, "gdn_v", 8, v_unit, ConvSilu(v, conv, 2 * GQ * P))
            gdn_gates(k, g, w, ins["gdn_a_log"][0], ins["gdn_dt_bias"][0])
            tile = lambda base: lambda j: qk[:, bass.ds(j + base, 1), :].rearrange("p o t -> p (o t)")
            head_norm(k, "gdn_qn", GQ, tile(0), k.ones[:, :], 1.0, lambda g, j: float(P) ** -0.5)
            head_norm(k, "gdn_kn", GQ, tile(GQ), k.ones[:, :], 1.0, lambda g, j: 1.0)
            gdn_recurrence(k, g, qk, v)
        head_norm(k, "gdn_on", GV, tile(0), k.ones[:, :], 1.0 / P, lambda g, j: g[:, 0:1],
                  ins["gdn_norm"].rearrange("o p -> p o"), first_units(z_unit))
        with ExitStack() as c3:
            weight_ring(k, "gdno", c3)
            o = lambda g, m: qk[:, bass.ds(2 * g + (m % 2) * GQ + m // 2, 1), :].rearrange("p o t -> p (o t)")
            up_down(k, "gdn_out", GV // 4, z_unit, ins["gdn_out"][0], SiluTimes(o), k.h, False, None, then)



class Store:

    def __init__(self, dst, scale=lambda j: 1.0):
        self.dst, self.scale = dst, scale

    def open(self, k, name, ctx):
        self.left = k.sem(f"{name}_left")

    def free(self, pe, j):
        pe.wait_ge(self.left, j + 1)

    def sync(self, k, sp):
        pass

    def dve_start(self, k, dve):
        pass

    def act(self, k, act, j, r, t0):
        act.wait_ge(k.tile_full, t0 + j + 1)
        k.nc.scalar.activation(two(self.dst(j)), halves(k.ps[r]), ACT.Copy, scale=self.scale(j)).then_inc(self.left, 1)

    def act_end(self, k, act, n, t0):
        pass

    def dve(self, k, dve, j, r, t0):
        pass

    def dve_end(self, k, dve, n, t0):
        pass


MH = 8
MK = 64
CAP = 15.0


def small_product(k, pe, s, c0, n, ps):
    for kt in range(KD):
        for m, (w, x) in enumerate(((s.hi, k.xhi), (s.hi, k.xlo), (s.lo, k.xhi))):
            for b, half in enumerate(HALVES):
                mm = pe.matmul(ps[0:n, b, 0:HT], w[:, kt, c0:c0 + n], x[:, kt, half],
                               start=kt == 0 and m == 0, stop=kt == KD - 1 and m == 2)
    return mm


def mlstm_gates(k, g, w_in, bias):
    nc = k.nc
    c0 = 2 * MH * MK + 2 * D
    with ExitStack() as ctx:
        sb = lambda nm, shape: ctx.enter_context(nc.sbuf_tensor(f"mlg_{nm}", shape, F32))
        s = gate_rows(k, "mlg", ctx, [(w_in[:, c0:c0 + 2 * MH], 0)], 2 * MH)
        bi = sb("bias", [MH, 2])
        i, f, e, mask, cum = (sb(x, [MH, T]) for x in ("i", "f", "e", "mask", "cum"))
        bias_in, a, v, made, turned = (k.sem(f"mlg_{x}") for x in ("bias_in", "act", "dve", "mask", "turned"))
        block = ctx.enter_context(stage(k))

        @block.sync
        def _(sp):
            with nc.allow_non_contiguous_dma(reason="a few gate weights and parameters"):
                sp.dma_start(bi[:, :], bias.rearrange("(o h) -> h o", o=2)).then_inc(bias_in, 16)
                gate_load(k, sp, s)

        @block.tensor
        def _(pe):
            pe.wait_ge(s.lo_done, 1)
            small_product(k, pe, s, 0, MH, k.ps[0])
            small_product(k, pe, s, MH, MH, k.ps[1]).then_inc(s.ready, 1)
            pe.wait_ge(v, 8)
            for c, (t, n) in enumerate(chunks()):
                mm = pe.transpose(k.ps[2][0:n, 0, 16 * c:16 * c + MH], e[0:MH, t:t + n], k.ident[0:MH, 0:MH])
            mm.then_inc(turned, 1)

        @block.scalar
        def _(act):
            gate_hi(k, act, s)
            act.wait_ge(s.ready, 1)
            act.wait_ge(v, 1)
            nc.scalar.activation(two(i[:, :]), k.ps[0][0:MH, :, 0:HT], ACT.Tanh, bias=bi[:, 0:1], scale=1.0 / CAP)\
                .then_inc(a, 1)
            nc.scalar.activation(two(f[:, :]), k.ps[1][0:MH, :, 0:HT], ACT.Tanh, bias=bi[:, 1:2], scale=1.0 / CAP)\
                .then_inc(a, 1)
            act.wait_ge(v, 3)
            nc.scalar.activation(e[:, :], f[:, :], ACT.Abs).then_inc(a, 1)
            act.wait_ge(a, 3)
            nc.scalar.activation(e[:, :], e[:, :], ACT.Exp, scale=-1.0).then_inc(a, 1)
            act.wait_ge(a, 4)
            nc.scalar.activation(e[:, :], e[:, :], ACT.Ln, bias=k.ones[0:MH, 0:1]).then_inc(a, 1)

        @block.vector
        def _(dve):
            gate_clear(k, dve, s)
            chunk_scan_mask(dve, mask[:, :], made)
            gate_lo(k, dve, s)
            dve.wait_ge(bias_in, 16)
            dve.tensor_scalar(bi[:, :], bi[:, :], 1.0 / CAP, None, ALU.mult).then_inc(v, 1)
            dve.wait_ge(a, 2)
            dve.tensor_scalar(i[:, :], i[:, :], CAP, None, ALU.mult).then_inc(v, 1)
            dve.tensor_scalar(f[:, :], f[:, :], CAP, None, ALU.mult).then_inc(v, 1)
            dve.wait_ge(a, 5)
            dve.wait_ge(v, 3)
            dve.scalar_tensor_tensor(out=f[:, :], in0=f[:, :], scalar=0.0, in1=e[:, :], op0=ALU.min,
                                     op1=ALU.subtract).then_inc(v, 1)
            dve.wait_ge(v, 4)
            dve.wait_ge(made, 1 + len(chunks()))
            dve.tensor_tensor_scan(cum[:, :], mask[:, :], f[:, :], 0.0, ALU.mult, ALU.add).then_inc(v, 1)
            dve.tensor_tensor_scan(g.m[:, :], f[:, :], i[:, :], 0.0, ALU.add, ALU.max).then_inc(v, 1)
            dve.wait_ge(v, 6)
            dve.tensor_tensor(g.am[:, :], cum[:, :], g.m[:, :], ALU.subtract).then_inc(v, 1)
            dve.tensor_tensor(e[:, :], i[:, :], cum[:, :], ALU.subtract).then_inc(v, 1)
            dve.wait_ge(turned, 1)
            cols = k.ps[2][:, 0, 0:16 * (1 + NCH)].rearrange("p (c x) -> p c x", x=16)[:, :, 0:MH]
            for c0, c1, n in ((0, 1, META), (1, 1 + NCH, CH)):
                dve.tensor_copy(g.b[0:n, c0:c1, :], cols[0:n, c0:c1]).then_inc(v, 1)


def mlstm_recurrence(k, g, qk, vf):
    nc = k.nc
    NG2 = MH // GRP
    with ExitStack() as ctx:
        sb = lambda nm, shape: ctx.enter_context(nc.sbuf_tensor(f"ml_{nm}", shape, F32))
        st = sb("st", [P, MH // 2, P + 1])
        kc, vc = sb("kc", [P, MH // 2, CH]), sb("vc", [P, MH, CH])
        qz = sb("qz", [P, MH, CH])
        amc, mc, mp = sb("amc", [MH, CH]), sb("mc", [MH, CH]), sb("mp", [MH, 1])
        w = sb("w", [P, NG2, GRP, CH])
        inn = sb("in", [P, NG2, 2, CH])
        qd = sb("qd", [P, NG2, GRP, CH])
        floor, dm = sb("floor", [P, NG2, GRP, CH]), sb("dm", [P, NG2, GRP, CH])
        vt = sb("vt", [P, NG2, GRP, CH])
        num = sb("num", [P, NG2, GRP, CH])
        kd = sb("kd", [P, NG2, 2, 2, MK])
        we = sb("we", [P, MH])
        mpc = sb("mpc", [P, MH // 2])
        below = sb("below", [P, CH])
        names = ("masks", "staged", "bcast", "gram", "diffed", "clamped", "w_exp", "floor_done", "mp_done", "in_done",
                 "we_done", "w_done", "qd_done", "v_turned", "v_done", "k_turned", "k_done", "num_ready", "den_ready",
                 "dm_done", "rden", "h_done", "left", "su_ready", "s_done", "s_zero")
        s = Named(**{x: k.sem(f"ml_{x}") for x in names})
        heads = lambda ap: ap.rearrange("p (h n) -> p h n", h=GRP)
        bank_a = [heads(k.ps[2 * i][:, 0, :]) for i in range(NG2)]
        bank_b = [heads(k.ps[2 * i][:, 1, :]) for i in range(NG2)]
        bank_c = [k.ps[2 * i + 1][:, 0, :] for i in range(NG2)]
        bank_e = [k.ps[2 * i + 1][:, 1, :] for i in range(NG2)]
        is0 = lambda c: isinstance(c, int) and c == 0
        first_token = lambda c: 0 if is0(c) else c * CH + (META - CH)
        q = lambda c, i: NG2 * c + i

        def walk(eng, body):
            body(0, META)
            with eng.Fori(0, NCH) as i:
                body(i + 1, CH)

        block = ctx.enter_context(stage(k))

        @block.gpsimd
        def _(pool):
            pool.memset(below[:, :], 0.0).then_inc(s.masks, 1)
            pool.memset(qz[:, :, :], 0.0).then_inc(s.masks, 1)
            pool.wait_ge(s.masks, 2)
            nc.gpsimd.affine_select(out=below[:, :], in_=below[:, :], compare_op=ALU.is_ge, fill=-1e30, base=0,
                                    pattern=[[1, CH]], channel_multiplier=-1).then_inc(s.masks, 1)
            def body(c, n):
                t = first_token(c)
                if not is0(c):
                    pool.wait_ge(s.k_turned, q(c, 0))
                    pool.wait_ge(s.qd_done, q(c, 0))
                    pool.tensor_copy(mp[:, :], g.m[:, bass.ds(t - 1, 1)]).then_inc(s.staged, 1)
                else:
                    pool.memset(mp[:, :], 0.0).then_inc(s.staged, 1)
                now = bass.ds(t, n)
                pool.tensor_copy(amc[:, 0:n], g.am[:, now]).then_inc(s.staged, 1)
                pool.tensor_copy(mc[:, 0:n], g.m[:, now]).then_inc(s.staged, 1)
                pool.tensor_copy(kc[:, :, 0:n], qk[:, MH // 2:MH, now]).then_inc(s.staged, 1)
                for o in range(2):
                    pool.wait_ge(s.staged, 7 * c + 4 + o)
                    pool.tensor_copy(qz[MK * o:MK * (o + 1), o:MH:2, 0:n],
                                     qk[MK * o:MK * (o + 1), 0:MH // 2, now]).then_inc(s.staged, 1)
                pool.wait_ge(s.staged, 7 * c + 6)
                pool.tensor_copy(vc[:, :, 0:n], vf[:, :, now]).then_inc(s.staged, 1)
            walk(pool, body)

        @block.tensor
        def _(pe):
            one_hot = lambda h: k.ident[0:MH, h:h + 1].to_broadcast([MH, P])
            def body(c, n):
                for i in range(NG2):
                    pe.wait_ge(s.staged, 7 * c + 3)
                    if not is0(c):
                        pe.wait_ge(s.left, 2 * q(c - 1, i) + 2)
                        pe.wait_ge(s.s_done, q(c - 1, i) + 1)
                    for h in range(GRP):
                        pe.matmul(bank_a[i][:, h, 0:n], one_hot(GRP * i + h), amc[:, 0:n], start=True, stop=True)
                    for h in range(GRP):
                        pe.matmul(bank_b[i][:, h, 0:n], one_hot(GRP * i + h), mc[:, 0:n], start=True, stop=True)
                    for p in range(2):
                        hd = GRP * i + 2 * p
                        for o in range(2):
                            sel = k.ident[0:MH, hd + o:hd + o + 1].to_broadcast([MH, MK])
                            pe.matmul(bank_c[i][MK * o:MK * (o + 1), CH * p:CH * p + n], sel, amc[:, 0:n],
                                      start=True, stop=True)
                            mm = pe.matmul(bank_c[i][MK * o:MK * (o + 1), 2 * CH + p:2 * CH + p + 1], sel, mp[:, :],
                                           start=True, stop=True)
                    mm.then_inc(s.bcast, 1)
                for i in range(NG2):
                    pe.wait_ge(s.staged, 7 * c + 6)
                    for h in range(GRP):
                        hd = GRP * i + h
                        mm = pe.matmul(bank_e[i][0:n, CH * h:CH * h + n], kc[:, hd // 2, 0:n],
                                       qz[:, hd, 0:n], start=True, stop=True)
                    mm.then_inc(s.gram, 1)
                for i in range(NG2):
                    pe.wait_ge(s.staged, 7 * c + 7)
                    pe.wait_ge(s.in_done, 2 * q(c, i) + 2)
                    for h in range(GRP):
                        mm = pe.transpose(bank_c[i][0:n, CH * h:CH * (h + 1)], vc[:, GRP * i + h, 0:n], k.ident[:, :])
                    mm.then_inc(s.v_turned, 1)
                for i in range(NG2):
                    pe.wait_ge(s.w_done, q(c, i) + 1)
                    for p in range(2):
                        mm = pe.transpose(bank_e[i][0:n, CH * p:CH * (p + 1)], kc[:, 2 * i + p, 0:n], k.ident[:, :])
                    mm.then_inc(s.k_turned, 1)
                for i in range(NG2):
                    pe.wait_ge(s.qd_done, q(c, i) + 1)
                    pe.wait_ge(s.v_done, q(c, i) + 1)
                    pe.wait_ge(s.floor_done, q(c, i) + 1)
                    if is0(c):
                        pe.wait_ge(s.s_zero, 1)
                    for h in range(GRP):
                        hd = GRP * i + h
                        pe.matmul(bank_a[i][:, h, 0:n], st[:, hd // 2, 0:P], qd[:, i, h, 0:n],
                                  start=True, stop=False)
                        mm = pe.matmul(bank_a[i][:, h, 0:n], vt[0:n, i, h, :], w[0:n, i, h, 0:n],
                                       start=False, stop=True)
                    mm.then_inc(s.num_ready, 1)
                    for h in range(GRP):
                        hd = GRP * i + h
                        pe.matmul(bank_b[i][:, h, 0:n], st[:, hd // 2, P:P + 1].to_broadcast([P, P]),
                                  qd[:, i, h, 0:n], start=True, stop=False)
                        mm = pe.matmul(bank_b[i][:, h, 0:n], k.ones[0:n, :], w[0:n, i, h, 0:n],
                                       start=False, stop=True)
                    mm.then_inc(s.den_ready, 1)
                for i in range(NG2):
                    pe.wait_ge(s.k_done, q(c, i) + 1)
                    for p in range(2):
                        kk = kd[0:n, i, p, :, :].rearrange("p h d -> p (h d)")
                        pe.matmul(bank_c[i][:, 2 * CH * p:2 * CH * (p + 1)], kk,
                                  vt[0:n, i, 2 * p:2 * p + 2, :].rearrange("p h d -> p (h d)"), start=True, stop=True)
                        mm = pe.matmul(bank_e[i][:, p:p + 1], kk, k.ones[0:n, 0:1], start=True, stop=True)
                    mm.then_inc(s.su_ready, 1)
            walk(pe, body)

        @block.scalar
        def _(act):
            nc.scalar.preload_act_table_set("exp_and_others")
            def body(c, n):
                for i in range(NG2):
                    act.wait_ge(s.bcast, q(c, i) + 1)
                    if not is0(c):
                        act.wait_ge(s.dm_done, q(c - 1, i) + 1)
                    nc.scalar.copy(mpc[:, 2 * i:2 * i + 2], bank_c[i][:, 2 * CH:2 * CH + 2]).then_inc(s.mp_done, 1)
                    nc.scalar.activation(floor[:, i, :, 0:n], bank_b[i][:, :, 0:n], ACT.Exp, scale=-1.0)\
                        .then_inc(s.floor_done, 1)
                    act.wait_ge(s.mp_done, q(c, i) + 1)
                    for p in range(2):
                        nc.scalar.activation(inn[:, i, p, 0:n], bank_c[i][:, CH * p:CH * p + n], ACT.Exp,
                                             bias=mpc[:, 2 * i + p:2 * i + p + 1]).then_inc(s.in_done, 1)
                for i in range(NG2):
                    act.wait_ge(s.clamped, q(c, i) + 1)
                    nc.scalar.activation(w[0:n, i, :, 0:n], w[0:n, i, :, 0:n], ACT.Exp).then_inc(s.w_exp, 1)
                for i in range(NG2):
                    act.wait_ge(s.v_turned, q(c, i) + 1)
                    nc.scalar.copy(vt[0:n, i, :, :], heads(bank_c[i])[0:n]).then_inc(s.v_done, 1)
                for i in range(NG2):
                    act.wait_ge(s.num_ready, q(c, i) + 1)
                    if not is0(c):
                        act.wait_ge(s.h_done, q(c - 1, i) + 1)
                    nc.scalar.copy(num[:, i, :, 0:n], bank_a[i][:, :, 0:n]).then_inc(s.left, 1)
                    act.wait_ge(s.den_ready, q(c, i) + 1)
                    nc.scalar.activation(dm[:, i, :, 0:n], bank_b[i][:, :, 0:n], ACT.Abs).then_inc(s.left, 1)
            walk(act, body)

        @block.vector
        def _(dve):
            dve.memset(st[:, :, :], 0.0).then_inc(s.s_zero, 1)
            def outputs(c, n):
                for i in range(NG2):
                    dve.wait_ge(s.dm_done, q(c, i) + 1)
                    dve.reciprocal(dm[:, i, :, 0:n], dm[:, i, :, 0:n]).then_inc(s.rden, 1)
                    dve.wait_ge(s.rden, q(c, i) + 1)
                    dve.tensor_tensor(vf[:, GRP * i:GRP * (i + 1), bass.ds(first_token(c), n)], num[:, i, :, 0:n],
                                      dm[:, i, :, 0:n], ALU.mult).then_inc(s.h_done, 1)
            def body(c, n):
                t = first_token(c)
                head = lambda i: slice(GRP * i, GRP * (i + 1))
                if is0(c):
                    dve.wait_ge(s.masks, 3)
                for i in range(NG2):
                    dve.wait_ge(s.bcast, q(c, i) + 1)
                    b = g.b[0:n, bass.ds(c, 1), head(i)].rearrange("p o h -> p (o h)")
                    dve.tensor_tensor(w[0:n, i, :, 0:n], bank_a[i][0:n, :, 0:n],
                                      b.unsqueeze(2).to_broadcast([n, GRP, n]), ALU.add).then_inc(s.diffed, 1)
                    dve.wait_ge(s.diffed, q(c, i) + 1)
                    dve.scalar_tensor_tensor(out=w[0:n, i, :, 0:n], in0=w[0:n, i, :, 0:n], scalar=0.0,
                                             in1=below[0:n, 0:n].unsqueeze(1).to_broadcast([n, GRP, n]),
                                             op0=ALU.min, op1=ALU.add).then_inc(s.clamped, 1)
                for i in range(NG2):
                    dve.wait_ge(s.in_done, 2 * q(c, i) + 2)
                    dve.wait_ge(s.staged, 7 * c + 6)
                    dve.tensor_tensor(qd[:, i, :, 0:n].rearrange("p (a b) n -> p a b n", b=2),
                                      qz[:, head(i), 0:n].rearrange("p (a b) n -> p a b n", b=2),
                                      inn[:, i, :, 0:n].unsqueeze(2).to_broadcast([P, 2, 2, n]), ALU.mult)\
                        .then_inc(s.qd_done, 1)
                    dve.wait_ge(s.w_exp, q(c, i) + 1)
                    dve.tensor_copy(we[0:n, head(i)].unsqueeze(2), w[0:n, i, :, n - 1:n]).then_inc(s.we_done, 1)
                    dve.wait_ge(s.we_done, q(c, i) + 1)
                    dve.wait_ge(s.gram, q(c, i) + 1)
                    dve.tensor_tensor(w[0:n, i, :, 0:n], w[0:n, i, :, 0:n], heads(bank_e[i])[0:n, :, 0:n],
                                      ALU.mult).then_inc(s.w_done, 1)
                for i in range(NG2):
                    dve.wait_ge(s.k_turned, q(c, i) + 1)
                    dve.tensor_tensor(kd[0:n, i].rearrange("p a h d -> p (a h) d"),
                                      bank_e[i][0:n, 0:2 * CH].rearrange("p (h d) -> p h d", d=MK),
                                      we[0:n, head(i)].unsqueeze(2).to_broadcast([n, GRP, MK]), ALU.mult)\
                        .then_inc(s.k_done, 1)
                if not is0(c) and not (isinstance(c, int) and c == 1):
                    outputs(c - 1, n)
                for i in range(NG2):
                    dve.wait_ge(s.su_ready, q(c, i) + 1)
                    for p in range(2):
                        pr = 2 * i + p
                        keep = inn[:, i, p, n - 1:n]
                        for o in range(2):
                            r = slice(MK * o, MK * (o + 1))
                            c0 = 2 * CH * p + CH * o
                            dve.scalar_tensor_tensor(out=st[r, pr, 0:P], in0=st[r, pr, 0:P], scalar=keep[r],
                                                     in1=bank_c[i][r, c0:c0 + P], op0=ALU.mult, op1=ALU.add)
                        ins = dve.scalar_tensor_tensor(out=st[:, pr, P:P + 1], in0=st[:, pr, P:P + 1], scalar=keep,
                                                       in1=bank_e[i][:, p:p + 1], op0=ALU.mult, op1=ALU.add)
                    ins.then_inc(s.s_done, 1)
                for i in range(NG2):
                    dve.wait_ge(s.left, 2 * q(c, i) + 2)
                    dve.tensor_tensor(dm[:, i, :, 0:n], dm[:, i, :, 0:n], floor[:, i, :, 0:n], ALU.max)\
                        .then_inc(s.dm_done, 1)
                if is0(c):
                    outputs(c, n)
            body(0, META)
            body(1, CH)
            with dve.Fori(0, NCH - 1) as i:
                body(i + 2, CH)
            outputs(NCH, CH)


class SigmoidTimes(SiluTimes):

    def act(self, k, act, s, g, m, ps):
        k.nc.scalar.activation(two(k.b[:, m % 2, :]), halves(ps), ACT.Sigmoid).then_inc(s.up_free, 1)


def mlstm_unit(ins):
    return lambda u: tall(ins["mlstm_in"][0], u * 256)


def mlstm(k, ins, then=()):
    nc = k.nc
    w = ins["mlstm_in"][0]
    with ExitStack() as c:
        sb = lambda nm, shape: c.enter_context(nc.sbuf_tensor(f"mls_{nm}", shape, F32))
        split_rings(k, "mls", c)
        g = Named(am=sb("am", [MH, T]), m=sb("m", [MH, T]), b=sb("b", [P, 1 + NCH, MH]))
        vf = sb("v", [P, MH, T])
        gate_unit = lambda g, j: tall(w, g * 512 + 256 * j + 2 * MH * MK + D)
        with ExitStack() as c2:
            qk = c2.enter_context(nc.sbuf_tensor("mls_qk", [P, MH, T], F32))
            with ExitStack() as c3:
                weight_ring(k, "mlsp", c3)
                project(k, "mls_p", 8, mlstm_unit(ins),
                        Store(lambda j: qk[:, j, :] if j < MH else vf[:, j - MH, :],
                              lambda j: MK ** -0.5 if MH // 2 <= j < MH else 1.0),
                        RmsNorm("mls_in_norm", k.h, ins["attn_norm"][1]), first_units(gate_unit))
            mlstm_gates(k, g, w, ins["mlstm_gate_bias"][0])
            mlstm_recurrence(k, g, qk, vf)
        tile = lambda j: vf[:, bass.ds(j, 1), :].rearrange("p o t -> p (o t)")
        head_norm(k, "mls_on", MH, tile, k.ones[:, :], 1.0 / P,
                  lambda g, j: g[:, bass.ds(j, 1)], ins["mlstm_norm"][0].rearrange("(h p) -> p h", p=P))
        with ExitStack() as c3:
            weight_ring(k, "mlso", c3)
            up_down(k, "mls_out", MH // 4, gate_unit, ins["mlstm_out"][0],
                    SigmoidTimes(lambda g, m: tile(g * 4 + m)), k.h, False, None, then)



S0 = META
LN2_60 = 41.58883083359672
HW = 64
FH = 8


def linked(eng, sem):
    count = [0]

    def link(ins):
        count[0] += 1
        ins.then_inc(sem, 1)
        eng.wait_ge(sem, count[0])
    return link


def hgrn_gates(k, qa, fa, b, lower):
    nc = k.nc
    with ExitStack() as ctx:
        sb = lambda nm, shape: ctx.enter_context(nc.sbuf_tensor(f"hg_{nm}", shape, F32))
        e1, e2, small = sb("e1", [P, 2, T]), sb("e2", [P, 2, T]), sb("small", [P, 2, T])
        mask, lx, lb = sb("mask", [P, T]), sb("lx", [P, 2]), sb("lb", [P, 3, 2])
        lx_in, ev, silu, e0, one, ln = (k.sem(f"hg_{x}") for x in ("lx_in", "exps", "silu", "lb_exp", "lb_diff", "ln"))
        ready, chain, q1 = k.sem("hg_ready"), k.sem("hg_chain"), k.sem("hg_ln_in")
        block = ctx.enter_context(stage(k))

        @block.sync
        def _(sp):
            with nc.allow_non_contiguous_dma(reason="256 bounds, feature on partitions"):
                sp.dma_start(lx[:, :], lower[0].rearrange("(t p) -> p t", p=P)).then_inc(lx_in, 16)

        @block.scalar
        def _(act):
            nc.scalar.preload_act_table_set("exp_and_others")
            nc.scalar.activation(e1[:, :, :], fa, ACT.Exp, scale=-1.0).then_inc(ev, 1)
            nc.scalar.activation(e2[:, :, :], fa, ACT.Exp).then_inc(ev, 1)
            act.wait_ge(one, 1)
            nc.scalar.activation(lb[:, 0, :], lb[:, 0, :], ACT.Exp).then_inc(e0, 1)
            act.wait_ge(q1, 1)
            nc.scalar.activation(b[:, :, :], e1[:, :, :], ACT.Ln).then_inc(ln, 1)
            nc.scalar.activation(qa, qa, ACT.Silu).then_inc(silu, 1)

        @block.vector
        def _(dve):
            link = linked(dve, chain)
            dve.wait_ge(lx_in, 16)
            dve.tensor_tensor(lb[:, 0, :], lx[:, :], lx[:, :], ALU.subtract).then_inc(one, 1)
            dve.wait_ge(e0, 1)
            link(dve.reciprocal(lb[:, 1, :], lb[:, 0, :]))
            link(dve.tensor_tensor(lb[:, 1, :], lb[:, 1, :], lb[:, 0, :], ALU.mult))
            link(dve.tensor_tensor(lb[:, 0, :], lb[:, 1, :], lb[:, 1, :], ALU.subtract))
            link(dve.tensor_scalar(lb[:, 2, :], lb[:, 0, :], -1.0, 1.0, ALU.mult, ALU.add))
            dve.wait_ge(ev, 2)
            link(dve.tensor_scalar(e1[:, :, :], e1[:, :, :], 1.0, None, ALU.add))
            link(dve.reciprocal(e1[:, :, :], e1[:, :, :]))
            for j in range(2):
                link(dve.tensor_scalar(e1[:, j, :], e1[:, j, :], lb[:, 2, j:j + 1], lb[:, 0, j:j + 1],
                                       ALU.mult, ALU.add))
            link(dve.tensor_scalar(e1[:, :, :], e1[:, :, :], 1e-30, None, ALU.max))
            link(dve.tensor_scalar(small[:, :, :], e1[:, :, :], 2.0 ** -40, None, ALU.is_lt))
            link(dve.tensor_scalar(b[:, :, :], small[:, :, :], 2.0 ** 60, 1.0, ALU.mult, ALU.add))
            dve.tensor_tensor(e1[:, :, :], e1[:, :, :], b[:, :, :], ALU.mult).then_inc(q1, 1)
            link(dve.tensor_scalar(e2[:, :, :], e2[:, :, :], 1.0, None, ALU.add))
            link(dve.reciprocal(e2[:, :, :], e2[:, :, :]))
            for j in range(2):
                dve.tensor_scalar(fa[:, j, :], e2[:, j, :], lb[:, 2, j:j + 1], None, ALU.mult).then_inc(ready, 1)
            link(dve.memset(mask[:, :], 1.0))
            for t, _ in chunks():
                link(dve.memset(mask[:, t:t + 1], 0.0))
            dve.wait_ge(ln, 1)
            link(dve.scalar_tensor_tensor(out=small[:, :, :], in0=small[:, :, :], scalar=-LN2_60, in1=b[:, :, :],
                                          op0=ALU.mult, op1=ALU.add))
            for j in range(2):
                link(dve.tensor_tensor_scan(b[:, j, :], mask[:, :], small[:, j, :], 0.0, ALU.mult, ALU.add))
            dve.wait_ge(silu, 1)


def hgrn(k, qa, ka, va, b):
    nc = k.nc
    with ExitStack() as ctx:
        sb = lambda nm, shape: ctx.enter_context(nc.sbuf_tensor(f"hr_{nm}", shape, F32))
        e = sb("e", [P, 2, 2, SEQ])
        st = sb("st", [P, 2, 2, NCH, CH])
        lev = sb("lev", [P, LEVELS, CH // 2])
        qd, kd = sb("qd", [P, 2, SEQ]), sb("kd", [P, 2, SEQ])
        vt, kt = sb("vt", [P, 2, NCH, P]), sb("kt", [P, 2, NCH, P])
        s2, keep = sb("s2", [P, 2, P]), sb("keep", [P, 2, NCH])
        names = ("masks", "diff", "exps", "scaled", "scores", "taken", "zero", "ends", "end_exp", "end_scaled",
                 "v_turned", "v_done", "k_turned", "k_done", "o_ready", "o_done", "su", "s_done", "keep_done")
        s = Named(**{x: k.sem(f"hr_{x}") for x in names})
        tok = slice(S0, T)
        bank = lambda j, o, l: k.ps[2 * (l % 2) + j][:, o, :]
        block = ctx.enter_context(stage(k))

        @block.gpsimd
        def _(pool):
            pool.memset(lev[:, :, :], 1.0).then_inc(s.masks, 1)
            n = 1
            pool.wait_ge(s.masks, n)
            for l in range(LEVELS):
                hf, bl = 1 << l, 2 << l
                for sign, base in ((1, 0), (-1, hf - 1)):
                    v = lev[:, l, :].rearrange("p (b w) -> p b w", w=hf)
                    nc.gpsimd.affine_select(out=v, in_=v, compare_op=ALU.is_ge, fill=0.0, base=base,
                                            pattern=[[-bl * sign, CH // bl], [0, hf]], channel_multiplier=sign)\
                        .then_inc(s.masks, 1)
                    n += 1
                    pool.wait_ge(s.masks, n)
            pool.memset(st[:, :, :, :, :], 0.0).then_inc(s.zero, 1)
            pool.memset(s2[:, :, :], 0.0).then_inc(s.zero, 1)

        @block.vector
        def _(dve):
            def split(ap, l):
                v = ap.rearrange("p j (c w) -> p j c w", w=2 << l)
                return v[:, :, :, 0:1 << l], v[:, :, :, 1 << l:2 << l]
            def exponents(l):
                hf = 1 << l
                if l >= 2:
                    dve.wait_ge(s.scores, l - 1)
                first, second = split(b[:, :, tok], l)
                efirst, esecond = split(e[:, l % 2, :, :], l)
                mid = first[:, :, :, hf - 1:hf].to_broadcast(list(first.shape))
                dve.tensor_tensor(esecond, second, mid, ALU.subtract).then_inc(s.diff, 1)
                dve.tensor_tensor(efirst, mid, first, ALU.subtract).then_inc(s.diff, 1)
            def scale(l):
                efirst, esecond = split(e[:, l % 2, :, :], l)
                dve.wait_ge(s.exps, l + 1)
                dve.tensor_tensor(esecond, esecond, split(qa[:, :, tok], l)[1], ALU.mult).then_inc(s.scaled, 1)
                dve.tensor_tensor(efirst, efirst, split(ka[:, :, tok], l)[0], ALU.mult).then_inc(s.scaled, 1)
            def take(l):
                hf, bl = 1 << l, 2 << l
                dve.wait_ge(s.scores, l + 1)
                if l >= 1:
                    dve.wait_ge(s.taken, 4 * l)
                m = lev[:, l, :].rearrange("p (b w) -> p b w", w=hf).bitcast(U32).unsqueeze(1)
                for j in range(2):
                    for o in range(2):
                        out = st[:, j, o, :, :].rearrange("p c (b w) -> p c b w", w=bl)[:, :, :, hf:bl]
                        src = bank(j, o, l)[:, 0:SEQ // 2].rearrange("p (c b w) -> p c b w", c=NCH, w=hf)
                        dve.copy_predicated(out, m.to_broadcast([P, NCH, CH // bl, hf]), src).then_inc(s.taken, 1)
            last = b[:, :, tok].rearrange("p j (c w) -> p j c w", w=CH)[:, :, :, CH - 1:CH]
            b4 = b[:, :, tok].rearrange("p j (c w) -> p j c w", w=CH)
            dve.tensor_tensor(kd[:, :, :].rearrange("p j (c w) -> p j c w", w=CH),
                              last.to_broadcast([P, 2, NCH, CH]), b4, ALU.subtract).then_inc(s.ends, 1)
            exponents(0)
            dve.wait_ge(s.end_exp, 2)
            dve.tensor_tensor(kd[:, :, :], kd[:, :, :], ka[:, :, tok], ALU.mult).then_inc(s.end_scaled, 1)
            dve.tensor_copy(keep[:, :, :].unsqueeze(3),
                            qd[:, :, :].rearrange("p j (c w) -> p j c w", w=CH)[:, :, :, CH - 1:CH])\
                .then_inc(s.keep_done, 1)
            dve.wait_ge(s.keep_done, 1)
            dve.tensor_tensor(qd[:, :, :], qd[:, :, :], qa[:, :, tok], ALU.mult).then_inc(s.end_scaled, 1)
            dve.wait_ge(s.masks, 1 + 2 * LEVELS)
            dve.wait_ge(s.zero, 2)
            for l in range(LEVELS):
                if l + 1 < LEVELS:
                    exponents(l + 1)
                scale(l)
                if l >= 1:
                    take(l - 1)
            take(LEVELS - 1)
            dve.wait_ge(s.scores, LEVELS + 1)
            dve.wait_ge(s.taken, 4 * LEVELS)
            for j in range(2):
                for o in range(2):
                    dve.copy_predicated(st[:, j, o, :, :],
                                        k.ident[:, :].bitcast(U32).unsqueeze(1).to_broadcast([P, NCH, CH]),
                                        bank(j, o, LEVELS).rearrange("p (c w) -> p c w", c=NCH)).then_inc(s.taken, 1)
            for c in range(NCH):
                for j in range(2):
                    dve.wait_ge(s.su, 2 * c + j + 1)
                    if c > 0:
                        dve.wait_ge(s.s_done, 4 * c)
                    for o in range(2):
                        r = slice(HW * o, HW * (o + 1))
                        dve.scalar_tensor_tensor(out=s2[r, j, r], in0=s2[r, j, r], scalar=keep[r, j, c:c + 1],
                                                 in1=k.ps[1][r, j, HW * o:HW * (o + 1)], op0=ALU.mult, op1=ALU.add)\
                            .then_inc(s.s_done, 1)

        @block.scalar
        def _(act):
            nc.scalar.preload_act_table_set("exp_and_others")
            nc.scalar.activation(qd[:, :, :], b[:, :, tok], ACT.Exp).then_inc(s.end_exp, 1)
            act.wait_ge(s.ends, 1)
            nc.scalar.activation(kd[:, :, :], kd[:, :, :], ACT.Exp).then_inc(s.end_exp, 1)
            for l in range(LEVELS):
                act.wait_ge(s.diff, 2 * l + 2)
                nc.scalar.activation(e[:, l % 2, :, :], e[:, l % 2, :, :], ACT.Exp).then_inc(s.exps, 1)
                if l < 2:
                    act.wait_ge(s.v_turned, l + 1)
                    nc.scalar.copy(vt[:, l, :, :], k.ps[2 + l][:, 0, :].rearrange("p (c n) -> p c n", c=NCH))\
                        .then_inc(s.v_done, 1)
                    act.wait_ge(s.k_turned, l + 1)
                    nc.scalar.copy(kt[:, l, :, :], k.ps[2 + l][:, 1, :].rearrange("p (c n) -> p c n", c=NCH))\
                        .then_inc(s.k_done, 1)
            for c in range(NCH):
                act.wait_ge(s.o_ready, c + 1)
                nc.scalar.copy(va[:, :, S0 + CH * c:S0 + CH * (c + 1)], k.ps[0][:, :, 0:CH]).then_inc(s.o_done, 1)

        @block.tensor
        def _(pe):
            for j in range(2):
                for c in range(NCH):
                    mm = pe.transpose(k.ps[2 + j][:, 0, CH * c:CH * (c + 1)], va[:, j, S0 + CH * c:S0 + CH * (c + 1)],
                                      k.ident[:, :])
                mm.then_inc(s.v_turned, 1)
            pe.wait_ge(s.end_scaled, 1)
            for j in range(2):
                for c in range(NCH):
                    mm = pe.transpose(k.ps[2 + j][:, 1, CH * c:CH * (c + 1)], kd[:, j, CH * c:CH * (c + 1)],
                                      k.ident[:, :])
                mm.then_inc(s.k_turned, 1)
            for l in range(LEVELS):
                hf, bl = 1 << l, 2 << l
                pe.wait_ge(s.scaled, 2 * l + 2)
                if l == 1:
                    pe.wait_ge(s.v_done, 2)
                    pe.wait_ge(s.k_done, 2)
                if l >= 2:
                    pe.wait_ge(s.taken, 4 * (l - 1))
                for j in range(2):
                    for c in range(NCH):
                        for o in range(2):
                            r = slice(HW * o, HW * (o + 1))
                            v = e[r, l % 2, j, CH * c:CH * (c + 1)]
                            mm = pe.matmul(bank(j, o, l)[:, CH // 2 * c:CH // 2 * (c + 1)], v,
                                           v.rearrange("p (b w) -> p b w", w=bl)[:, :, hf:bl], start=True, stop=True)
                mm.then_inc(s.scores, 1)
            pe.wait_ge(s.taken, 4 * (LEVELS - 1))
            for j in range(2):
                for c in range(NCH):
                    for o in range(2):
                        r, t = slice(HW * o, HW * (o + 1)), slice(S0 + CH * c, S0 + CH * (c + 1))
                        mm = pe.matmul(bank(j, o, LEVELS)[:, CH * c:CH * (c + 1)], ka[r, j, t], qa[r, j, t],
                                       start=True, stop=True)
            mm.then_inc(s.scores, 1)
            pe.wait_ge(s.end_scaled, 2)
            pe.wait_ge(s.taken, 4 * (LEVELS + 1))
            for c in range(NCH):
                if c > 0:
                    pe.wait_ge(s.o_done, c)
                    pe.wait_ge(s.s_done, 4 * c)
                for j in range(2):
                    pe.matmul(k.ps[0][:, j, 0:CH], s2[:, j, :], qd[:, j, CH * c:CH * (c + 1)], start=True, stop=False,
                              skip_group_check=True)
                    for o in range(2):
                        r = slice(HW * o, HW * (o + 1))
                        mm = pe.matmul(k.ps[0][r, j, 0:CH], vt[:, j, c, r], st[:, j, o, c, :], start=False, stop=True,
                                       skip_group_check=True)
                mm.then_inc(s.o_ready, 1)
                for j in range(2):
                    pe.matmul(k.ps[1][:, j, 0:P], kt[:, j, c, :], vt[:, j, c, :], start=True, stop=True)\
                        .then_inc(s.su, 1)


WINDOWS = (2, 4, 8, 16)


def pooling(k, u, pool_w, pool_scale):
    nc = k.nc
    with ExitStack() as ctx:
        sb = lambda nm, shape, dt=F32: ctx.enter_context(nc.sbuf_tensor(f"pl_{nm}", shape, dt))
        w, sc = sb("w", [P, 2, P]), sb("sc", [P, 2])
        a, c = sb("a", [P, 2, T]), sb("c", [P, 2, T])
        head = sb("head", [P, 2, META])
        cnt_i, cnt = sb("cnt_i", [P, META], mybir.dt.int32), sb("cnt", [P, 2, META])
        w_zero, w_in, sc_in, count, chain = (k.sem(f"pl_{x}") for x in ("w_zero", "w_in", "sc_in", "count", "chain"))
        pooled, mixed, left = k.sem("pl_pooled"), k.sem("pl_mixed"), k.sem("pl_left")
        group = lambda g: (slice(HW * (g % 2), HW * (g % 2) + HW), g // 2)
        block = ctx.enter_context(stage(k))

        @block.gpsimd
        def _(pool):
            nc.gpsimd.iota(cnt_i[:, :], pattern=[[1, META]], base=1, channel_multiplier=0).then_inc(count, 1)
            pool.memset(w[:, :, :], 0.0).then_inc(w_zero, 1)

        @block.sync
        def _(sp):
            sp.wait_ge(w_zero, 1)
            for g in range(4):
                r, j = group(g)
                sp.dma_start(w[r, j, r], pool_w[g]).then_inc(w_in, 16)
            with nc.allow_non_contiguous_dma(reason="256 scales, feature on partitions"):
                sp.dma_start(sc[:, :], pool_scale.rearrange("(t p) -> p t", p=P)).then_inc(sc_in, 16)

        @block.vector
        def _(dve):
            link = linked(dve, chain)
            link(dve.memset(u[:, :, 0:S0], 0.0))
            link(dve.memset(a[:, :, 0:S0], 0.0))
            link(dve.memset(c[:, :, 0:S0], 0.0))
            dve.wait_ge(count, 1)
            for g, win in enumerate(WINDOWS):
                r, j = group(g)
                link(dve.tensor_copy(cnt[r, j, :], cnt_i[r, :]))
                link(dve.tensor_scalar(cnt[r, j, :], cnt[r, j, :], float(win), None, ALU.min))
            link(dve.reciprocal(cnt[:, :, :], cnt[:, :, :]))
            src, dst = u, a
            for n, win in enumerate(WINDOWS):
                d = win // 2
                for j in range(n // 2, 2):
                    r = slice(0, P) if 2 * j >= n else slice(HW, P)
                    link(dve.tensor_tensor(dst[r, j, S0:T], src[r, j, S0:T], src[r, j, S0 - d:T - d], ALU.add))
                r, j = group(n)
                link(dve.tensor_tensor(head[r, j, :], dst[r, j, S0:S0 + META], cnt[r, j, :], ALU.mult))
                if n < 3:
                    src, dst = dst, (c if dst is a else a)
            for g, win in enumerate(WINDOWS):
                r, j = group(g)
                v = a if g % 2 == 0 else c
                link(dve.scalar_tensor_tensor(out=v[r, j, S0 + META:T], in0=v[r, j, S0 + META:T], scalar=1.0 / win,
                                              in1=u[r, j, S0 + META:T], op0=ALU.mult, op1=ALU.subtract))
                link(dve.tensor_tensor(v[r, j, S0:S0 + META], head[r, j, :], u[r, j, S0:S0 + META], ALU.subtract))
            for j in range(2):
                dve.tensor_copy(a[HW:P, j, S0:T], c[HW:P, j, S0:T]).then_inc(pooled, 1)

        @block.tensor
        def _(pe):
            pe.wait_ge(w_in, 64)
            pe.wait_ge(pooled, 2)
            for j in range(2):
                for b in range(2):
                    half = slice(S0 + b * (SEQ // 2), S0 + (b + 1) * (SEQ // 2))
                    mm = pe.matmul(k.ps[j][:, b, 0:SEQ // 2], w[:, j, :], a[:, j, half], start=True, stop=True)
                mm.then_inc(mixed, 1)

        @block.scalar
        def _(act):
            act.wait_ge(sc_in, 16)
            for j in range(2):
                act.wait_ge(mixed, j + 1)
                nc.scalar.activation(two(u[:, j, S0:T]), k.ps[j][:, :, 0:SEQ // 2], ACT.Copy,
                                     scale=sc[:, j:j + 1]).then_inc(left, 1)


def fox_gates(k, negc, w_in, bias):
    nc = k.nc
    with ExitStack() as ctx:
        sb = lambda nm, shape: ctx.enter_context(nc.sbuf_tensor(f"fg_{nm}", shape, F32))
        s = gate_rows(k, "fg", ctx, [(w_in, 0)], FH)
        bi, f, e, one = sb("bias", [FH, 1]), sb("f", [FH, T]), sb("e", [FH, T]), sb("one", [FH, SEQ])
        bias_in, a, v = k.sem("fg_bias_in"), k.sem("fg_act"), k.sem("fg_dve")
        block = ctx.enter_context(stage(k))

        @block.sync
        def _(sp):
            with nc.allow_non_contiguous_dma(reason="a few gate weights and parameters"):
                sp.dma_start(bi[:, :], bias.rearrange("(h o) -> h o", o=1)).then_inc(bias_in, 16)
                gate_load(k, sp, s)

        @block.tensor
        def _(pe):
            pe.wait_ge(s.lo_done, 1)
            small_product(k, pe, s, 0, FH, k.ps[0]).then_inc(s.ready, 1)

        @block.scalar
        def _(act):
            gate_hi(k, act, s)
            act.wait_ge(v, 2)
            nc.scalar.activation(e[:, :], f[:, :], ACT.Abs).then_inc(a, 1)
            act.wait_ge(a, 1)
            nc.scalar.activation(e[:, :], e[:, :], ACT.Exp, scale=-1.0).then_inc(a, 1)
            act.wait_ge(a, 2)
            nc.scalar.activation(e[:, :], e[:, :], ACT.Ln, bias=k.ones[0:FH, 0:1]).then_inc(a, 1)

        @block.vector
        def _(dve):
            gate_clear(k, dve, s)
            dve.memset(one[:, :], 1.0).then_inc(v, 1)
            gate_lo(k, dve, s)
            dve.wait_ge(s.ready, 1)
            dve.wait_ge(bias_in, 16)
            dve.tensor_scalar(two(f[:, :]), halves(k.ps[0], FH), bi[:, 0:1], None, ALU.add).then_inc(v, 1)
            dve.wait_ge(a, 3)
            dve.wait_ge(v, 2)
            dve.tensor_scalar(f[:, :], f[:, :], 0.0, -1.0, ALU.min, ALU.mult).then_inc(v, 1)
            dve.wait_ge(v, 3)
            dve.tensor_tensor(f[:, :], f[:, :], e[:, :], ALU.add).then_inc(v, 1)
            dve.wait_ge(v, 4)
            dve.tensor_tensor_scan(negc[:, :], one[:, :], f[:, S0:T], 0.0, ALU.mult, ALU.add).then_inc(v, 1)


def fox(k, qc, kc, vc, negc):
    nc = k.nc
    with ExitStack() as ctx:
        sb = lambda nm, shape: ctx.enter_context(nc.sbuf_tensor(f"fx_{nm}", shape, F32))
        nb = sb("nb", [P, FH, SEQ])
        vt = sb("vt", [P, NCH, FH, HW])
        above = sb("above", [P, CH])
        sc, pt = sb("sc", [P, 4, SEQ]), sb("pt", [P, 2, SEQ])
        mx, sm = sb("mx", [P, NCH * FH, 2]), sb("sm", [P, NCH, FH])
        o = sb("o", [P, 2, FH, HW])
        names = ("masks", "bcast", "nb_done", "v_turned", "v_done", "scores", "maxed", "negated", "probs", "p_turned",
                 "p_done", "o_ready", "inverse", "o_done", "o_turned", "out_done")
        s = Named(**{x: k.sem(f"fx_{x}") for x in names})
        score = [k.ps[i // 2][:, i % 2, :] for i in range(4)]
        turned = [k.ps[2][:, i, :] for i in range(2)]
        o_bank, ot_bank = k.ps[3][:, 0, :], k.ps[3][:, 1, :]
        steps_ = [(c, h) for c in range(NCH) for h in range(FH)]
        block = ctx.enter_context(stage(k))

        @block.gpsimd
        def _(pool):
            pool.memset(above[:, :], 0.0).then_inc(s.masks, 1)
            pool.wait_ge(s.masks, 1)
            nc.gpsimd.affine_select(out=above[:, :], in_=above[:, :], compare_op=ALU.is_ge, fill=-1e30, base=0,
                                    pattern=[[-1, CH]], channel_multiplier=1).then_inc(s.masks, 1)

        @block.tensor
        def _(pe):
            for h in range(FH):
                if h >= 2:
                    pe.wait_ge(s.nb_done, h - 1)
                pe.matmul(turned[h % 2], k.ident[0:FH, h:h + 1].to_broadcast([FH, P]), negc[:, :], start=True,
                          stop=True).then_inc(s.bcast, 1)
            for c in range(NCH):
                if c >= 2:
                    pe.wait_ge(s.v_done, c - 1)
                for j in range(4):
                    mm = pe.transpose((o_bank, ot_bank)[c % 2][:, P * j:P * (j + 1)],
                                      vc[:, j, S0 + CH * c:S0 + CH * (c + 1)], k.ident[:, :])
                mm.then_inc(s.v_turned, 1)
            pe.wait_ge(s.masks, 2)

            def scores(i):
                c, h = steps_[i]
                r, n = slice(HW * (h % 2), HW * (h % 2) + HW), CH * (c + 1)
                if i >= 4:
                    pe.wait_ge(s.maxed, i - 3)
                pe.matmul(score[h % 4][:, 0:n], qc[r, h // 2, S0 + CH * c:S0 + n], kc[r, h // 2, S0:S0 + n],
                          start=True, stop=False)
                pe.matmul(score[h % 4][:, n - CH:n], k.ident[:, :], above[:, :], start=False, stop=True)\
                    .then_inc(s.scores, 1)

            def turn(i):
                c, h = steps_[i]
                pe.wait_ge(s.probs, i + 1)
                if i >= 2:
                    pe.wait_ge(s.p_done, i - 1)
                elif i == 0:
                    pe.wait_ge(s.nb_done, FH)
                for b in range(c + 1):
                    mm = pe.transpose(turned[i % 2][:, CH * b:CH * (b + 1)], sc[:, i % 4, CH * b:CH * (b + 1)],
                                      k.ident[:, :])
                mm.then_inc(s.p_turned, 1)

            def values(i):
                c, h = steps_[i]
                pe.wait_ge(s.p_done, i + 1)
                if h == 0:
                    pe.wait_ge(s.v_done, NCH)
                    if c > 0:
                        pe.wait_ge(s.o_done, c)
                for b in range(c + 1):
                    mm = pe.matmul(o_bank[:, HW * h:HW * (h + 1)], pt[:, i % 2, CH * b:CH * (b + 1)],
                                   vt[:, b, h, :], start=b == 0, stop=b == c)
                mm.then_inc(s.o_ready, 1)
                if h == FH - 1:
                    pe.wait_ge(s.o_done, c + 1)
                    if c > 0:
                        pe.wait_ge(s.out_done, c)
                    for j in range(4):
                        mm = pe.transpose(ot_bank[:, P * j:P * (j + 1)],
                                          o[:, c % 2, 2 * j:2 * j + 2, :].rearrange("p h d -> p (h d)"),
                                          k.ident[:, :])
                    mm.then_inc(s.o_turned, 1)

            n = len(steps_)
            for i in range(n + 3):
                if i < n:
                    scores(i)
                if 2 <= i < n + 2:
                    turn(i - 2)
                if i >= 3:
                    values(i - 3)

        @block.vector
        def _(dve):
            for c in range(NCH):
                dve.wait_ge(s.v_turned, c + 1)
                dve.tensor_copy(vt[:, c, :, :].rearrange("p h d -> p (h d)"), (o_bank, ot_bank)[c % 2])\
                    .then_inc(s.v_done, 1)
            dve.wait_ge(s.nb_done, FH)
            def top(i):
                c, h = steps_[i]
                n = CH * (c + 1)
                dve.wait_ge(s.scores, i + 1)
                if i >= 4:
                    dve.wait_ge(s.p_turned, i - 3)
                dve.tensor_tensor_reduce(out=sc[:, i % 4, 0:n], in0=score[h % 4][:, 0:n], in1=nb[:, h, 0:n], scale=1.0,
                                         scalar=-3e38, op0=ALU.add, op1=ALU.max, accum_out=mx[:, i, 0:1])\
                    .then_inc(s.maxed, 1)
                dve.wait_ge(s.maxed, i + 1)
                dve.tensor_scalar(mx[:, i, 1:2], mx[:, i, 0:1], -1.0, None, ALU.mult).then_inc(s.negated, 1)
            def out(c):
                dve.wait_ge(s.probs, FH * (c + 1))
                dve.reciprocal(sm[:, c, :], sm[:, c, :]).then_inc(s.inverse, 1)
                dve.wait_ge(s.inverse, c + 1)
                dve.wait_ge(s.o_ready, FH * (c + 1))
                if c >= 2:
                    dve.wait_ge(s.o_turned, c - 1)
                dve.tensor_tensor(o[:, c % 2, :, :], o_bank.rearrange("p (h d) -> p h d", d=HW),
                                  sm[:, c, :].unsqueeze(2).to_broadcast([P, FH, HW]), ALU.mult).then_inc(s.o_done, 1)
            n = len(steps_)
            for i in range(n + 4):
                if i < n:
                    top(i)
                if i >= 3 and i - 3 < n and (i - 3) % FH == FH - 1:
                    out((i - 3) // FH)

        @block.scalar
        def _(act):
            nc.scalar.preload_act_table_set("exp_and_others")
            for h in range(FH):
                act.wait_ge(s.bcast, h + 1)
                nc.scalar.copy(nb[:, h, :], turned[h % 2]).then_inc(s.nb_done, 1)
            def probs(i):
                c, h = steps_[i]
                n = CH * (c + 1)
                act.wait_ge(s.negated, i + 1)
                nc.scalar.activation(sc[:, i % 4, 0:n], sc[:, i % 4, 0:n], ACT.Exp, bias=mx[:, i, 1:2],
                                     accum_out=sm[:, c, h:h + 1]).then_inc(s.probs, 1)
            def take(i):
                c, h = steps_[i]
                act.wait_ge(s.p_turned, i + 1)
                nc.scalar.copy(pt[:, i % 2, 0:CH * (c + 1)], turned[i % 2][:, 0:CH * (c + 1)]).then_inc(s.p_done, 1)
            def out(c):
                act.wait_ge(s.o_turned, c + 1)
                nc.scalar.copy(qc[:, :, S0 + CH * c:S0 + CH * (c + 1)], ot_bank.rearrange("p (j n) -> p j n", j=4))\
                    .then_inc(s.out_done, 1)
            n = len(steps_)
            for i in range(n + 2):
                if i < n:
                    probs(i)
                if 1 <= i <= n:
                    take(i - 1)
                if i >= 2 and (i - 2) % FH == 3 and i - 2 >= FH:
                    out((i - 2) // FH - 1)
            out(NCH - 1)


def add_normed(k, name, y, gain_row):
    nc = k.nc
    with ExitStack() as ctx:
        sb = lambda nm, shape: ctx.enter_context(nc.sbuf_tensor(f"{name}_{nm}", shape, F32))
        sq, gain, ms, rinv = sb("sq", [P, 2, T]), sb("gain", [P, KD]), sb("ms", [P, T]), sb("rinv", [P, T])
        gain_in, squared, summed = k.sem(f"{name}_gain"), k.sem(f"{name}_squared"), k.sem(f"{name}_summed")
        mean, log, inv = k.sem(f"{name}_mean"), k.sem(f"{name}_log"), k.sem(f"{name}_inv")
        scaled, added = k.sem(f"{name}_scaled"), k.sem(f"{name}_added")
        block = ctx.enter_context(stage(k))

        @block.sync
        def _(sp):
            with nc.allow_non_contiguous_dma(reason="1024 gains, feature on partitions"):
                sp.dma_start(gain[:, :], gain_row.rearrange("(k p) -> p k", p=P)).then_inc(gain_in, 16)

        @block.scalar
        def _(act):
            nc.scalar.preload_act_table_set("natural_log_exp_and_others")
            for t in range(KD):
                if t >= 2:
                    act.wait_ge(summed, t - 1)
                nc.scalar.square(sq[:, t % 2, :], y[:, t, :]).then_inc(squared, 1)
            act.wait_ge(mean, 1)
            nc.scalar.activation(ms[:, :], ms[:, :], ACT.Ln).then_inc(log, 1)
            act.wait_ge(log, 1)
            nc.scalar.activation(rinv[:, :], ms[:, :], ACT.Exp, scale=-0.5).then_inc(inv, 1)

        @block.vector
        def _(dve):
            dve.wait_ge(summed, KD)
            dve.tensor_scalar(two(ms[:, :]), halves(k.ps[0]), 1.0 / D, EPS, ALU.mult, ALU.add).then_inc(mean, 1)
            dve.wait_ge(gain_in, 16)
            dve.wait_ge(inv, 1)
            def add(t):
                dve.wait_ge(scaled, t + 1)
                dve.tensor_tensor(k.h[:, t, :], k.h[:, t, :], y[:, t, :], ALU.add).then_inc(added, 1)
            for t in range(KD):
                dve.scalar_tensor_tensor(out=y[:, t, :], in0=y[:, t, :], scalar=gain[:, t:t + 1],
                                         in1=rinv[:, :], op0=ALU.mult, op1=ALU.mult).then_inc(scaled, 1)
                if t >= 1:
                    add(t - 1)
            add(KD - 1)

        @block.tensor
        def _(pe):
            for t in range(KD):
                pe.wait_ge(squared, t + 1)
                for b, half in enumerate(HALVES):
                    mm = pe.matmul(k.ps[0][:, b, 0:HT], k.ones[:, :], sq[:, t % 2, half], start=t == 0,
                                   stop=t == KD - 1)
                mm.then_inc(summed, 1)


SEC_COLS = (0, 256, 512, 1024, 1536, 1792, 2048, 2304, 2560, 2816)


def second_unit(ins):
    return lambda u: tall(ins["w_in_2"][0], SEC_COLS[u])


def second(k, ins):
    nc = k.nc
    w = ins["w_in_2"][0]
    with ExitStack() as c:
        sb = lambda nm, shape: c.enter_context(nc.sbuf_tensor(f"sec_{nm}", shape, F32))
        split_rings(k, "sec", c)
        negc = sb("negc", [FH, SEQ])
        gate_unit = lambda g, j: tall(w, ((768, 1280), (3072, 3328))[g][j])
        mix = sb("mix", [P, KD, T])
        ones2 = sb("ones2", [P, P])
        with ExitStack() as c2:
            rest = c2.enter_context(nc.sbuf_tensor("sec_rest", [P, 12, T], F32))
            place = ((rest, 0), (rest, 2), (mix, 0), (mix, 2), (mix, 4), (mix, 6), (rest, 4), (rest, 6), (rest, 8),
                     (rest, 10))
            with ExitStack() as c3:
                weight_ring(k, "secp", c3)
                def dst(j):
                    buf, t = place[j // 2]
                    return buf[:, t + j % 2, :]
                project(k, "sec_p", 10, second_unit(ins),
                        Store(dst, lambda j: HW ** -0.5 if 4 <= j // 2 < 6 else 1.0),
                        RmsNorm("sec_in_norm", k.h, ins["pre_norm_g_2"][0]), first_units(gate_unit))
            fox_gates(k, negc, w[:, 3584:3584 + FH], ins["fox_f_bias_2"][0])
            with ExitStack() as c3:
                b = c3.enter_context(nc.sbuf_tensor("sec_b", [P, 2, T], F32))
                hgrn_gates(k, rest[:, 0:2, :], rest[:, 2:4, :], b, ins["lower_bounds_2"])
                hgrn(k, rest[:, 0:2, :], rest[:, 2:4, :], mix[:, 0:2, :], b)
            pooling(k, mix[:, 2:4, :], ins["pool_w_2"][0], ins["pool_scale_2"][0])
            fox(k, mix[:, 4:8, :], rest[:, 4:8, :], rest[:, 8:12, :], negc)
        block_ones(k, ones2)
        head_norm(k, "sec_hn", 2, lambda j: mix[:, j, :], ones2[:, :], 1.0 / HW, lambda g, j: g[:, j:j + 1],
                  ins["hgrn_norm_g_2"][0].rearrange("(j p) -> p j", p=P))
        k.y = sb("y", [P, KD, T])
        with ExitStack() as c3:
            weight_ring(k, "seco", c3)
            up_down(k, "sec_out", 2, gate_unit, ins["w_out_2"][0],
                    SiluTimes(lambda g, m: mix[:, g * 4 + m, :]), k.y, True)
        add_normed(k, "sec_post", k.y, ins["post_norm_g_2"][0])


def block_ones(k, ones2):
    made = k.sem("ones2_made")
    with stage(k) as block:
        @block.gpsimd
        def _(pool):
            pool.memset(ones2[:, :], 0.0).then_inc(made, 1)
            pool.wait_ge(made, 1)
            for o in range(2):
                r = slice(HW * o, HW * (o + 1))
                pool.memset(ones2[r, r], 1.0).then_inc(made, 1)



_USED = ["x", "meta_tokens", "attn_norm", "ffn_norm", "ff_up", "ff_down", "gdn_in", "gdn_conv", "gdn_a_log",
         "gdn_dt_bias", "gdn_norm", "gdn_out", "mlstm_in", "mlstm_gate_bias", "mlstm_norm", "mlstm_out",
         "lower_bounds_2", "pre_norm_g_2", "w_in_2", "hgrn_norm_g_2", "fox_f_bias_2", "pool_w_2", "pool_scale_2",
         "w_out_2", "post_norm_g_2"]


def ffn_unit(ins, layer):
    return lambda g, j: tall(ins["ff_up"][layer], g * 512 + 256 * j)


def ffn(k, ins, layer, then=()):
    with ExitStack() as c:
        split_rings(k, f"ffn{layer}", c)
        weight_ring(k, f"ffn{layer}w", c)
        up_down(k, f"ffn{layer}", 8, ffn_unit(ins, layer), ins["ff_down"][layer], SquaredRelu(), k.h, False,
                RmsNorm(f"ffn{layer}_norm", k.h, ins["ffn_norm"][layer]), then)


def STAGES(k, ctx, ins):
    gdn(k, ins, first_units(ffn_unit(ins, 0)))
    ffn(k, ins, 0, [mlstm_unit(ins)(u) for u in range(4)])
    mlstm(k, ins, first_units(ffn_unit(ins, 1)))
    ffn(k, ins, 1, [second_unit(ins)(u) for u in range(4)])
    second(k, ins)
    k.y = k.h


def build(nc, ins, out):
    with ExitStack() as ctx:
        k = persistent(nc, ctx)
        load_tokens(k, ins["x"], ins["meta_tokens"])
        STAGES(k, ctx, ins)
        store_tokens(k, k.y, out)


_OUT = ((1, SEQ, D), "float32")


def kernel(**inputs):
    import numpy as _np
    import concourse.bacc as _bacc
    from concourse import mybir as _mybir
    from concourse.bass_utils import run_bass_kernel_spmd as _run

    nc = _bacc.Bacc("TRN2", target_bir_lowering=False, num_devices=1)
    arrays, args = {}, {}
    for name in _USED:
        a = _np.ascontiguousarray(inputs[name])
        arrays[f"in_{name}_dram"] = a
        args[name] = nc.dram_tensor(f"in_{name}_dram", a.shape, _mybir.dt.from_np(a.dtype), kind="ExternalInput").ap()
    out = nc.dram_tensor("out_dram", _OUT[0], _mybir.dt.from_np(_np.dtype(_OUT[1])), kind="ExternalOutput").ap()
    build(nc, args, out)
    r = _run(nc, [arrays], core_ids=[0])
    return r.results[0]["out_dram"]
```

```python
from contextlib import ExitStack, contextmanager

import concourse.bass as bass
from concourse import mybir

F32 = mybir.dt.float32
F32R = mybir.dt.float32r
U32 = mybir.dt.uint32
ALU = mybir.AluOpType
ACT = mybir.ActivationFunctionType
AX = mybir.AxisListType

P = 128
D = 1024
KD = D // P
META = 16
SEQ = 512
T = META + SEQ
HT = T // 2
CH = 128
NCH = SEQ // CH
EPS = 1e-6

RAW_SLOTS = 4
SPLIT_SLOTS = 2
UNIT = 2048
HALVES = (slice(0, HT), slice(HT, T))


class Named(dict):
    __getattr__ = dict.__getitem__


def chunks():
    return [(0, META)] + [(META + CH * c, CH) for c in range(NCH)]


def persistent(nc, ctx):
    k = Named(nc=nc)
    sb = lambda name, shape, dt=F32: ctx.enter_context(nc.sbuf_tensor(name, shape, dt))
    sem = lambda name: ctx.enter_context(nc.semaphore(name))
    k.stage_sems, k.last_sems, k.uncleared = ExitStack(), ExitStack(), []
    k.opened = []

    def stage_sem(name):
        k.opened.append(k.stage_sems.enter_context(nc.semaphore(name)))
        return k.opened[-1]
    k.sem = stage_sem
    k.h = sb("h", [P, KD, T])
    k.raw = sb("raw", [P, RAW_SLOTS, UNIT])
    k.ones = sb("ones", [P, P])
    k.ident = sb("ident", [P, P])
    k.eps = sb("eps", [P, 1])
    k.ps = [ctx.enter_context(nc.psum_tensor(f"ps{i}", [P, 2, 512], F32)) for i in range(4)]
    k.raw_landed = [sem(f"raw_landed{i}") for i in range(RAW_SLOTS)]
    k.hi_done = sem("hi_done")
    k.lo_done = sem("lo_done")
    k.tile_full = sem("tile_full")
    k.unit = 0
    k.tile = 0
    k.loaded = 0
    return k


@contextmanager
def stage(k):
    with k.nc.Block() as block:
        if k.uncleared:
            nums = sorted(x.num for x in k.uncleared)

            @block.sync
            def _(sp):
                first = prev = nums[0]
                for x in nums[1:] + [None]:
                    if x != prev + 1:
                        sp.sem_clear(range(first, prev + 1))
                        first = x
                    prev = x
        yield block
    k.last_sems.close()
    k.last_sems, k.stage_sems = k.stage_sems, ExitStack()
    k.uncleared, k.opened = k.opened, []



def tall(w, c0):
    return w.rearrange("(k p) n -> p k n", p=P)[:, :, bass.ds(c0, 256)]


def wide(w, r0, c0):
    return w[bass.ds(r0, 512), c0:c0 + 512].rearrange("(k p) n -> p k n", p=P)


def load_unit(k, sp, u, src, slot):
    if not (isinstance(u, int) and u < RAW_SLOTS):
        sp.wait_ge(k.lo_done, u - RAW_SLOTS + 1)
    kt = src.shape[1]
    dst = k.raw[:, slot, :].rearrange("p (k n) -> p k n", k=kt)
    sp.dma_start(dst, src).then_inc(k.raw_landed[slot], 16)


def load_ahead(k, sp, u0, srcs):
    for j, src in enumerate(srcs):
        load_unit(k, sp, u0 + j, src, (u0 + j) % RAW_SLOTS)
    k.loaded = len(srcs)


def landed_value(u, slot):
    return (u - slot) * (16 // RAW_SLOTS) + 16


def split_hi(k, act, u, slot, used):
    act.wait_ge(k.raw_landed[slot], landed_value(u, slot))
    if used is not None:
        act.wait_ge(k.tile_full, used)
    k.nc.scalar.copy(k.whi[:, slot % SPLIT_SLOTS, :], k.raw[:, slot, :]).then_inc(k.hi_done, 1)


def split_lo(k, eng, u, slot):
    eng.wait_ge(k.hi_done, u + 1)
    s = slot % SPLIT_SLOTS
    eng.tensor_tensor(k.wlo[:, s, :], k.raw[:, slot, :], k.whi[:, s, :].bitcast(F32),
                      ALU.subtract).then_inc(k.lo_done, 1)


def product(pe, ps, whi, wlo, xhi, xlo, first, last):
    for n, (w, x) in enumerate(((whi, xhi), (whi, xlo), (wlo, xhi))):
        for b, half in enumerate(HALVES):
            mm = pe.matmul(ps[:, b, 0:HT], w, x[:, half], start=first and n == 0, stop=last and n == 2)
    return mm


def halves(ps, n=P):
    return ps[0:n, :, 0:HT]


def two(ap):
    return ap.rearrange("p (b t) -> p b t", b=2)


def unit_tiles(k, pe, u, slot, kts, xhi, xlo, first_slot, tile_free, x_ready=None):
    pe.wait_ge(k.lo_done, u + 1)
    s = slot % SPLIT_SLOTS
    whi = k.whi[:, s, :].rearrange("p (k n) -> p k n", k=kts)
    wlo = k.wlo[:, s, :].rearrange("p (k n) -> p k n", k=kts)
    def one(m, kt):
        cols = slice(m * P, (m + 1) * P)
        return product(pe, k.ps[first_slot + m], whi[:, kt, cols], wlo[:, kt, cols], xhi[:, kt, :],
                       xlo[:, kt, :], kt == 0, kt == kts - 1)
    tiles = range(UNIT // kts // P)
    if x_ready is not None:
        for kt in range(kts):
            x_ready(kt)
            for m in tiles:
                mm = one(m, kt)
                if kt == kts - 1:
                    mm.then_inc(k.tile_full, 1)
        return
    for m in tiles:
        tile_free(m)
        for kt in range(kts):
            mm = one(m, kt)
        mm.then_inc(k.tile_full, 1)



def steps(eng, n, step, first, last):
    first()
    step(0, 0)
    loops = (n - 2) // 2 if n > 4 else 0
    if loops:
        with eng.Fori(0, loops) as i:
            step(i * 2 + 1, 1)
            step(i * 2 + 2, 0)
    for g in range(1 + 2 * loops, n - 1):
        step(g, g % 2)
    last()


def first_units(up_cols):
    return [up_cols(0, 0), up_cols(0, 1), up_cols(1, 0), up_cols(1, 1)]


def up_down(k, name, n, up_cols, w_down, activate, acc, acc_new, norm=None, then=()):
    nc = k.nc
    u0, t0, loaded = k.unit, k.tile, k.loaded
    norm = norm or NoNorm()
    with ExitStack() as ctx:
        sb = lambda nm, shape, dt=F32: ctx.enter_context(nc.sbuf_tensor(f"{name}_{nm}", shape, dt))
        ahi, alo = sb("ahi", [P, 2, 4, T], F32R), sb("alo", [P, 2, 4, T], F32R)
        k.a = sb("a", [P, 2, T])
        k.b = sb("b", [P, 2, T])
        s = Named(
            up_free=k.sem(f"{name}_up_free"), a_ready=k.sem(f"{name}_a_ready"),
            hi=k.sem(f"{name}_hi"), lo=k.sem(f"{name}_lo"), down_free=k.sem(f"{name}_down_free"))
        step_unit = lambda g: u0 + 2 + 4 * g
        step_tile = lambda g: t0 + 4 + 12 * g
        slot = lambda j: (u0 + 2 + j) % RAW_SLOTS
        up_tile = lambda g: t0 if isinstance(g, int) and g == 0 else step_tile(g - 1)
        def down_tile(g):
            return t0 + 12 * g + (4 if isinstance(g, int) and g == n - 1 else 8)
        norm.open(k, ctx)

        block = ctx.enter_context(stage(k))

        @block.sync
        def _(sp):
            def down(g, j):
                return wide(w_down, g * 512, 512 * j)
            norm.sync(k, sp)
            def first():
                for j in range(loaded, 2):
                    load_unit(k, sp, u0 + j, up_cols(0, j), (u0 + j) % RAW_SLOTS)
            def step(g, par):
                for j in range(2):
                    if not (isinstance(g, int) and g == 0 and 2 + j < loaded):
                        load_unit(k, sp, step_unit(g) + j, up_cols(g + 1, j), slot(j))
                for j in range(2):
                    load_unit(k, sp, step_unit(g) + 2 + j, down(g, j), slot(2 + j))
            def last():
                for j in range(2):
                    load_unit(k, sp, step_unit(n - 1) + j, down(n - 1, j), slot(j))
            steps(sp, n, step, first, last)
            load_ahead(k, sp, u0 + 4 * n, then)

        @block.scalar
        def _(act):
            def hi_tile(g, m, par):
                act.wait_ge(s.a_ready, 4 * g + m + 1)
                if not (isinstance(g, int) and g < 2):
                    if m == 0:
                        act.wait_ge(k.tile_full, down_tile_end(g - 2))
                nc.scalar.copy(ahi[:, par, m, :], k.a[:, m % 2, :]).then_inc(s.hi, 1)
            def down_tile_end(g):
                return t0 + 12 * g + 16
            def ups(g, par, tiles):
                for m in tiles:
                    if not (isinstance(g, int) and g == 0 and m < 2):
                        act.wait_ge(s.lo, 4 * g + m - 1)
                    act.wait_ge(k.tile_full, up_tile(g) + m + 1)
                    activate.act(k, act, s, g, m, k.ps[m])
                    hi_tile(g, m, par)
            def first():
                norm.act_sum(k, act)
                split_hi(k, act, u0, u0 % RAW_SLOTS, t0 if u0 else None)
                norm.act(k, act)
                split_hi(k, act, u0 + 1, (u0 + 1) % RAW_SLOTS, t0 if u0 else None)
                split_hi(k, act, u0 + 2, (u0 + 2) % RAW_SLOTS, t0 + 2)
                ups(0, 0, (0, 1))
                split_hi(k, act, u0 + 3, (u0 + 3) % RAW_SLOTS, t0 + 4)
                ups(0, 0, (2, 3))
            def step(g, par):
                split_hi(k, act, step_unit(g) + 2, slot(2), step_tile(g) + 2)
                ups(g + 1, 1 - par, (0, 1))
                split_hi(k, act, step_unit(g) + 3, slot(3), step_tile(g) + 4)
                ups(g + 1, 1 - par, (2, 3))
                split_hi(k, act, step_unit(g) + 4, slot(0), step_tile(g) + 8)
                split_hi(k, act, step_unit(g) + 5, slot(1), step_tile(g) + 12)
            def last():
                pass
            steps(act, n, step, first, last)

        @block.vector
        def _(dve):
            def lo_tile(g, m, par):
                dve.wait_ge(s.hi, 4 * g + m + 1)
                dve.tensor_tensor(alo[:, par, m, :], k.a[:, m % 2, :], ahi[:, par, m, :].bitcast(F32),
                                  ALU.subtract).then_inc(s.lo, 1)
            def ups(g, par, tiles):
                for m in tiles:
                    activate.dve(k, dve, s, g, m, k.ps[m])
                    lo_tile(g, m, par)
            def one_down(g, j):
                dve.wait_ge(k.tile_full, down_tile(g) + j + 1)
                if acc_new and isinstance(g, int) and g == 0:
                    dve.tensor_copy(two(acc[:, j, :]), halves(k.ps[j % 4])).then_inc(s.down_free, 1)
                    return
                if not (isinstance(g, int) and g == 0):
                    dve.wait_ge(s.down_free, 8 * g - 8 + j + 1)
                dve.tensor_tensor(two(acc[:, j, :]), two(acc[:, j, :]), halves(k.ps[j % 4]),
                                  ALU.add).then_inc(s.down_free, 1)
            def downs(g, tiles):
                for j in tiles:
                    one_down(g, j)
            def first():
                norm.dve_sum(k, dve)
                split_lo(k, dve, u0, u0 % RAW_SLOTS)
                norm.dve(k, dve)
                for j in range(1, 3):
                    split_lo(k, dve, u0 + j, (u0 + j) % RAW_SLOTS)
                ups(0, 0, (0, 1))
                split_lo(k, dve, u0 + 3, (u0 + 3) % RAW_SLOTS)
                ups(0, 0, (2, 3))
            def step(g, par):
                split_lo(k, dve, step_unit(g) + 2, slot(2))
                ups(g + 1, 1 - par, (0, 1))
                split_lo(k, dve, step_unit(g) + 3, slot(3))
                ups(g + 1, 1 - par, (2, 3))
                downs(g, range(4))
                split_lo(k, dve, step_unit(g) + 4, slot(0))
                downs(g, range(4, 8))
                split_lo(k, dve, step_unit(g) + 5, slot(1))
            def last():
                downs(n - 1, range(8))
            steps(dve, n, step, first, last)

        @block.tensor
        def _(pe):
            def up(g, ub, us, par, prev):
                for j in range(2):
                    def free(m, j=j):
                        if prev is not None:
                            prev(2 * j + m)
                    unit_tiles(k, pe, ub + j, us[j], 8, k.xhi, k.xlo, 2 * j, free,
                               norm.x_ready(k, pe) if prev is None and j == 0 else None)
            def down(g, ub, us, par, prev):
                pe.wait_ge(s.lo, 4 * g + 4)
                for j in range(2):
                    def free(m, j=j):
                        if j == 0:
                            prev(m)
                        else:
                            pe.wait_ge(s.down_free, 8 * g + m + 1)
                    unit_tiles(k, pe, ub + j, us[j], 4, ahi[:, par], alo[:, par], 0, free)
            def first():
                norm.pe(k, pe)
                up(0, u0, [(u0 + j) % RAW_SLOTS for j in range(2)], 0, None)
            def step(g, par):
                if isinstance(g, int) and g == 0:
                    freed = lambda m: pe.wait_ge(s.up_free, m + 1)
                else:
                    freed = lambda m: pe.wait_ge(s.down_free, 8 * g - 4 + m + 1)
                up(g + 1, step_unit(g), (slot(0), slot(1)), 1 - par, freed)
                down(g, step_unit(g) + 2, (slot(2), slot(3)), par,
                     lambda m: pe.wait_ge(s.up_free, 4 * g + 4 + m + 1))
            def last():
                down(n - 1, step_unit(n - 1), (slot(0), slot(1)), (n - 1) % 2,
                     lambda m: pe.wait_ge(s.down_free, 8 * n - 16 + 4 + m + 1))
            steps(pe, n, step, first, last)
    k.unit += 4 * n
    k.tile += 12 * n


class SquaredRelu:

    def act(self, k, act, s, g, m, ps):
        k.nc.scalar.activation(two(k.b[:, m % 2, :]), halves(ps), ACT.Relu).then_inc(s.up_free, 1)
        act.wait_ge(s.up_free, 4 * g + m + 1)
        k.nc.scalar.square(k.a[:, m % 2, :], k.b[:, m % 2, :]).then_inc(s.a_ready, 1)

    def dve(self, k, dve, s, g, m, ps):
        pass



class NoNorm:

    def open(self, k, ctx):
        pass

    def sync(self, k, sp):
        pass

    act_sum = act = dve_sum = dve = pe = sync

    def x_ready(self, k, pe):
        return None


class RmsNorm:

    def __init__(self, name, src, gain_row):
        self.name, self.src, self.gain_row = name, src, gain_row

    def open(self, k, ctx):
        sb = lambda nm, shape: ctx.enter_context(k.nc.sbuf_tensor(f"{self.name}_{nm}", shape, F32))
        self.sq, self.gain, self.rinv, self.y = sb("sq", [P, 4, T]), sb("gain", [P, KD]), sb("rinv", [P, T]), None
        sem = lambda nm: k.sem(f"{self.name}_{nm}")
        self.gain_in, self.squared, self.paired, self.summed = (sem(x) for x in ("gain", "squared", "paired", "summed"))
        self.log, self.inv, self.scaled, self.hi, self.lo = (sem(x) for x in ("log", "inv", "scaled", "hi", "lo"))
        self.y = self.sq

    def sync(self, k, sp):
        with k.nc.allow_non_contiguous_dma(reason="1024 gains, feature on partitions"):
            sp.dma_start(self.gain[:, :], self.gain_row.rearrange("(k p) -> p k", p=P)).then_inc(self.gain_in, 16)

    def act_sum(self, k, act):
        k.nc.scalar.preload_act_table_set("natural_log_exp_and_others")
        for t in range(KD):
            if t >= 4:
                act.wait_ge(self.summed, t // 2 - 1)
            k.nc.scalar.square(self.sq[:, t % 4, :], self.src[:, t, :]).then_inc(self.squared, 1)

    def dve_sum(self, k, dve):
        for n in range(KD // 2):
            t = 2 * n
            dve.wait_ge(self.squared, t + 2)
            dve.tensor_tensor(self.sq[:, t % 4, :], self.sq[:, t % 4, :], self.sq[:, t % 4 + 1, :], ALU.add)\
                .then_inc(self.paired, 1)

    def pe(self, k, pe):
        for n in range(KD // 2):
            pe.wait_ge(self.paired, n + 1)
            for b, half in enumerate(HALVES):
                mm = pe.matmul(k.ps[3][:, b, 0:HT], k.ones[:, :], self.sq[:, 2 * n % 4, half], start=n == 0,
                               stop=n == KD // 2 - 1)
            mm.then_inc(self.summed, 1)

    def act_root(self, k, act):
        act.wait_ge(self.summed, KD // 2)
        k.nc.scalar.activation(two(self.rinv[:, :]), halves(k.ps[3]), ACT.Ln, scale=1.0 / D, bias=k.eps[:, :])\
            .then_inc(self.log, 1)
        act.wait_ge(self.log, 1)
        k.nc.scalar.activation(self.rinv[:, :], self.rinv[:, :], ACT.Exp, scale=-0.5).then_inc(self.inv, 1)

    def act(self, k, act):
        self.act_root(k, act)
        for t in range(KD):
            act.wait_ge(self.scaled, t + 1)
            k.nc.scalar.copy(k.xhi[:, t, :], self.y[:, t % 4, :]).then_inc(self.hi, 1)

    def dve(self, k, dve):
        dve.wait_ge(self.gain_in, 16)
        dve.wait_ge(self.inv, 1)
        def take_lo(t):
            dve.wait_ge(self.hi, t + 1)
            dve.tensor_tensor(k.xlo[:, t, :], self.y[:, t % 4, :], k.xhi[:, t, :].bitcast(F32), ALU.subtract)\
                .then_inc(self.lo, 1)
        for t in range(KD):
            if t >= 4:
                dve.wait_ge(self.lo, t - 3)
            dve.scalar_tensor_tensor(out=self.y[:, t % 4, :], in0=self.src[:, t, :], scalar=self.gain[:, t:t + 1],
                                     in1=self.rinv[:, :], op0=ALU.mult, op1=ALU.mult).then_inc(self.scaled, 1)
            if t >= 1:
                take_lo(t - 1)
        take_lo(KD - 1)

    def x_ready(self, k, pe):
        return lambda kt: pe.wait_ge(self.lo, kt + 1)


def load_tokens(k, x, meta):
    nc = k.nc
    with ExitStack() as ctx:
        tok = ctx.enter_context(nc.sbuf_tensor("tok", [P, 1 + NCH, D], F32))
        ident_made, zeroed = k.sem("ident_made"), k.sem("ident_zeroed")
        landed = [k.sem(f"tok_landed{c}") for c in range(1 + NCH)]
        turned = k.sem("tok_turned")
        stored = [k.sem("tok_stored_dve"), k.sem("tok_stored_act")]
        block = ctx.enter_context(stage(k))

        @block.sync
        def _(sp):
            for c, (t0, n) in enumerate(chunks()):
                src = meta if c == 0 else x[0, t0 - META:t0 - META + n, :]
                sp.dma_start(tok[0:n, c, :], src).then_inc(landed[c], 16)

        @block.gpsimd
        def _(pool):
            pool.memset(k.eps[:, :], EPS).then_inc(zeroed, 1)
            pool.memset(k.ones[:, :], 1.0).then_inc(zeroed, 1)
            pool.wait_ge(zeroed, 2)
            nc.gpsimd.affine_select(out=k.ident[:, :], in_=k.ones[:, :], compare_op=ALU.is_equal, fill=0.0, base=0,
                                    pattern=[[-1, P]], channel_multiplier=1).then_inc(ident_made, 1)

        @block.tensor
        def _(pe):
            pe.wait_ge(ident_made, 1)
            for c, (t0, n) in enumerate(chunks()):
                pe.wait_ge(landed[c], 16)
                if c >= 2:
                    for st in stored:
                        pe.wait_ge(st, c - 1)
                for t in range(KD):
                    mm = pe.transpose(k.ps[2 * (c % 2) + t // 4][:, t % 4 // 2, t % 2 * P:t % 2 * P + n],
                                      tok[0:n, c, t * P:(t + 1) * P], k.ident[0:n, 0:n])
                    if t % 4 == 3:
                        mm.then_inc(turned, 1)

        def store(eng, copy, half):
            for c, (t0, n) in enumerate(chunks()):
                eng.wait_ge(turned, 2 * c + half + 1)
                src = k.ps[2 * (c % 2) + half][:, :, 0:2 * P].rearrange("p b (t n) -> p b t n", t=2)[:, :, :, 0:n]
                dst = k.h[:, 4 * half:4 * half + 4, t0:t0 + n].rearrange("p (b t) n -> p b t n", b=2)
                copy(dst, src).then_inc(stored[half], 1)

        @block.vector
        def _(dve):
            store(dve, nc.vector.tensor_copy, 0)

        @block.scalar
        def _(act):
            nc.scalar.preload_act_table_set("natural_log_exp_and_others")
            store(act, nc.scalar.copy, 1)


def store_tokens(k, src, out):
    nc = k.nc
    with ExitStack() as ctx:
        tok = ctx.enter_context(nc.sbuf_tensor("tok_out", [P, NCH, D], F32))
        turned, written = k.sem("out_turned"), k.sem("out_written")
        stored = [k.sem("out_stored_dve"), k.sem("out_stored_act")]
        block = ctx.enter_context(stage(k))

        @block.tensor
        def _(pe):
            for c in range(NCH):
                t0 = META + CH * c
                if c >= 2:
                    for st in stored:
                        pe.wait_ge(st, c - 1)
                for t in range(KD):
                    mm = pe.transpose(k.ps[2 * (c % 2) + t // 4][:, t % 4 // 2, t % 2 * P:(t % 2 + 1) * P],
                                      src[:, t, t0:t0 + CH], k.ident[:, :])
                    if t % 4 == 3:
                        mm.then_inc(turned, 1)

        def store(eng, copy, half):
            for c in range(NCH):
                eng.wait_ge(turned, 2 * c + half + 1)
                dst = tok[:, c, 512 * half:512 * half + 512].rearrange("p (b n) -> p b n", b=2)
                copy(dst, k.ps[2 * (c % 2) + half][:, :, 0:2 * P]).then_inc(stored[half], 1)

        @block.vector
        def _(dve):
            store(dve, nc.vector.tensor_copy, 0)

        @block.scalar
        def _(act):
            store(act, nc.scalar.copy, 1)

        @block.sync
        def _(sp):
            for c in range(NCH):
                for st in stored:
                    sp.wait_ge(st, c + 1)
                sp.dma_start(out[0, CH * c:CH * (c + 1), :], tok[:, c, :]).then_inc(written, 16)
            sp.wait_ge(written, 16 * NCH)


def rounds(eng, n, body, period=2):
    for j in range(min(period, n)):
        body(j, j % period)
    loops = (n - 2 * period) // period
    if loops > 1:
        with eng.Fori(0, loops) as i:
            for r in range(period):
                body(i * period + period + r, r)
    else:
        loops = 0
    for j in range(period + period * loops, n):
        body(j, j % period)


def split_rings(k, name, ctx):
    sb = lambda nm, shape, dt: ctx.enter_context(k.nc.sbuf_tensor(f"{name}_{nm}", shape, dt))
    k.xhi, k.xlo = sb("xhi", [P, KD, T], F32R), sb("xlo", [P, KD, T], F32R)


def weight_ring(k, name, ctx):
    sb = lambda nm, shape, dt: ctx.enter_context(k.nc.sbuf_tensor(f"{name}_{nm}", shape, dt))
    k.whi, k.wlo = sb("whi", [P, SPLIT_SLOTS, UNIT], F32R), sb("wlo", [P, SPLIT_SLOTS, UNIT], F32R)



class NoSide:

    def open(self, k, ctx):
        pass

    def sync(self, k, sp):
        pass

    def act(self, k, act, n):
        pass

    dve = pe = act
    free = free1 = sync
    slot1 = False


def project(k, name, n, cols, leave, norm=None, then=(), side=None):
    side = side or NoSide()
    u0, t0, loaded = k.unit, k.tile, k.loaded
    norm = norm or NoNorm()
    body = 4
    with ExitStack() as ctx:
        leave.open(k, name, ctx)
        free = leave.free
        norm.open(k, ctx)
        side.open(k, ctx)
        block = ctx.enter_context(stage(k))

        def walk(eng, one):
            loops = n // body - 1
            for u in range(min(n, body)):
                one(u, u)
            if loops > 1:
                with eng.Fori(0, loops) as i:
                    for r in range(body):
                        one(i * body + body + r, r)
            else:
                loops = 0
            for u in range(body * (1 + loops), n):
                one(u, u % body)

        def walk_split(eng, one):
            loops = n // body - 2
            for u in range(min(n, body)):
                one(u, u)
            if loops > 1:
                with eng.Fori(0, loops) as i:
                    for r in range(body):
                        one(i * body + body + r, r)
            else:
                loops = 0
            for u in range(body * (1 + loops), n):
                one(u, u % body)

        ring = lambda r: (u0 + r) % RAW_SLOTS

        @block.sync
        def _(sp):
            norm.sync(k, sp)
            def one(u, r):
                if not (isinstance(u, int) and u < loaded):
                    load_unit(k, sp, u0 + u, cols(u), ring(r))
                if isinstance(u, int) and u == 1:
                    leave.sync(k, sp)
                    side.sync(k, sp)
            walk(sp, one)
            load_ahead(k, sp, u0 + n, then)

        @block.scalar
        def _(act):
            norm.act_sum(k, act)
            split_hi(k, act, u0, ring(0), t0 if u0 else None)
            norm.act(k, act)
            split_hi(k, act, u0 + 1, ring(1), t0 if u0 else None)
            side.act(k, act, 0)

            def one(u, r):
                for m in range(2):
                    leave.act(k, act, 2 * u + m, (2 * r + m) % 4, t0)
                if not (isinstance(u, int) and u + 2 >= n):
                    split_hi(k, act, u0 + u + 2, ring(r + 2), t0 + 2 * u + 2)
                if isinstance(u, int):
                    side.act(k, act, u + 1)
            walk_split(act, one)
            leave.act_end(k, act, 2 * n, t0)

        @block.vector
        def _(dve):
            leave.dve_start(k, dve)
            side.dve(k, dve, -1)
            norm.dve_sum(k, dve)
            split_lo(k, dve, u0, ring(0))
            norm.dve(k, dve)
            split_lo(k, dve, u0 + 1, ring(1))
            side.dve(k, dve, 0)

            def one(u, r):
                for m in range(2):
                    leave.dve(k, dve, 2 * u + m, (2 * r + m) % 4, t0)
                if not (isinstance(u, int) and u + 2 >= n):
                    split_lo(k, dve, u0 + u + 2, ring(r + 2))
                if isinstance(u, int):
                    side.dve(k, dve, u + 1)
            walk_split(dve, one)
            leave.dve_end(k, dve, 2 * n, t0)

        @block.tensor
        def _(pe):
            norm.pe(k, pe)
            def one(u, r):
                def tile_free(m):
                    if not (isinstance(u, int) and u < 2):
                        free(pe, 2 * u + m - 4)
                        if isinstance(u, int) and u == 4 and m == 1:
                            side.free1(k, pe)
                    elif u == 1 and m == 1:
                        side.free(k, pe)
                unit_tiles(k, pe, u0 + u, ring(r), KD, k.xhi, k.xlo, 2 * (r % 2), tile_free,
                           norm.x_ready(k, pe) if isinstance(u, int) and u == 0 else None)
                if isinstance(u, int):
                    if u == 3 and side.slot1:
                        free(pe, 5)
                    side.pe(k, pe, u + 1)
            walk(pe, one)
    k.unit += n
    k.tile += 2 * n


class ConvSilu:

    def __init__(self, dst, conv, c0):
        self.dst, self.conv = dst, conv[:, c0:c0 + dst.shape[1] * P]

    def open(self, k, name, ctx):
        nc = k.nc
        sb = lambda nm, shape: ctx.enter_context(nc.sbuf_tensor(f"{name}_{nm}", shape, F32))
        self.taps = self.conv.shape[0]
        self.tiles = self.conv.shape[1] // P
        self.w = sb("convw", [P, self.taps, self.tiles])
        self.pre = sb("pre", [P, 2, T + self.taps - 1])
        self.y = sb("y", [P, 2, T])
        self.w_in, self.zeroed = k.sem(f"{name}_convw_in"), k.sem(f"{name}_zeroed")
        self.out = k.sem(f"{name}_left")
        self.tapped = k.sem(f"{name}_tapped")
        self.done = k.sem(f"{name}_silu")

    def free(self, pe, j):
        pe.wait_ge(self.out, 2 * j + 2)

    def sync(self, k, sp):
        with k.nc.allow_non_contiguous_dma(reason="small table, feature on partitions"):
            for i in range(self.taps):
                sp.dma_start(self.w[:, i, :], self.conv[i].rearrange("(t p) -> p t", p=P)).then_inc(self.w_in, 16)

    def dve_start(self, k, dve):
        dve.memset(self.pre[:, :, 0:self.taps - 1], 0.0).then_inc(self.zeroed, 1)

    def act(self, k, act, j, r, t0):
        b, last = r % 2, self.taps - 1
        if isinstance(j, int) and j == 0:
            act.wait_ge(self.w_in, 16 * self.taps)
        act.wait_ge(k.tile_full, t0 + j + 1)
        if not (isinstance(j, int) and j < 2):
            act.wait_ge(self.tapped, last * (j - 1))
            act.wait_ge(self.done, j - 1)
        k.nc.scalar.copy(two(self.pre[:, b, last:last + T]), halves(k.ps[r])).then_inc(self.out, 1)
        k.nc.scalar.activation(two(self.y[:, b, :]), halves(k.ps[r]), ACT.Copy,
                               scale=self.w[:, last, bass.ds(j, 1)]).then_inc(self.out, 1)
        if not (isinstance(j, int) and j == 0):
            self.silu(k, act, j - 1, 1 - b)

    def silu(self, k, act, j, b):
        act.wait_ge(self.tapped, (self.taps - 1) * (j + 1))
        k.nc.scalar.activation(self.dst[:, bass.ds(j, 1), :].rearrange("p o t -> p (o t)"), self.y[:, b, :],
                               ACT.Silu).then_inc(self.done, 1)

    def act_end(self, k, act, n, t0):
        self.silu(k, act, n - 1, (n - 1) % 2)

    def dve(self, k, dve, j, r, t0):
        b = r % 2
        if isinstance(j, int) and j == 0:
            dve.wait_ge(self.w_in, 16 * self.taps)
            dve.wait_ge(self.zeroed, 1)
        for i in range(self.taps - 1):
            if i == 0:
                dve.wait_ge(self.out, 2 * j + 2)
            else:
                dve.wait_ge(self.tapped, (self.taps - 1) * j + i)
            dve.scalar_tensor_tensor(out=self.y[:, b, :], in0=self.pre[:, b, i:i + T],
                                     scalar=self.w[:, i, bass.ds(j, 1)], in1=self.y[:, b, :],
                                     op0=ALU.mult, op1=ALU.add).then_inc(self.tapped, 1)

    def dve_end(self, k, dve, n, t0):
        pass


def head_norm(k, name, n, tile, ones, scale, gain, gain_src=None, then=()):
    nc = k.nc
    with ExitStack() as ctx:
        sb = lambda nm, shape: ctx.enter_context(nc.sbuf_tensor(f"{name}_{nm}", shape, F32))
        sq, rinv = sb("sq", [P, 4, T]), sb("rinv", [P, 4, T])
        g = sb("g", [P, n]) if gain_src is not None else None
        sem = lambda nm: k.sem(f"{name}_{nm}")
        gain_in, squared, summed, log, inv, done = (sem(x) for x in (
            "gain_in", "squared", "summed", "log", "inv", "done"))
        past4 = lambda j: not (isinstance(j, int) and j < 4)
        block = ctx.enter_context(stage(k))

        @block.sync
        def _(sp):
            if gain_src is not None:
                with nc.allow_non_contiguous_dma(reason="gains, feature on partitions"):
                    sp.dma_start(g[:, 0:gain_src.shape[1]], gain_src).then_inc(gain_in, 16)
            if then:
                load_ahead(k, sp, k.unit, then)

        @block.gpsimd
        def _(pool):
            def square(j, b):
                if past4(j):
                    pool.wait_ge(summed, j - 3)
                pool.tensor_tensor(sq[:, b, :], tile(j), tile(j), ALU.mult).then_inc(squared, 1)
            rounds(pool, n, square, 4)

        @block.tensor
        def _(pe):
            def one(j, b):
                pe.wait_ge(squared, j + 1)
                if past4(j):
                    pe.wait_ge(log, j - 3)
                for hf, half in enumerate(HALVES):
                    mm = pe.matmul(k.ps[b][:, hf, 0:HT], ones, sq[:, b, half], start=True, stop=True)
                mm.then_inc(summed, 1)
            rounds(pe, n, one, 4)

        @block.scalar
        def _(act):
            def logarithm(j, b):
                act.wait_ge(summed, j + 1)
                if past4(j):
                    act.wait_ge(done, j - 3)
                nc.scalar.activation(two(rinv[:, b, :]), halves(k.ps[b]), ACT.Ln, scale=scale, bias=k.eps[:, :])\
                    .then_inc(log, 1)
            def one(j, b):
                if not (isinstance(j, int) and j == n - 1):
                    logarithm(j + 1, (b + 1) % 4)
                act.wait_ge(log, j + 1)
                nc.scalar.activation(rinv[:, b, :], rinv[:, b, :], ACT.Exp, scale=-0.5).then_inc(inv, 1)
            nc.scalar.preload_act_table_set("natural_log_exp_and_others")
            logarithm(0, 0)
            rounds(act, n, one, 4)

        @block.vector
        def _(dve):
            if gain_src is not None:
                dve.wait_ge(gain_in, 16)
            def one(j, b):
                dve.wait_ge(inv, j + 1)
                dve.scalar_tensor_tensor(out=tile(j), in0=tile(j), scalar=gain(g, j), in1=rinv[:, b, :],
                                         op0=ALU.mult, op1=ALU.mult).then_inc(done, 1)
            rounds(dve, n, one, 4)



GV, GQ = 16, 8
GRP = 4
NG = GV // GRP


def gate_rows(k, name, ctx, w_cols, rows):
    sb = lambda nm, shape, dt=F32: ctx.enter_context(k.nc.sbuf_tensor(f"{name}_{nm}", shape, dt))
    s = Named(rows=rows, w_cols=w_cols)
    s.raw = sb("gw", [P, KD, rows])
    s.hi, s.lo = sb("gwhi", [P, KD, rows], F32R), sb("gwlo", [P, KD, rows], F32R)
    s.cleared, s.landed = k.sem(f"{name}_gw_cleared"), k.sem(f"{name}_gw_landed")
    s.hi_done, s.lo_done, s.ready = (k.sem(f"{name}_{x}") for x in ("gw_hi", "gw_lo", "gate_ready"))
    return s


def gate_load(k, sp, s):
    sp.wait_ge(s.cleared, 1)
    for w, r in s.w_cols:
        sp.dma_start(s.raw[:, :, r:r + w.shape[1]], w.rearrange("(k p) n -> p k n", p=P)).then_inc(s.landed, 16)


def gate_hi(k, act, s):
    act.wait_ge(s.landed, 16 * len(s.w_cols))
    k.nc.scalar.copy(s.hi[:, :, :], s.raw[:, :, :]).then_inc(s.hi_done, 1)


def gate_clear(k, dve, s):
    dve.memset(s.raw[:, :, :], 0.0).then_inc(s.cleared, 1)


def gate_lo(k, dve, s):
    dve.wait_ge(s.hi_done, 1)
    dve.tensor_tensor(s.lo[:, :, :], s.raw[:, :, :], s.hi[:, :, :].bitcast(F32), ALU.subtract).then_inc(s.lo_done, 1)


def gate_product(k, pe, s, ps):
    pe.wait_ge(s.lo_done, 1)
    for kt in range(KD):
        for n, (w, x) in enumerate(((s.hi, k.xhi), (s.hi, k.xlo), (s.lo, k.xhi))):
            for b, half in enumerate(HALVES):
                mm = pe.matmul(ps[0:s.rows, b, 0:HT], w[:, kt, :], x[:, kt, half],
                               start=kt == 0 and n == 0, stop=kt == KD - 1 and n == 2)
    mm.then_inc(s.ready, 1)


def chunk_scan_mask(dve, mask, made):
    dve.memset(mask, 1.0).then_inc(made, 1)
    dve.wait_ge(made, 1)
    for n, (t, _) in enumerate(chunks()):
        ins = dve.memset(mask[:, t:t + 1], 0.0).then_inc(made, 1)


class GdnGates:

    slot1 = True

    def __init__(self, g, w_in, a_log, dt_bias):
        self.g, self.w_in, self.a_log, self.dt_bias = g, w_in, a_log, dt_bias

    def open(self, k, ctx):
        sb = lambda nm, shape: ctx.enter_context(k.nc.sbuf_tensor(f"gdng_{nm}", shape, F32))
        c0 = 2 * GQ * P + 2 * GV * P
        self.s = gate_rows(k, "gdng", ctx, [(self.w_in[:, c0 + GV:c0 + 2 * GV], 0), (self.w_in[:, c0:c0 + GV], 32)], 48)
        self.par = sb("par", [GV, 3])
        self.y, self.e, self.mask = sb("y", [GV, T]), sb("e", [GV, T]), sb("mask", [GV, T])
        self.beta = sb("beta", [48, T])
        self.par_in, self.act_step, self.dve_step, self.made, self.turned, self.tok_done = (
            k.sem(f"gdng_{x}") for x in ("par_in", "act", "dve", "mask_made", "turned", "tok"))
        self.spare = [k.ps[1][:, b, 0:32 * (1 + NCH)] for b in range(2)]

    def sync(self, k, sp):
        with k.nc.allow_non_contiguous_dma(reason="a few gate weights and parameters"):
            sp.dma_start(self.par[:, 0:1], self.a_log.rearrange("(h o) -> h o", o=1)).then_inc(self.par_in, 16)
            sp.dma_start(self.par[:, 1:2], self.dt_bias.rearrange("(h o) -> h o", o=1)).then_inc(self.par_in, 16)
            gate_load(k, sp, self.s)

    def free(self, k, pe):
        pe.wait_ge(self.act_step, 3)
        pe.wait_ge(self.dve_step, 1)

    def free1(self, k, pe):
        pe.wait_ge(self.tok_done, 5)

    def pe(self, k, pe, n):
        if n == 1:
            gate_product(k, pe, self.s, k.ps[3])
        if n == 4:
            pe.wait_ge(self.dve_step, 6)
            for c, (t, m) in enumerate(chunks()):
                pe.transpose(self.spare[0][0:m, 32 * c:32 * c + GV], self.g.cum[0:GV, t:t + m], k.ident[0:GV, 0:GV])
                mm = pe.transpose(self.spare[1][0:m, 32 * c:32 * c + GV], self.beta[32:48, t:t + m],
                                  k.ident[32:48, 32:48])
            mm.then_inc(self.turned, 1)

    def act(self, k, act, n):
        e, par, step, scalar = self.e, self.par, self.act_step, k.nc.scalar
        if n == 0:
            gate_hi(k, act, self.s)
        if n == 1:
            act.wait_ge(self.par_in, 32)
            scalar.activation(par[:, 2:3], par[:, 0:1], ACT.Exp).then_inc(step, 1)
            act.wait_ge(self.s.ready, 1)
            scalar.activation(two(self.beta[32:48, :]), k.ps[3][32:48, :, 0:HT], ACT.Exp, scale=-1.0).then_inc(step, 1)
            scalar.activation(two(e[:, :]), k.ps[3][0:GV, :, 0:HT], ACT.Abs, bias=par[:, 1:2]).then_inc(step, 1)
            act.wait_ge(step, 3)
            scalar.activation(e[:, :], e[:, :], ACT.Exp, scale=-1.0).then_inc(step, 1)
            act.wait_ge(step, 4)
            scalar.activation(e[:, :], e[:, :], ACT.Ln, bias=k.ones[0:GV, 0:1]).then_inc(step, 1)
        if n == 5:
            act.wait_ge(self.tok_done, 3)
            scalar.activation(self.g.tok[:, :, 2, :], self.g.tok[:, :, 0, :], ACT.Exp).then_inc(step, 1)

    def dve(self, k, dve, n):
        g, y, e, par, beta, step, tok_done = self.g, self.y, self.e, self.par, self.beta, self.dve_step, self.tok_done
        if n == -1:
            gate_clear(k, dve, self.s)
        if n == 0:
            chunk_scan_mask(dve, self.mask[:, :], self.made)
            gate_lo(k, dve, self.s)
        if n == 1:
            dve.wait_ge(self.act_step, 3)
            dve.tensor_scalar(two(y[:, :]), k.ps[3][0:GV, :, 0:HT], par[:, 1:2], 0.0, ALU.add, ALU.max)\
                .then_inc(step, 1)
            dve.tensor_scalar(beta[32:48, :], beta[32:48, :], 1.0, None, ALU.add).then_inc(step, 1)
            dve.wait_ge(self.act_step, 5)
            dve.wait_ge(step, 2)
            dve.tensor_tensor(y[:, :], y[:, :], e[:, :], ALU.add).then_inc(step, 1)
            dve.reciprocal(beta[32:48, :], beta[32:48, :]).then_inc(step, 1)
            dve.wait_ge(step, 4)
            dve.tensor_scalar(y[:, :], y[:, :], par[:, 2:3], -1.0, ALU.mult, ALU.mult).then_inc(step, 1)
            dve.wait_ge(step, 5)
            dve.wait_ge(self.made, 1 + len(chunks()))
            dve.tensor_tensor_scan(g.cum[:, :], self.mask[:, :], y[:, :], 0.0, ALU.mult, ALU.add).then_inc(step, 1)
            dve.memset(g.tok[:, :, :, :], 0.0).then_inc(tok_done, 1)
        if n == 4:
            dve.wait_ge(self.turned, 1)
            dve.wait_ge(tok_done, 1)
            cols = lambda b, c0, c1: self.spare[b][:, 32 * c0:32 * c1].rearrange("p (c x) -> p c x", x=32)[:, :, 0:GV]
            parts = ((0, 1, META), (1, 1 + NCH, CH))
            for c0, c1, m in parts:
                dve.tensor_copy(g.tok[0:m, c0:c1, 0, :], cols(0, c0, c1)[0:m]).then_inc(tok_done, 1)
            for c0, c1, m in parts:
                dve.tensor_copy(g.beta[0:m, c0:c1, :], cols(1, c0, c1)[0:m]).then_inc(tok_done, 1)
            dve.wait_ge(tok_done, 5)
            for c0, c1, m in parts:
                dve.tensor_scalar(g.tok[0:m, c0:c1, 1, :], g.beta[0:m, c0:c1, :], -1.0, None, ALU.mult)\
                    .then_inc(tok_done, 1)
        if n == 6:
            dve.wait_ge(tok_done, 7)
            dve.wait_ge(self.act_step, 6)
            dve.tensor_tensor(g.tok[:, :, 2, :], g.tok[:, :, 2, :], g.tok[:, :, 1, :], ALU.mult).then_inc(tok_done, 1)


LEVELS = 7
SHORT = 4


def gdn_recurrence(k, g, qkv, vf):
    nc = k.nc
    with ExitStack() as ctx:
        sb = lambda nm, shape: ctx.enter_context(nc.sbuf_tensor(f"gdn_{nm}", shape, F32))
        raw = k.raw[:, :, :].rearrange("p s (g h n) -> p s g h n", g=NG, h=GRP)
        an, yt, xp = raw[:, 0], raw[:, 1], raw[:, 2]
        st = raw[:, 3]
        vc = xp
        new, new_dec = an, xp
        dt = sb("dt", [P, NG, GRP, CH])
        eq = sb("eq", [P, NG, GRP, CH])
        z = sb("z", [P, NG, 2 * CH])
        kt = z[:, :, :].rearrange("p g (h n) -> p g h n", h=2)
        vt = sb("vt", [P, NG, GRP, CH])
        kc = sb("kc", [P, GQ, CH])
        dl = sb("dl", [P, 2, GRP, CH])
        cc = sb("cc", [GV, CH])
        go = sb("go", [P, NG * LEVELS])
        kd, el = sb("kd", [P, GV]), sb("el", [P, GV])
        below, strict = sb("below", [P, CH]), sb("strict", [P, CH])
        lev = sb("lev", [P, LEVELS, CH // 2])
        names = ("masks", "k_staged", "v_staged", "y_staged", "bcast", "diffed", "clamped", "eq_exp", "d_exp", "gram", "small", "an_done",
                 "attn_done", "qd_done", "v_turned", "v_done", "z_ready", "z_done", "yz_ready", "y_done", "x_ready",
                 "x_done", "ks_ready", "r_done", "new_ready", "new_done", "dec_done", "o_ready", "o_done",
                 "kt_ready", "kt_done", "su_ready", "s_done", "s_zero", "cum_in")
        s = Named(**{x: k.sem(f"gdn_{x}") for x in names})
        bank_a = [k.ps[i][:, 0, :].rearrange("p (h n) -> p h n", h=GRP) for i in range(NG)]
        bank_b = [k.ps[i][:, 1, :].rearrange("p (h n) -> p h n", h=GRP) for i in range(NG)]
        zb = [k.ps[i][:, 0, 0:2 * CH] for i in range(NG)]
        yzb = [k.ps[i][:, 1, 0:2 * CH] for i in range(NG)]
        is0 = lambda c: isinstance(c, int) and c == 0
        levels = lambda c: SHORT if is0(c) else LEVELS
        first_token = lambda c: 0 if is0(c) else c * CH + (META - CH)
        q = lambda c, i: 4 * c + i
        lv = lambda c, l, i: 4 * l + i if is0(c) else c * (4 * LEVELS) + (4 * SHORT - 4 * LEVELS) + 4 * l + i

        part = lambda c, l, i: 4 * l + i if is0(c) else (c * (4 * (LEVELS - 1)) + 4 * (SHORT - LEVELS) + 4 * l + i)
        xr = part
        yr = lambda c, l, i: part(c, l - 1, i)

        def walk(eng, body):
            body(0, META)
            with eng.Fori(0, NCH) as i:
                body(i + 1, CH)

        block = ctx.enter_context(stage(k))

        @block.gpsimd
        def _(pool):
            pool.memset(below[:, :], 0.0).then_inc(s.masks, 1)
            pool.memset(strict[:, :], 0.0).then_inc(s.masks, 1)
            pool.memset(lev[:, :, :], 1.0).then_inc(s.masks, 1)
            pool.wait_ge(s.masks, 3)
            nc.gpsimd.affine_select(out=below[:, :], in_=below[:, :], compare_op=ALU.is_ge, fill=-1e30, base=0,
                                    pattern=[[1, CH]], channel_multiplier=-1).then_inc(s.masks, 1)
            nc.gpsimd.affine_select(out=strict[:, :], in_=strict[:, :], compare_op=ALU.is_ge, fill=1e30, base=-1,
                                    pattern=[[-1, CH]], channel_multiplier=1).then_inc(s.masks, 1)
            n = 5
            for l in range(LEVELS):
                hf, b = 1 << l, 2 << l
                for sign, base in ((1, 0), (-1, hf - 1)):
                    v = lev[:, l, :].rearrange("p (b w) -> p b w", w=hf)
                    nc.gpsimd.affine_select(out=v, in_=v, compare_op=ALU.is_ge, fill=0.0, base=base,
                                            pattern=[[-b * sign, CH // b], [0, hf]], channel_multiplier=sign)\
                        .then_inc(s.masks, 1)
                    n += 1
                    pool.wait_ge(s.masks, n)
            def body(c, n):
                t = first_token(c)
                if not is0(c):
                    pool.wait_ge(s.bcast, q(c - 1, NG - 1) + 1)
                pool.tensor_copy(cc[:, 0:n], g.cum[0:GV, bass.ds(t, n)]).then_inc(s.cum_in, 1)
                for i in range(NG):
                    if not is0(c):
                        pool.wait_ge(s.kt_ready, q(c - 1, i) + 1)
                    pool.tensor_copy(kc[:, 2 * i:2 * i + 2, 0:n],
                                     qkv[:, GQ + 2 * i:GQ + 2 * i + 2, bass.ds(t, n)]).then_inc(s.k_staged, 1)
                    pool.tensor_copy(yt[:, i, :, :], k.ident[:, :].unsqueeze(1).to_broadcast([P, GRP, CH]))\
                        .then_inc(s.y_staged, 1)
                for i in range(NG):
                    if not is0(c):
                        pool.wait_ge(s.su_ready, q(c - 1, i) + 1)
                    pool.tensor_copy(vc[:, i, :, 0:n],
                                     vf[:, GRP * i:GRP * (i + 1), bass.ds(t, n)]).then_inc(s.v_staged, 1)
                for i in range(NG):
                    pool.wait_ge(s.eq_exp, q(c, i) + 1)
                    e4 = eq[:, i, :, 0:n].rearrange("p (q o) n -> p q o n", o=2)
                    qs = qkv[:, 2 * i:2 * i + 2, bass.ds(t, n)]
                    pool.tensor_tensor(e4, e4, qs.unsqueeze(2).to_broadcast([P, 2, 2, n]), ALU.mult)\
                        .then_inc(s.qd_done, 1)
            walk(pool, body)

        @block.tensor
        def _(pe):
            def body(c, n):
                t = first_token(c)
                for i in range(NG):
                    pe.wait_ge(s.cum_in, c + 1)
                    if not is0(c):
                        pe.wait_ge(s.s_done, q(c - 1, i) + 1)
                    for h in range(GRP):
                        hd = GRP * i + h
                        mm = pe.matmul(bank_a[i][:, h, 0:n], k.ident[0:GV, hd:hd + 1].to_broadcast([GV, P]),
                                       cc[:, 0:n], start=True, stop=True)
                    mm.then_inc(s.bcast, 1)
                for i in range(NG):
                    pe.wait_ge(s.k_staged, q(c, i) + 1)
                    if not is0(c):
                        pe.wait_ge(s.kt_done, q(c - 1, i) + 1)
                    for h in range(2):
                        kk = kc[:, 2 * i + h, 0:n]
                        pe.matmul(bank_b[i][0:n, h, 0:n], kk, kk, start=True, stop=True)
                        mm = pe.matmul(bank_b[i][0:n, 2 + h, 0:n], kk, qkv[:, 2 * i + h, bass.ds(t, n)],
                                       start=True, stop=True)
                    mm.then_inc(s.gram, 1)
                for i in range(NG):
                    pe.wait_ge(s.v_staged, q(c, i) + 1)
                    pe.wait_ge(s.eq_exp, q(c, i) + 1)
                    for h in range(GRP):
                        mm = pe.transpose(bank_a[i][0:n, h, :], vc[:, i, h, 0:n], k.ident[:, :])
                    mm.then_inc(s.v_turned, 1)
                for l in range(levels(c)):
                    hf, b = 1 << l, 2 << l
                    second = lambda ap: ap.rearrange("p (b w) -> p b w", w=b)[:, :, hf:b]
                    for i in range(NG):
                        if l == 0:
                            pe.wait_ge(s.an_done, GRP * q(c, i) + GRP)
                            pe.wait_ge(s.v_done, q(c, i) + 1)
                        else:
                            pe.wait_ge(s.x_done, xr(c, l - 1, i) + 1)
                        for h in range(GRP):
                            y = k.ident[0:n, 0:n] if l == 0 else yt[0:n, i, h, 0:n]
                            mm = pe.matmul(zb[i][0:n, h * (n // 2):(h + 1) * (n // 2)], an[0:n, i, h, 0:n],
                                           second(y), start=True, stop=True)
                        mm.then_inc(s.z_ready, 1)
                    if l > 0:
                        for i in range(NG):
                            pe.wait_ge(s.z_done, yr(c, l, i) + 1)
                            if l == 1:
                                pe.wait_ge(s.attn_done, q(c, i) + 1)
                            for h in range(GRP):
                                mm = pe.matmul(yzb[i][0:n, h * (n // 2):(h + 1) * (n // 2)], xp[0:n, i, h, 0:n],
                                               z[0:n, i, h * (n // 2):(h + 1) * (n // 2)], start=True, stop=True)
                            mm.then_inc(s.yz_ready, 1)
                    if l < levels(c) - 1:
                        for i in range(NG):
                            pe.wait_ge(s.y_done, lv(c, l, i) + 1)
                            for h in range(GRP):
                                mm = pe.transpose(bank_a[i][0:n, h, 0:n], yt[0:n, i, h, 0:n], k.ident[0:n, 0:n])
                            mm.then_inc(s.x_ready, 1)
                for i in range(NG):
                    if is0(c):
                        pe.wait_ge(s.s_zero, 1)
                    for h in range(GRP):
                        mm = pe.matmul(bank_a[i][0:n, h, :], kc[:, 2 * i + h // 2, 0:n], st[:, i, h, :],
                                       start=True, stop=True)
                    mm.then_inc(s.ks_ready, 1)
                for i in range(NG):
                    pe.wait_ge(s.y_done, lv(c, levels(c) - 1, i) + 1)
                    pe.wait_ge(s.r_done, GRP * q(c, i) + GRP)
                    for h in range(GRP):
                        mm = pe.matmul(bank_b[i][0:n, h, :], yt[0:n, i, h, 0:n], vt[0:n, i, h, :],
                                       start=True, stop=True)
                    mm.then_inc(s.new_ready, 1)
                for i in range(NG):
                    pe.wait_ge(s.new_done, q(c, i) + 1)
                    pe.wait_ge(s.qd_done, q(c, i) + 1)
                    for h in range(GRP):
                        pe.matmul(bank_a[i][:, h, 0:n], st[:, i, h, :], eq[:, i, h, 0:n], start=True, stop=False)
                        mm = pe.matmul(bank_a[i][:, h, 0:n], new[0:n, i, h, :], dt[0:n, i, h, 0:n],
                                       start=False, stop=True)
                    mm.then_inc(s.o_ready, 1)
                for i in range(NG):
                    pe.wait_ge(s.dec_done, q(c, i) + 1)
                    for h in range(2):
                        mm = pe.transpose(bank_b[i][0:n, h, :], kc[:, 2 * i + h, 0:n], k.ident[:, :])
                    mm.then_inc(s.kt_ready, 1)
                for i in range(NG):
                    pe.wait_ge(s.kt_done, q(c, i) + 1)
                    pe.wait_ge(s.o_done, q(c, i) + 1)
                    for h in range(GRP):
                        mm = pe.matmul(bank_a[i][:, h, :], kt[0:n, i, h // 2, :], new_dec[0:n, i, h, :],
                                       start=True, stop=True)
                    mm.then_inc(s.su_ready, 1)
            walk(pe, body)

        @block.scalar
        def _(act):
            out = qkv[:, 0:2 * GQ, :].rearrange("p (o q) t -> p o q t", o=2)
            def body(c, n):
                t = first_token(c)
                for i in range(NG):
                    act.wait_ge(s.diffed, q(c, i) + 1)
                    nc.scalar.activation(eq[:, i, :, 0:n], bank_a[i][:, :, 0:n], ACT.Exp)
                    nc.scalar.activation(el[:, GRP * i:GRP * (i + 1)].unsqueeze(2), bank_a[i][:, :, n - 1:n],
                                         ACT.Exp).then_inc(s.eq_exp, 1)
                    act.wait_ge(s.clamped, 2 * q(c, i) + 1)
                    nc.scalar.activation(dl[0:n, i % 2, :, 0:n], dl[0:n, i % 2, :, 0:n], ACT.Exp, scale=-1.0)\
                        .then_inc(s.d_exp, 1)
                    act.wait_ge(s.clamped, 2 * q(c, i) + 2)
                    nc.scalar.activation(dt[0:n, i, :, 0:n], dt[0:n, i, :, 0:n], ACT.Exp).then_inc(s.d_exp, 1)
                for i in range(NG):
                    act.wait_ge(s.v_turned, q(c, i) + 1)
                    for h in range(GRP):
                        hd = GRP * i + h
                        ins = nc.scalar.activation(vt[0:n, i, h, :], bank_a[i][0:n, h, :], ACT.Copy,
                                                   scale=g.beta[0:n, bass.ds(c, 1), hd:hd + 1].rearrange(
                                                       "p o h -> p (o h)"))
                    ins.then_inc(s.v_done, 1)
                for l in range(levels(c)):
                    if l > 0:
                        for i in range(NG):
                            act.wait_ge(s.z_ready, lv(c, l, i) + 1)
                            nc.scalar.copy(z[0:n, i, 0:2 * n], zb[i][0:n, 0:2 * n]).then_inc(s.z_done, 1)
                    if l < levels(c) - 1:
                        for i in range(NG):
                            act.wait_ge(s.x_ready, xr(c, l, i) + 1)
                            nc.scalar.copy(xp[0:n, i, :, 0:n], bank_a[i][0:n, :, 0:n]).then_inc(s.x_done, 1)
                for i in range(NG):
                    act.wait_ge(s.new_ready, q(c, i) + 1)
                    nc.scalar.copy(new[0:n, i, :, :], bank_b[i][0:n, :, :]).then_inc(s.new_done, 1)
                for i in range(NG):
                    act.wait_ge(s.o_ready, q(c, i) + 1)
                    nc.scalar.copy(out[:, :, 2 * i:2 * i + 2, bass.ds(t, n)],
                                   bank_a[i][:, :, 0:n].rearrange("p (q o) n -> p o q n", o=2)).then_inc(s.o_done, 1)
                for i in range(NG):
                    act.wait_ge(s.kt_ready, q(c, i) + 1)
                    nc.scalar.copy(kt[0:n, i, :, :], bank_b[i][0:n, 0:2, :]).then_inc(s.kt_done, 1)
            walk(act, body)

        @block.vector
        def _(dve):
            dve.memset(k.raw[:, 3, :], 0.0).then_inc(s.s_zero, 1)
            def body(c, n):
                t = first_token(c)
                head = lambda i: slice(GRP * i, GRP * (i + 1))
                def decay(i):
                    b = i % 2
                    dve.wait_ge(s.bcast, q(c, i) + 1)
                    cum = g.tok[0:n, bass.ds(c, 1), 0, head(i)].rearrange("p o h -> p (o h)")
                    dve.tensor_tensor(dt[0:n, i, :, 0:n], bank_a[i][0:n, :, 0:n],
                                      cum.unsqueeze(2).to_broadcast([n, GRP, n]), ALU.subtract).then_inc(s.diffed, 1)
                    dve.wait_ge(s.diffed, q(c, i) + 1)
                    mask = lambda m: m[0:n, 0:n].unsqueeze(1).to_broadcast([n, GRP, n])
                    dve.scalar_tensor_tensor(out=dl[0:n, b, :, 0:n], in0=dt[0:n, i, :, 0:n], scalar=0.0,
                                             in1=mask(strict), op0=ALU.max, op1=ALU.add).then_inc(s.clamped, 1)
                    dve.scalar_tensor_tensor(out=dt[0:n, i, :, 0:n], in0=dt[0:n, i, :, 0:n], scalar=0.0,
                                             in1=mask(below), op0=ALU.min, op1=ALU.add).then_inc(s.clamped, 1)
                def scores(i):
                    b = i % 2
                    dve.wait_ge(s.gram, q(c, i) + 1)
                    dve.wait_ge(s.d_exp, 2 * q(c, i) + 1)
                    for h in range(GRP):
                        hd = GRP * i + h
                        dve.scalar_tensor_tensor(out=an[0:n, i, h, 0:n], in0=bank_b[i][0:n, h // 2, 0:n],
                                                 scalar=g.tok[0:n, bass.ds(c, 1), 1, hd:hd + 1].rearrange(
                                                     "p o h -> p (o h)"),
                                                 in1=dl[0:n, b, h, 0:n], op0=ALU.mult, op1=ALU.mult)\
                            .then_inc(s.an_done, 1)
                    dve.wait_ge(s.d_exp, 2 * q(c, i) + 2)
                    dve.tensor_copy(kd[0:n, head(i)].unsqueeze(2), dt[0:n, i, :, n - 1:n]).then_inc(s.small, 1)
                    dve.wait_ge(s.small, q(c, i) + 1)
                    d4 = dt[0:n, i, :, 0:n].rearrange("p (q o) n -> p q o n", o=2)
                    dve.tensor_tensor(d4, d4, bank_b[i][0:n, 2:4, 0:n].unsqueeze(2).to_broadcast([n, 2, 2, n]),
                                      ALU.mult).then_inc(s.attn_done, 1)
                if is0(c):
                    dve.wait_ge(s.masks, 5 + 2 * LEVELS)
                decay(0)
                for i in range(NG):
                    if i < NG - 1:
                        if i >= 1:
                            dve.wait_ge(s.an_done, GRP * q(c, i - 1) + GRP)
                        decay(i + 1)
                    scores(i)
                for l in range(levels(c)):
                    hf, b = 1 << l, 2 << l
                    for i in range(NG):
                        if l == 0:
                            dve.wait_ge(s.z_ready, lv(c, 0, i) + 1)
                            dve.wait_ge(s.y_staged, q(c, i) + 1)
                            src = zb
                        else:
                            dve.wait_ge(s.yz_ready, yr(c, l, i) + 1)
                            src = yzb
                        dve.memset(go[:, NG * l + i:NG * l + i + 1], 0.0)
                        y = yt[0:n, i, :, 0:n].rearrange("p h (b w) -> p h b w", w=b)[:, :, :, hf:b]
                        m = lev[0:n, l, 0:n // 2].rearrange("p (b w) -> p b w", w=hf).bitcast(U32)
                        dve.copy_predicated(
                            y, m.unsqueeze(1).to_broadcast([n, GRP, n // b, hf]),
                            src[i][0:n, 0:2 * n].rearrange("p (h b w) -> p h b w", h=GRP, w=hf)).then_inc(s.y_done, 1)
                for i in range(NG):
                    dve.wait_ge(s.ks_ready, q(c, i) + 1)
                    for h in range(GRP):
                        hd = GRP * i + h
                        dve.scalar_tensor_tensor(out=vt[0:n, i, h, :], in0=bank_a[i][0:n, h, :],
                                                 scalar=g.tok[0:n, bass.ds(c, 1), 2, hd:hd + 1].rearrange(
                                                     "p o h -> p (o h)"),
                                                 in1=vt[0:n, i, h, :], op0=ALU.mult, op1=ALU.add)\
                            .then_inc(s.r_done, 1)
                for i in range(NG):
                    dve.wait_ge(s.new_done, q(c, i) + 1)
                    dve.tensor_tensor(new_dec[0:n, i, :, :], bank_b[i][0:n, :, :],
                                      kd[0:n, head(i)].unsqueeze(2).to_broadcast([n, GRP, CH]), ALU.mult)\
                        .then_inc(s.dec_done, 1)
                for i in range(NG):
                    dve.wait_ge(s.su_ready, q(c, i) + 1)
                    for h in range(GRP):
                        hd = GRP * i + h
                        ins = dve.scalar_tensor_tensor(out=st[:, i, h, :], in0=st[:, i, h, :],
                                                       scalar=el[:, hd:hd + 1], in1=bank_a[i][:, h, :],
                                                       op0=ALU.mult, op1=ALU.add)
                    ins.then_inc(s.s_done, 1)
            walk(dve, body)


class SiluTimes:

    def __init__(self, other):
        self.other = other

    def act(self, k, act, s, g, m, ps):
        k.nc.scalar.activation(two(k.b[:, m % 2, :]), halves(ps), ACT.Silu).then_inc(s.up_free, 1)

    def dve(self, k, dve, s, g, m, ps):
        dve.wait_ge(s.up_free, 4 * g + m + 1)
        dve.tensor_tensor(k.a[:, m % 2, :], k.b[:, m % 2, :], self.other(g, m), ALU.mult).then_inc(s.a_ready, 1)


def gdn(k, ins, then=()):
    nc = k.nc
    w, conv = ins["gdn_in"][0], ins["gdn_conv"][0]
    with ExitStack() as c:
        sb = lambda nm, shape: c.enter_context(nc.sbuf_tensor(f"gdn_{nm}", shape, F32))
        split_rings(k, "gdn", c)
        norm = RmsNorm("gdn_in_norm", k.h, ins["attn_norm"][0])
        g = Named(cum=sb("cum", [GV, T]), tok=sb("tok", [P, 1 + NCH, 3, GV]), beta=sb("beta", [P, 1 + NCH, GV]))
        qk = sb("qk", [P, 2 * GQ, T])
        qk_unit = lambda u: tall(w, u * 256)
        v_unit = lambda u: tall(w, u * 256 + 2 * GQ * P)
        z_unit = lambda g, j: tall(w, g * 512 + 256 * j + 2 * GQ * P + GV * P)
        with ExitStack() as c3:
            weight_ring(k, "gdnqk", c3)
            project(k, "gdn_qk", 8, qk_unit, ConvSilu(qk, conv, 0), norm, [v_unit(u) for u in range(4)],
                    GdnGates(g, w, ins["gdn_a_log"][0], ins["gdn_dt_bias"][0]))
        with ExitStack() as c2:
            v = c2.enter_context(nc.sbuf_tensor("gdn_v", [P, GV, T], F32))
            with ExitStack() as c3:
                weight_ring(k, "gdnv", c3)
                project(k, "gdn_v", 8, v_unit, ConvSilu(v, conv, 2 * GQ * P))
            tile = lambda base: lambda j: qk[:, bass.ds(j + base, 1), :].rearrange("p o t -> p (o t)")
            head_norm(k, "gdn_qn", GQ, tile(0), k.ones[:, :], 1.0, lambda g, j: float(P) ** -0.5)
            head_norm(k, "gdn_kn", GQ, tile(GQ), k.ones[:, :], 1.0, lambda g, j: 1.0)
            gdn_recurrence(k, g, qk, v)
        head_norm(k, "gdn_on", GV, tile(0), k.ones[:, :], 1.0 / P, lambda g, j: g[:, 0:1],
                  ins["gdn_norm"].rearrange("o p -> p o"), first_units(z_unit))
        with ExitStack() as c3:
            weight_ring(k, "gdno", c3)
            o = lambda g, m: qk[:, bass.ds(2 * g + (m % 2) * GQ + m // 2, 1), :].rearrange("p o t -> p (o t)")
            up_down(k, "gdn_out", GV // 4, z_unit, ins["gdn_out"][0], SiluTimes(o), k.h, False, None, then)



class Store:

    def __init__(self, dst, scale=lambda j: 1.0):
        self.dst, self.scale = dst, scale

    def open(self, k, name, ctx):
        self.left = k.sem(f"{name}_left")

    def free(self, pe, j):
        pe.wait_ge(self.left, j + 1)

    def sync(self, k, sp):
        pass

    def dve_start(self, k, dve):
        pass

    def act(self, k, act, j, r, t0):
        act.wait_ge(k.tile_full, t0 + j + 1)
        k.nc.scalar.activation(two(self.dst(j)), halves(k.ps[r]), ACT.Copy, scale=self.scale(j)).then_inc(self.left, 1)

    def act_end(self, k, act, n, t0):
        pass

    def dve(self, k, dve, j, r, t0):
        pass

    def dve_end(self, k, dve, n, t0):
        pass


MH = 8
MK = 64
CAP = 15.0


class MlstmGates:

    slot1 = True

    def __init__(self, g, w_in, bias):
        self.g, self.w_in, self.bias = g, w_in, bias

    def open(self, k, ctx):
        sb = lambda nm, shape: ctx.enter_context(k.nc.sbuf_tensor(f"mlg_{nm}", shape, F32))
        c0 = 2 * MH * MK + 2 * D
        self.s = gate_rows(k, "mlg", ctx, [(self.w_in[:, c0:c0 + MH], 0), (self.w_in[:, c0 + MH:c0 + 2 * MH], 32)],
                           32 + MH)
        self.bi = sb("bias", [MH, 2])
        self.i, self.f, self.e, self.mask, self.cum = (sb(x, [MH, T]) for x in ("i", "f", "e", "mask", "cum"))
        self.bias_in, self.a, self.v, self.made, self.turned = (
            k.sem(f"mlg_{x}") for x in ("bias_in", "act", "dve", "mask", "turned"))
        self.spare = k.ps[1][:, 0, 0:16 * (1 + NCH)]

    def sync(self, k, sp):
        with k.nc.allow_non_contiguous_dma(reason="a few gate weights and parameters"):
            sp.dma_start(self.bi[:, :], self.bias.rearrange("(o h) -> h o", o=2)).then_inc(self.bias_in, 16)
            gate_load(k, sp, self.s)

    def free(self, k, pe):
        pe.wait_ge(self.a, 2)

    def free1(self, k, pe):
        pe.wait_ge(self.v, 10)

    def pe(self, k, pe, n):
        if n == 1:
            gate_product(k, pe, self.s, k.ps[3])
        if n == 4:
            pe.wait_ge(self.v, 8)
            for c, (t, m) in enumerate(chunks()):
                mm = pe.transpose(self.spare[0:m, 16 * c:16 * c + MH], self.e[0:MH, t:t + m], k.ident[0:MH, 0:MH])
            mm.then_inc(self.turned, 1)

    def act(self, k, act, n):
        a, e, f, scalar = self.a, self.e, self.f, k.nc.scalar
        if n == 0:
            gate_hi(k, act, self.s)
        if n == 1:
            act.wait_ge(self.s.ready, 1)
            act.wait_ge(self.v, 1)
            scalar.activation(two(self.i[:, :]), k.ps[3][0:MH, :, 0:HT], ACT.Tanh, bias=self.bi[:, 0:1],
                              scale=1.0 / CAP).then_inc(a, 1)
            scalar.activation(two(f[:, :]), k.ps[3][32:32 + MH, :, 0:HT], ACT.Tanh, bias=self.bi[:, 1:2],
                              scale=1.0 / CAP).then_inc(a, 1)
            act.wait_ge(self.v, 3)
            scalar.activation(e[:, :], f[:, :], ACT.Abs).then_inc(a, 1)
            act.wait_ge(a, 3)
            scalar.activation(e[:, :], e[:, :], ACT.Exp, scale=-1.0).then_inc(a, 1)
            act.wait_ge(a, 4)
            scalar.activation(e[:, :], e[:, :], ACT.Ln, bias=k.ones[0:MH, 0:1]).then_inc(a, 1)

    def dve(self, k, dve, n):
        g, i, f, e, v, bi, cum = self.g, self.i, self.f, self.e, self.v, self.bi, self.cum
        if n == -1:
            gate_clear(k, dve, self.s)
        if n == 0:
            chunk_scan_mask(dve, self.mask[:, :], self.made)
            gate_lo(k, dve, self.s)
            dve.wait_ge(self.bias_in, 16)
            dve.tensor_scalar(bi[:, :], bi[:, :], 1.0 / CAP, None, ALU.mult).then_inc(v, 1)
        if n == 1:
            dve.wait_ge(self.a, 2)
            dve.tensor_scalar(i[:, :], i[:, :], CAP, None, ALU.mult).then_inc(v, 1)
            dve.tensor_scalar(f[:, :], f[:, :], CAP, None, ALU.mult).then_inc(v, 1)
            dve.wait_ge(self.a, 5)
            dve.wait_ge(v, 3)
            dve.scalar_tensor_tensor(out=f[:, :], in0=f[:, :], scalar=0.0, in1=e[:, :], op0=ALU.min,
                                     op1=ALU.subtract).then_inc(v, 1)
            dve.wait_ge(v, 4)
            dve.wait_ge(self.made, 1 + len(chunks()))
            dve.tensor_tensor_scan(cum[:, :], self.mask[:, :], f[:, :], 0.0, ALU.mult, ALU.add).then_inc(v, 1)
            dve.tensor_tensor_scan(g.m[:, :], f[:, :], i[:, :], 0.0, ALU.add, ALU.max).then_inc(v, 1)
            dve.wait_ge(v, 6)
            dve.tensor_tensor(g.am[:, :], cum[:, :], g.m[:, :], ALU.subtract).then_inc(v, 1)
            dve.tensor_tensor(e[:, :], i[:, :], cum[:, :], ALU.subtract).then_inc(v, 1)
        if n == 4:
            dve.wait_ge(self.turned, 1)
            cols = self.spare.rearrange("p (c x) -> p c x", x=16)[:, :, 0:MH]
            for c0, c1, m in ((0, 1, META), (1, 1 + NCH, CH)):
                dve.tensor_copy(g.b[0:m, c0:c1, :], cols[0:m, c0:c1]).then_inc(v, 1)


def mlstm_recurrence(k, g, qk, vf):
    nc = k.nc
    NG2 = MH // GRP
    with ExitStack() as ctx:
        sb = lambda nm, shape: ctx.enter_context(nc.sbuf_tensor(f"ml_{nm}", shape, F32))
        st = sb("st", [P, MH // 2, P + 1])
        kc, vc = sb("kc", [P, MH // 2, CH]), sb("vc", [P, MH, CH])
        qz = sb("qz", [P, MH, CH])
        amc, mc, mp = sb("amc", [MH, CH]), sb("mc", [MH, CH]), sb("mp", [MH, 1])
        w = sb("w", [P, NG2, GRP, CH])
        inn = sb("in", [P, NG2, 2, CH])
        qd = sb("qd", [P, NG2, GRP, CH])
        floor, dm = sb("floor", [P, NG2, GRP, CH]), sb("dm", [P, NG2, GRP, CH])
        vt = sb("vt", [P, NG2, GRP, CH])
        num = sb("num", [P, NG2, GRP, CH])
        kd = sb("kd", [P, NG2, 2, 2, MK])
        we = sb("we", [P, MH])
        mpc = sb("mpc", [P, MH // 2])
        below = sb("below", [P, CH])
        names = ("masks", "staged", "bcast", "gram", "diffed", "clamped", "w_exp", "floor_done", "mp_done", "in_done",
                 "we_done", "w_done", "qd_done", "v_turned", "v_done", "k_turned", "k_done", "num_ready", "den_ready",
                 "dm_done", "rden", "h_done", "left", "su_ready", "s_done", "s_zero")
        s = Named(**{x: k.sem(f"ml_{x}") for x in names})
        heads = lambda ap: ap.rearrange("p (h n) -> p h n", h=GRP)
        bank_a = [heads(k.ps[2 * i][:, 0, :]) for i in range(NG2)]
        bank_b = [heads(k.ps[2 * i][:, 1, :]) for i in range(NG2)]
        bank_c = [k.ps[2 * i + 1][:, 0, :] for i in range(NG2)]
        bank_e = [k.ps[2 * i + 1][:, 1, :] for i in range(NG2)]
        is0 = lambda c: isinstance(c, int) and c == 0
        first_token = lambda c: 0 if is0(c) else c * CH + (META - CH)
        q = lambda c, i: NG2 * c + i

        def walk(eng, body):
            body(0, META)
            with eng.Fori(0, NCH) as i:
                body(i + 1, CH)

        block = ctx.enter_context(stage(k))

        @block.gpsimd
        def _(pool):
            pool.memset(below[:, :], 0.0).then_inc(s.masks, 1)
            pool.memset(qz[:, :, :], 0.0).then_inc(s.masks, 1)
            pool.wait_ge(s.masks, 2)
            nc.gpsimd.affine_select(out=below[:, :], in_=below[:, :], compare_op=ALU.is_ge, fill=-1e30, base=0,
                                    pattern=[[1, CH]], channel_multiplier=-1).then_inc(s.masks, 1)
            def body(c, n):
                t = first_token(c)
                if not is0(c):
                    pool.wait_ge(s.k_turned, q(c, 0))
                    pool.wait_ge(s.qd_done, q(c, 0))
                    pool.tensor_copy(mp[:, :], g.m[:, bass.ds(t - 1, 1)]).then_inc(s.staged, 1)
                else:
                    pool.memset(mp[:, :], 0.0).then_inc(s.staged, 1)
                now = bass.ds(t, n)
                pool.tensor_copy(amc[:, 0:n], g.am[:, now]).then_inc(s.staged, 1)
                pool.tensor_copy(mc[:, 0:n], g.m[:, now]).then_inc(s.staged, 1)
                pool.tensor_copy(kc[:, :, 0:n], qk[:, MH // 2:MH, now]).then_inc(s.staged, 1)
                for o in range(2):
                    pool.wait_ge(s.staged, 7 * c + 4 + o)
                    pool.tensor_copy(qz[MK * o:MK * (o + 1), o:MH:2, 0:n],
                                     qk[MK * o:MK * (o + 1), 0:MH // 2, now]).then_inc(s.staged, 1)
                pool.wait_ge(s.staged, 7 * c + 6)
                pool.tensor_copy(vc[:, :, 0:n], vf[:, :, now]).then_inc(s.staged, 1)
            walk(pool, body)

        @block.tensor
        def _(pe):
            one_hot = lambda h: k.ident[0:MH, h:h + 1].to_broadcast([MH, P])
            def body(c, n):
                for i in range(NG2):
                    pe.wait_ge(s.staged, 7 * c + 3)
                    if not is0(c):
                        pe.wait_ge(s.left, 2 * q(c - 1, i) + 2)
                        pe.wait_ge(s.s_done, q(c - 1, i) + 1)
                    for h in range(GRP):
                        pe.matmul(bank_a[i][:, h, 0:n], one_hot(GRP * i + h), amc[:, 0:n], start=True, stop=True)
                    for h in range(GRP):
                        pe.matmul(bank_b[i][:, h, 0:n], one_hot(GRP * i + h), mc[:, 0:n], start=True, stop=True)
                    for p in range(2):
                        hd = GRP * i + 2 * p
                        for o in range(2):
                            sel = k.ident[0:MH, hd + o:hd + o + 1].to_broadcast([MH, MK])
                            pe.matmul(bank_c[i][MK * o:MK * (o + 1), CH * p:CH * p + n], sel, amc[:, 0:n],
                                      start=True, stop=True)
                            mm = pe.matmul(bank_c[i][MK * o:MK * (o + 1), 2 * CH + p:2 * CH + p + 1], sel, mp[:, :],
                                           start=True, stop=True)
                    mm.then_inc(s.bcast, 1)
                for i in range(NG2):
                    pe.wait_ge(s.staged, 7 * c + 6)
                    for h in range(GRP):
                        hd = GRP * i + h
                        mm = pe.matmul(bank_e[i][0:n, CH * h:CH * h + n], kc[:, hd // 2, 0:n],
                                       qz[:, hd, 0:n], start=True, stop=True)
                    mm.then_inc(s.gram, 1)
                for i in range(NG2):
                    pe.wait_ge(s.staged, 7 * c + 7)
                    pe.wait_ge(s.in_done, 2 * q(c, i) + 2)
                    for h in range(GRP):
                        mm = pe.transpose(bank_c[i][0:n, CH * h:CH * (h + 1)], vc[:, GRP * i + h, 0:n], k.ident[:, :])
                    mm.then_inc(s.v_turned, 1)
                for i in range(NG2):
                    pe.wait_ge(s.w_done, q(c, i) + 1)
                    for p in range(2):
                        mm = pe.transpose(bank_e[i][0:n, CH * p:CH * (p + 1)], kc[:, 2 * i + p, 0:n], k.ident[:, :])
                    mm.then_inc(s.k_turned, 1)
                for i in range(NG2):
                    pe.wait_ge(s.qd_done, q(c, i) + 1)
                    pe.wait_ge(s.v_done, q(c, i) + 1)
                    pe.wait_ge(s.floor_done, q(c, i) + 1)
                    if is0(c):
                        pe.wait_ge(s.s_zero, 1)
                    for h in range(GRP):
                        hd = GRP * i + h
                        pe.matmul(bank_a[i][:, h, 0:n], st[:, hd // 2, 0:P], qd[:, i, h, 0:n],
                                  start=True, stop=False)
                        mm = pe.matmul(bank_a[i][:, h, 0:n], vt[0:n, i, h, :], w[0:n, i, h, 0:n],
                                       start=False, stop=True)
                    mm.then_inc(s.num_ready, 1)
                    for h in range(GRP):
                        hd = GRP * i + h
                        pe.matmul(bank_b[i][:, h, 0:n], st[:, hd // 2, P:P + 1].to_broadcast([P, P]),
                                  qd[:, i, h, 0:n], start=True, stop=False)
                        mm = pe.matmul(bank_b[i][:, h, 0:n], k.ones[0:n, :], w[0:n, i, h, 0:n],
                                       start=False, stop=True)
                    mm.then_inc(s.den_ready, 1)
                for i in range(NG2):
                    pe.wait_ge(s.k_done, q(c, i) + 1)
                    for p in range(2):
                        kk = kd[0:n, i, p, :, :].rearrange("p h d -> p (h d)")
                        pe.matmul(bank_c[i][:, 2 * CH * p:2 * CH * (p + 1)], kk,
                                  vt[0:n, i, 2 * p:2 * p + 2, :].rearrange("p h d -> p (h d)"), start=True, stop=True)
                        mm = pe.matmul(bank_e[i][:, p:p + 1], kk, k.ones[0:n, 0:1], start=True, stop=True)
                    mm.then_inc(s.su_ready, 1)
            walk(pe, body)

        @block.scalar
        def _(act):
            nc.scalar.preload_act_table_set("exp_and_others")
            def body(c, n):
                for i in range(NG2):
                    act.wait_ge(s.bcast, q(c, i) + 1)
                    if not is0(c):
                        act.wait_ge(s.dm_done, q(c - 1, i) + 1)
                    nc.scalar.copy(mpc[:, 2 * i:2 * i + 2], bank_c[i][:, 2 * CH:2 * CH + 2]).then_inc(s.mp_done, 1)
                    nc.scalar.activation(floor[:, i, :, 0:n], bank_b[i][:, :, 0:n], ACT.Exp, scale=-1.0)\
                        .then_inc(s.floor_done, 1)
                    act.wait_ge(s.mp_done, q(c, i) + 1)
                    for p in range(2):
                        nc.scalar.activation(inn[:, i, p, 0:n], bank_c[i][:, CH * p:CH * p + n], ACT.Exp,
                                             bias=mpc[:, 2 * i + p:2 * i + p + 1]).then_inc(s.in_done, 1)
                for i in range(NG2):
                    act.wait_ge(s.clamped, q(c, i) + 1)
                    nc.scalar.activation(w[0:n, i, :, 0:n], w[0:n, i, :, 0:n], ACT.Exp).then_inc(s.w_exp, 1)
                for i in range(NG2):
                    act.wait_ge(s.v_turned, q(c, i) + 1)
                    nc.scalar.copy(vt[0:n, i, :, :], heads(bank_c[i])[0:n]).then_inc(s.v_done, 1)
                for i in range(NG2):
                    act.wait_ge(s.num_ready, q(c, i) + 1)
                    if not is0(c):
                        act.wait_ge(s.h_done, q(c - 1, i) + 1)
                    nc.scalar.copy(num[:, i, :, 0:n], bank_a[i][:, :, 0:n]).then_inc(s.left, 1)
                    act.wait_ge(s.den_ready, q(c, i) + 1)
                    nc.scalar.activation(dm[:, i, :, 0:n], bank_b[i][:, :, 0:n], ACT.Abs).then_inc(s.left, 1)
            walk(act, body)

        @block.vector
        def _(dve):
            dve.memset(st[:, :, :], 0.0).then_inc(s.s_zero, 1)
            def outputs(c, n):
                for i in range(NG2):
                    dve.wait_ge(s.dm_done, q(c, i) + 1)
                    dve.reciprocal(dm[:, i, :, 0:n], dm[:, i, :, 0:n]).then_inc(s.rden, 1)
                    dve.wait_ge(s.rden, q(c, i) + 1)
                    dve.tensor_tensor(vf[:, GRP * i:GRP * (i + 1), bass.ds(first_token(c), n)], num[:, i, :, 0:n],
                                      dm[:, i, :, 0:n], ALU.mult).then_inc(s.h_done, 1)
            def body(c, n):
                t = first_token(c)
                head = lambda i: slice(GRP * i, GRP * (i + 1))
                if is0(c):
                    dve.wait_ge(s.masks, 3)
                for i in range(NG2):
                    dve.wait_ge(s.bcast, q(c, i) + 1)
                    b = g.b[0:n, bass.ds(c, 1), head(i)].rearrange("p o h -> p (o h)")
                    dve.tensor_tensor(w[0:n, i, :, 0:n], bank_a[i][0:n, :, 0:n],
                                      b.unsqueeze(2).to_broadcast([n, GRP, n]), ALU.add).then_inc(s.diffed, 1)
                    dve.wait_ge(s.diffed, q(c, i) + 1)
                    dve.scalar_tensor_tensor(out=w[0:n, i, :, 0:n], in0=w[0:n, i, :, 0:n], scalar=0.0,
                                             in1=below[0:n, 0:n].unsqueeze(1).to_broadcast([n, GRP, n]),
                                             op0=ALU.min, op1=ALU.add).then_inc(s.clamped, 1)
                for i in range(NG2):
                    dve.wait_ge(s.in_done, 2 * q(c, i) + 2)
                    dve.wait_ge(s.staged, 7 * c + 6)
                    dve.tensor_tensor(qd[:, i, :, 0:n].rearrange("p (a b) n -> p a b n", b=2),
                                      qz[:, head(i), 0:n].rearrange("p (a b) n -> p a b n", b=2),
                                      inn[:, i, :, 0:n].unsqueeze(2).to_broadcast([P, 2, 2, n]), ALU.mult)\
                        .then_inc(s.qd_done, 1)
                    dve.wait_ge(s.w_exp, q(c, i) + 1)
                    dve.tensor_copy(we[0:n, head(i)].unsqueeze(2), w[0:n, i, :, n - 1:n]).then_inc(s.we_done, 1)
                    dve.wait_ge(s.we_done, q(c, i) + 1)
                    dve.wait_ge(s.gram, q(c, i) + 1)
                    dve.tensor_tensor(w[0:n, i, :, 0:n], w[0:n, i, :, 0:n], heads(bank_e[i])[0:n, :, 0:n],
                                      ALU.mult).then_inc(s.w_done, 1)
                for i in range(NG2):
                    dve.wait_ge(s.k_turned, q(c, i) + 1)
                    dve.tensor_tensor(kd[0:n, i].rearrange("p a h d -> p (a h) d"),
                                      bank_e[i][0:n, 0:2 * CH].rearrange("p (h d) -> p h d", d=MK),
                                      we[0:n, head(i)].unsqueeze(2).to_broadcast([n, GRP, MK]), ALU.mult)\
                        .then_inc(s.k_done, 1)
                if not is0(c) and not (isinstance(c, int) and c == 1):
                    outputs(c - 1, n)
                for i in range(NG2):
                    dve.wait_ge(s.su_ready, q(c, i) + 1)
                    for p in range(2):
                        pr = 2 * i + p
                        keep = inn[:, i, p, n - 1:n]
                        for o in range(2):
                            r = slice(MK * o, MK * (o + 1))
                            c0 = 2 * CH * p + CH * o
                            dve.scalar_tensor_tensor(out=st[r, pr, 0:P], in0=st[r, pr, 0:P], scalar=keep[r],
                                                     in1=bank_c[i][r, c0:c0 + P], op0=ALU.mult, op1=ALU.add)
                        ins = dve.scalar_tensor_tensor(out=st[:, pr, P:P + 1], in0=st[:, pr, P:P + 1], scalar=keep,
                                                       in1=bank_e[i][:, p:p + 1], op0=ALU.mult, op1=ALU.add)
                    ins.then_inc(s.s_done, 1)
                for i in range(NG2):
                    dve.wait_ge(s.left, 2 * q(c, i) + 2)
                    dve.tensor_tensor(dm[:, i, :, 0:n], dm[:, i, :, 0:n], floor[:, i, :, 0:n], ALU.max)\
                        .then_inc(s.dm_done, 1)
                if is0(c):
                    outputs(c, n)
            body(0, META)
            body(1, CH)
            with dve.Fori(0, NCH - 1) as i:
                body(i + 2, CH)
            outputs(NCH, CH)


class SigmoidTimes(SiluTimes):

    def act(self, k, act, s, g, m, ps):
        k.nc.scalar.activation(two(k.b[:, m % 2, :]), halves(ps), ACT.Sigmoid).then_inc(s.up_free, 1)


def mlstm_unit(ins):
    return lambda u: tall(ins["mlstm_in"][0], u * 256)


def mlstm(k, ins, then=()):
    nc = k.nc
    w = ins["mlstm_in"][0]
    with ExitStack() as c:
        sb = lambda nm, shape: c.enter_context(nc.sbuf_tensor(f"mls_{nm}", shape, F32))
        split_rings(k, "mls", c)
        g = Named(am=sb("am", [MH, T]), m=sb("m", [MH, T]), b=sb("b", [P, 1 + NCH, MH]))
        vf = sb("v", [P, MH, T])
        gate_unit = lambda g, j: tall(w, g * 512 + 256 * j + 2 * MH * MK + D)
        with ExitStack() as c2:
            qk = c2.enter_context(nc.sbuf_tensor("mls_qk", [P, MH, T], F32))
            with ExitStack() as c3:
                weight_ring(k, "mlsp", c3)
                project(k, "mls_p", 8, mlstm_unit(ins),
                        Store(lambda j: qk[:, j, :] if j < MH else vf[:, j - MH, :],
                              lambda j: MK ** -0.5 if MH // 2 <= j < MH else 1.0),
                        RmsNorm("mls_in_norm", k.h, ins["attn_norm"][1]), first_units(gate_unit),
                        MlstmGates(g, w, ins["mlstm_gate_bias"][0]))
            mlstm_recurrence(k, g, qk, vf)
        tile = lambda j: vf[:, bass.ds(j, 1), :].rearrange("p o t -> p (o t)")
        head_norm(k, "mls_on", MH, tile, k.ones[:, :], 1.0 / P,
                  lambda g, j: g[:, bass.ds(j, 1)], ins["mlstm_norm"][0].rearrange("(h p) -> p h", p=P))
        with ExitStack() as c3:
            weight_ring(k, "mlso", c3)
            up_down(k, "mls_out", MH // 4, gate_unit, ins["mlstm_out"][0],
                    SigmoidTimes(lambda g, m: tile(g * 4 + m)), k.h, False, None, then)



S0 = META
LN2_60 = 41.58883083359672
HW = 64
FH = 8


def linked(eng, sem):
    count = [0]

    def link(ins):
        count[0] += 1
        ins.then_inc(sem, 1)
        eng.wait_ge(sem, count[0])
    return link


class HgrnGates:

    slot1 = False

    def __init__(self, qa, fa, b, lower, leave):
        self.qa, self.fa, self.b, self.lower, self.leave = qa, fa, b, lower, leave

    def open(self, k, ctx):
        sb = lambda nm, shape: ctx.enter_context(k.nc.sbuf_tensor(f"hg_{nm}", shape, F32))
        self.e1, self.e2, self.small = sb("e1", [P, 2, T]), sb("e2", [P, 2, T]), sb("small", [P, 2, T])
        self.mask, self.lx, self.lb = sb("mask", [P, T]), sb("lx", [P, 2]), sb("lb", [P, 3, 2])
        self.lx_in, self.ev, self.silu, self.e0, self.one, self.ln = (
            k.sem(f"hg_{x}") for x in ("lx_in", "exps", "silu", "lb_exp", "lb_diff", "ln"))
        self.ready, self.chain, self.q1 = k.sem("hg_ready"), k.sem("hg_chain"), k.sem("hg_ln_in")
        self.linked = 0

    def sync(self, k, sp):
        with k.nc.allow_non_contiguous_dma(reason="256 bounds, feature on partitions"):
            sp.dma_start(self.lx[:, :], self.lower[0].rearrange("(t p) -> p t", p=P)).then_inc(self.lx_in, 16)

    def free(self, k, pe):
        pass

    free1 = free

    def pe(self, k, pe, n):
        pass

    def act(self, k, act, n):
        e1, e2, lb, scalar = self.e1, self.e2, self.lb, k.nc.scalar
        if n == 2:
            act.wait_ge(self.one, 1)
            scalar.activation(lb[:, 0, :], lb[:, 0, :], ACT.Exp).then_inc(self.e0, 1)
        if n == 3:
            act.wait_ge(self.leave.left, 4)
            scalar.activation(e1[:, :, :], self.fa, ACT.Exp, scale=-1.0).then_inc(self.ev, 1)
            scalar.activation(e2[:, :, :], self.fa, ACT.Exp).then_inc(self.ev, 1)
        if n == 5:
            act.wait_ge(self.q1, 1)
            scalar.activation(self.b[:, :, :], e1[:, :, :], ACT.Ln).then_inc(self.ln, 1)
        if n == 6:
            scalar.activation(self.qa, self.qa, ACT.Silu).then_inc(self.silu, 1)

    def dve(self, k, dve, n):
        e1, e2, small, lb, b, fa, mask = self.e1, self.e2, self.small, self.lb, self.b, self.fa, self.mask
        def link(ins):
            self.linked += 1
            ins.then_inc(self.chain, 1)
            dve.wait_ge(self.chain, self.linked)
        if n == 1:
            dve.wait_ge(self.lx_in, 16)
            dve.tensor_tensor(lb[:, 0, :], self.lx[:, :], self.lx[:, :], ALU.subtract).then_inc(self.one, 1)
        if n == 3:
            dve.wait_ge(self.e0, 1)
            link(dve.reciprocal(lb[:, 1, :], lb[:, 0, :]))
            link(dve.tensor_tensor(lb[:, 1, :], lb[:, 1, :], lb[:, 0, :], ALU.mult))
            link(dve.tensor_tensor(lb[:, 0, :], lb[:, 1, :], lb[:, 1, :], ALU.subtract))
            link(dve.tensor_scalar(lb[:, 2, :], lb[:, 0, :], -1.0, 1.0, ALU.mult, ALU.add))
            dve.wait_ge(self.ev, 2)
            link(dve.tensor_scalar(e1[:, :, :], e1[:, :, :], 1.0, None, ALU.add))
            link(dve.reciprocal(e1[:, :, :], e1[:, :, :]))
        if n == 4:
            for j in range(2):
                link(dve.tensor_scalar(e1[:, j, :], e1[:, j, :], lb[:, 2, j:j + 1], lb[:, 0, j:j + 1],
                                       ALU.mult, ALU.add))
            link(dve.tensor_scalar(e1[:, :, :], e1[:, :, :], 1e-30, None, ALU.max))
            link(dve.tensor_scalar(small[:, :, :], e1[:, :, :], 2.0 ** -40, None, ALU.is_lt))
            link(dve.tensor_scalar(b[:, :, :], small[:, :, :], 2.0 ** 60, 1.0, ALU.mult, ALU.add))
            dve.tensor_tensor(e1[:, :, :], e1[:, :, :], b[:, :, :], ALU.mult).then_inc(self.q1, 1)
        if n == 5:
            link(dve.tensor_scalar(e2[:, :, :], e2[:, :, :], 1.0, None, ALU.add))
            link(dve.reciprocal(e2[:, :, :], e2[:, :, :]))
            for j in range(2):
                dve.tensor_scalar(fa[:, j, :], e2[:, j, :], lb[:, 2, j:j + 1], None, ALU.mult).then_inc(self.ready, 1)
        if n == 6:
            link(dve.memset(mask[:, :], 1.0))
            for t, _ in chunks():
                link(dve.memset(mask[:, t:t + 1], 0.0))
            dve.wait_ge(self.ln, 1)
            link(dve.scalar_tensor_tensor(out=small[:, :, :], in0=small[:, :, :], scalar=-LN2_60, in1=b[:, :, :],
                                          op0=ALU.mult, op1=ALU.add))
            for j in range(2):
                link(dve.tensor_tensor_scan(b[:, j, :], mask[:, :], small[:, j, :], 0.0, ALU.mult, ALU.add))


class Both:

    slot1 = False

    def __init__(self, first, other):
        self.parts = (first, other)
        self.free, self.free1, self.pe = first.free, first.free1, first.pe

    def open(self, k, ctx):
        for part in self.parts:
            part.open(k, ctx)

    def sync(self, k, sp):
        for part in self.parts:
            part.sync(k, sp)

    def act(self, k, act, n):
        for part in self.parts:
            part.act(k, act, n)

    def dve(self, k, dve, n):
        for part in self.parts:
            part.dve(k, dve, n)


def hgrn(k, qa, ka, va, b):
    nc = k.nc
    with ExitStack() as ctx:
        sb = lambda nm, shape: ctx.enter_context(nc.sbuf_tensor(f"hr_{nm}", shape, F32))
        e = sb("e", [P, 2, 2, SEQ])
        st = sb("st", [P, 2, 2, NCH, CH])
        lev = sb("lev", [P, LEVELS, CH // 2])
        qd, kd = sb("qd", [P, 2, SEQ]), sb("kd", [P, 2, SEQ])
        vt, kt = sb("vt", [P, 2, NCH, P]), sb("kt", [P, 2, NCH, P])
        s2, keep = sb("s2", [P, 2, P]), sb("keep", [P, 2, NCH])
        names = ("masks", "diff", "exps", "scaled", "scores", "taken", "zero", "ends", "end_exp", "end_scaled",
                 "v_turned", "v_done", "k_turned", "k_done", "o_ready", "o_done", "su", "s_done", "keep_done")
        s = Named(**{x: k.sem(f"hr_{x}") for x in names})
        tok = slice(S0, T)
        bank = lambda j, o, l: k.ps[2 * (l % 2) + j][:, o, :]
        block = ctx.enter_context(stage(k))

        @block.gpsimd
        def _(pool):
            pool.memset(lev[:, :, :], 1.0).then_inc(s.masks, 1)
            n = 1
            pool.wait_ge(s.masks, n)
            for l in range(LEVELS):
                hf, bl = 1 << l, 2 << l
                for sign, base in ((1, 0), (-1, hf - 1)):
                    v = lev[:, l, :].rearrange("p (b w) -> p b w", w=hf)
                    nc.gpsimd.affine_select(out=v, in_=v, compare_op=ALU.is_ge, fill=0.0, base=base,
                                            pattern=[[-bl * sign, CH // bl], [0, hf]], channel_multiplier=sign)\
                        .then_inc(s.masks, 1)
                    n += 1
                    pool.wait_ge(s.masks, n)
            pool.memset(st[:, :, :, :, :], 0.0).then_inc(s.zero, 1)
            pool.memset(s2[:, :, :], 0.0).then_inc(s.zero, 1)

        @block.vector
        def _(dve):
            def split(ap, l):
                v = ap.rearrange("p j (c w) -> p j c w", w=2 << l)
                return v[:, :, :, 0:1 << l], v[:, :, :, 1 << l:2 << l]
            def exponents(l):
                hf = 1 << l
                if l >= 2:
                    dve.wait_ge(s.scores, l - 1)
                first, second = split(b[:, :, tok], l)
                efirst, esecond = split(e[:, l % 2, :, :], l)
                mid = first[:, :, :, hf - 1:hf].to_broadcast(list(first.shape))
                dve.tensor_tensor(esecond, second, mid, ALU.subtract).then_inc(s.diff, 1)
                dve.tensor_tensor(efirst, mid, first, ALU.subtract).then_inc(s.diff, 1)
            def scale(l):
                efirst, esecond = split(e[:, l % 2, :, :], l)
                dve.wait_ge(s.exps, l + 1)
                dve.tensor_tensor(esecond, esecond, split(qa[:, :, tok], l)[1], ALU.mult).then_inc(s.scaled, 1)
                dve.tensor_tensor(efirst, efirst, split(ka[:, :, tok], l)[0], ALU.mult).then_inc(s.scaled, 1)
            def take(l):
                hf, bl = 1 << l, 2 << l
                dve.wait_ge(s.scores, l + 1)
                if l >= 1:
                    dve.wait_ge(s.taken, 4 * l)
                m = lev[:, l, :].rearrange("p (b w) -> p b w", w=hf).bitcast(U32).unsqueeze(1)
                for j in range(2):
                    for o in range(2):
                        out = st[:, j, o, :, :].rearrange("p c (b w) -> p c b w", w=bl)[:, :, :, hf:bl]
                        src = bank(j, o, l)[:, 0:SEQ // 2].rearrange("p (c b w) -> p c b w", c=NCH, w=hf)
                        dve.copy_predicated(out, m.to_broadcast([P, NCH, CH // bl, hf]), src).then_inc(s.taken, 1)
            last = b[:, :, tok].rearrange("p j (c w) -> p j c w", w=CH)[:, :, :, CH - 1:CH]
            b4 = b[:, :, tok].rearrange("p j (c w) -> p j c w", w=CH)
            dve.tensor_tensor(kd[:, :, :].rearrange("p j (c w) -> p j c w", w=CH),
                              last.to_broadcast([P, 2, NCH, CH]), b4, ALU.subtract).then_inc(s.ends, 1)
            exponents(0)
            dve.wait_ge(s.end_exp, 2)
            dve.tensor_tensor(kd[:, :, :], kd[:, :, :], ka[:, :, tok], ALU.mult).then_inc(s.end_scaled, 1)
            dve.tensor_copy(keep[:, :, :].unsqueeze(3),
                            qd[:, :, :].rearrange("p j (c w) -> p j c w", w=CH)[:, :, :, CH - 1:CH])\
                .then_inc(s.keep_done, 1)
            dve.wait_ge(s.keep_done, 1)
            dve.tensor_tensor(qd[:, :, :], qd[:, :, :], qa[:, :, tok], ALU.mult).then_inc(s.end_scaled, 1)
            dve.wait_ge(s.masks, 1 + 2 * LEVELS)
            dve.wait_ge(s.zero, 2)
            for l in range(LEVELS):
                if l + 1 < LEVELS:
                    exponents(l + 1)
                scale(l)
                if l >= 1:
                    take(l - 1)
            take(LEVELS - 1)
            dve.wait_ge(s.scores, LEVELS + 1)
            dve.wait_ge(s.taken, 4 * LEVELS)
            for j in range(2):
                for o in range(2):
                    dve.copy_predicated(st[:, j, o, :, :],
                                        k.ident[:, :].bitcast(U32).unsqueeze(1).to_broadcast([P, NCH, CH]),
                                        bank(j, o, LEVELS).rearrange("p (c w) -> p c w", c=NCH)).then_inc(s.taken, 1)
            for c in range(NCH):
                for j in range(2):
                    dve.wait_ge(s.su, 2 * c + j + 1)
                    if c > 0:
                        dve.wait_ge(s.s_done, 4 * c)
                    for o in range(2):
                        r = slice(HW * o, HW * (o + 1))
                        dve.scalar_tensor_tensor(out=s2[r, j, r], in0=s2[r, j, r], scalar=keep[r, j, c:c + 1],
                                                 in1=k.ps[1][r, j, HW * o:HW * (o + 1)], op0=ALU.mult, op1=ALU.add)\
                            .then_inc(s.s_done, 1)

        @block.scalar
        def _(act):
            nc.scalar.preload_act_table_set("exp_and_others")
            nc.scalar.activation(qd[:, :, :], b[:, :, tok], ACT.Exp).then_inc(s.end_exp, 1)
            act.wait_ge(s.ends, 1)
            nc.scalar.activation(kd[:, :, :], kd[:, :, :], ACT.Exp).then_inc(s.end_exp, 1)
            for l in range(LEVELS):
                act.wait_ge(s.diff, 2 * l + 2)
                nc.scalar.activation(e[:, l % 2, :, :], e[:, l % 2, :, :], ACT.Exp).then_inc(s.exps, 1)
                if l < 2:
                    act.wait_ge(s.v_turned, l + 1)
                    nc.scalar.copy(vt[:, l, :, :], k.ps[2 + l][:, 0, :].rearrange("p (c n) -> p c n", c=NCH))\
                        .then_inc(s.v_done, 1)
                    act.wait_ge(s.k_turned, l + 1)
                    nc.scalar.copy(kt[:, l, :, :], k.ps[2 + l][:, 1, :].rearrange("p (c n) -> p c n", c=NCH))\
                        .then_inc(s.k_done, 1)
            for c in range(NCH):
                act.wait_ge(s.o_ready, c + 1)
                nc.scalar.copy(va[:, :, S0 + CH * c:S0 + CH * (c + 1)], k.ps[0][:, :, 0:CH]).then_inc(s.o_done, 1)

        @block.tensor
        def _(pe):
            for j in range(2):
                for c in range(NCH):
                    mm = pe.transpose(k.ps[2 + j][:, 0, CH * c:CH * (c + 1)], va[:, j, S0 + CH * c:S0 + CH * (c + 1)],
                                      k.ident[:, :])
                mm.then_inc(s.v_turned, 1)
            pe.wait_ge(s.end_scaled, 1)
            for j in range(2):
                for c in range(NCH):
                    mm = pe.transpose(k.ps[2 + j][:, 1, CH * c:CH * (c + 1)], kd[:, j, CH * c:CH * (c + 1)],
                                      k.ident[:, :])
                mm.then_inc(s.k_turned, 1)
            for l in range(LEVELS):
                hf, bl = 1 << l, 2 << l
                pe.wait_ge(s.scaled, 2 * l + 2)
                if l == 1:
                    pe.wait_ge(s.v_done, 2)
                    pe.wait_ge(s.k_done, 2)
                if l >= 2:
                    pe.wait_ge(s.taken, 4 * (l - 1))
                for j in range(2):
                    for c in range(NCH):
                        for o in range(2):
                            r = slice(HW * o, HW * (o + 1))
                            v = e[r, l % 2, j, CH * c:CH * (c + 1)]
                            mm = pe.matmul(bank(j, o, l)[:, CH // 2 * c:CH // 2 * (c + 1)], v,
                                           v.rearrange("p (b w) -> p b w", w=bl)[:, :, hf:bl], start=True, stop=True)
                mm.then_inc(s.scores, 1)
            pe.wait_ge(s.taken, 4 * (LEVELS - 1))
            for j in range(2):
                for c in range(NCH):
                    for o in range(2):
                        r, t = slice(HW * o, HW * (o + 1)), slice(S0 + CH * c, S0 + CH * (c + 1))
                        mm = pe.matmul(bank(j, o, LEVELS)[:, CH * c:CH * (c + 1)], ka[r, j, t], qa[r, j, t],
                                       start=True, stop=True)
            mm.then_inc(s.scores, 1)
            pe.wait_ge(s.end_scaled, 2)
            pe.wait_ge(s.taken, 4 * (LEVELS + 1))
            for c in range(NCH):
                if c > 0:
                    pe.wait_ge(s.o_done, c)
                    pe.wait_ge(s.s_done, 4 * c)
                for j in range(2):
                    pe.matmul(k.ps[0][:, j, 0:CH], s2[:, j, :], qd[:, j, CH * c:CH * (c + 1)], start=True, stop=False,
                              skip_group_check=True)
                    for o in range(2):
                        r = slice(HW * o, HW * (o + 1))
                        mm = pe.matmul(k.ps[0][r, j, 0:CH], vt[:, j, c, r], st[:, j, o, c, :], start=False, stop=True,
                                       skip_group_check=True)
                mm.then_inc(s.o_ready, 1)
                for j in range(2):
                    pe.matmul(k.ps[1][:, j, 0:P], kt[:, j, c, :], vt[:, j, c, :], start=True, stop=True)\
                        .then_inc(s.su, 1)


WINDOWS = (2, 4, 8, 16)


def pooling(k, u, pool_w, pool_scale):
    nc = k.nc
    with ExitStack() as ctx:
        sb = lambda nm, shape, dt=F32: ctx.enter_context(nc.sbuf_tensor(f"pl_{nm}", shape, dt))
        w, sc = sb("w", [P, 2, P]), sb("sc", [P, 2])
        a, c = sb("a", [P, 2, T]), sb("c", [P, 2, T])
        head = sb("head", [P, 2, META])
        cnt_i, cnt = sb("cnt_i", [P, META], mybir.dt.int32), sb("cnt", [P, 2, META])
        w_zero, w_in, sc_in, count, chain = (k.sem(f"pl_{x}") for x in ("w_zero", "w_in", "sc_in", "count", "chain"))
        pooled, mixed, left = k.sem("pl_pooled"), k.sem("pl_mixed"), k.sem("pl_left")
        group = lambda g: (slice(HW * (g % 2), HW * (g % 2) + HW), g // 2)
        block = ctx.enter_context(stage(k))

        @block.gpsimd
        def _(pool):
            nc.gpsimd.iota(cnt_i[:, :], pattern=[[1, META]], base=1, channel_multiplier=0).then_inc(count, 1)
            pool.memset(w[:, :, :], 0.0).then_inc(w_zero, 1)

        @block.sync
        def _(sp):
            sp.wait_ge(w_zero, 1)
            for g in range(4):
                r, j = group(g)
                sp.dma_start(w[r, j, r], pool_w[g]).then_inc(w_in, 16)
            with nc.allow_non_contiguous_dma(reason="256 scales, feature on partitions"):
                sp.dma_start(sc[:, :], pool_scale.rearrange("(t p) -> p t", p=P)).then_inc(sc_in, 16)

        @block.vector
        def _(dve):
            link = linked(dve, chain)
            link(dve.memset(u[:, :, 0:S0], 0.0))
            link(dve.memset(a[:, :, 0:S0], 0.0))
            link(dve.memset(c[:, :, 0:S0], 0.0))
            dve.wait_ge(count, 1)
            for g, win in enumerate(WINDOWS):
                r, j = group(g)
                link(dve.tensor_copy(cnt[r, j, :], cnt_i[r, :]))
                link(dve.tensor_scalar(cnt[r, j, :], cnt[r, j, :], float(win), None, ALU.min))
            link(dve.reciprocal(cnt[:, :, :], cnt[:, :, :]))
            src, dst = u, a
            for n, win in enumerate(WINDOWS):
                d = win // 2
                for j in range(n // 2, 2):
                    r = slice(0, P) if 2 * j >= n else slice(HW, P)
                    link(dve.tensor_tensor(dst[r, j, S0:T], src[r, j, S0:T], src[r, j, S0 - d:T - d], ALU.add))
                r, j = group(n)
                link(dve.tensor_tensor(head[r, j, :], dst[r, j, S0:S0 + META], cnt[r, j, :], ALU.mult))
                if n < 3:
                    src, dst = dst, (c if dst is a else a)
            for g, win in enumerate(WINDOWS):
                r, j = group(g)
                v = a if g % 2 == 0 else c
                link(dve.scalar_tensor_tensor(out=v[r, j, S0 + META:T], in0=v[r, j, S0 + META:T], scalar=1.0 / win,
                                              in1=u[r, j, S0 + META:T], op0=ALU.mult, op1=ALU.subtract))
                link(dve.tensor_tensor(v[r, j, S0:S0 + META], head[r, j, :], u[r, j, S0:S0 + META], ALU.subtract))
            for j in range(2):
                dve.tensor_copy(a[HW:P, j, S0:T], c[HW:P, j, S0:T]).then_inc(pooled, 1)

        @block.tensor
        def _(pe):
            pe.wait_ge(w_in, 64)
            pe.wait_ge(pooled, 2)
            for j in range(2):
                for b in range(2):
                    half = slice(S0 + b * (SEQ // 2), S0 + (b + 1) * (SEQ // 2))
                    mm = pe.matmul(k.ps[j][:, b, 0:SEQ // 2], w[:, j, :], a[:, j, half], start=True, stop=True)
                mm.then_inc(mixed, 1)

        @block.scalar
        def _(act):
            act.wait_ge(sc_in, 16)
            for j in range(2):
                act.wait_ge(mixed, j + 1)
                nc.scalar.activation(two(u[:, j, S0:T]), k.ps[j][:, :, 0:SEQ // 2], ACT.Copy,
                                     scale=sc[:, j:j + 1]).then_inc(left, 1)


class FoxGates:

    slot1 = False

    def __init__(self, negc, w_in, bias):
        self.negc, self.w_in, self.bias = negc, w_in, bias

    def open(self, k, ctx):
        sb = lambda nm, shape: ctx.enter_context(k.nc.sbuf_tensor(f"fg_{nm}", shape, F32))
        self.s = gate_rows(k, "fg", ctx, [(self.w_in, 0)], FH)
        self.bi, self.f, self.e, self.one = sb("bias", [FH, 1]), sb("f", [FH, T]), sb("e", [FH, T]), sb("one", [FH, SEQ])
        self.bias_in, self.a, self.v = k.sem("fg_bias_in"), k.sem("fg_act"), k.sem("fg_dve")

    def sync(self, k, sp):
        with k.nc.allow_non_contiguous_dma(reason="a few gate weights and parameters"):
            sp.dma_start(self.bi[:, :], self.bias.rearrange("(h o) -> h o", o=1)).then_inc(self.bias_in, 16)
            gate_load(k, sp, self.s)

    def free(self, k, pe):
        pe.wait_ge(self.v, 2)

    def free1(self, k, pe):
        pass

    def pe(self, k, pe, n):
        if n == 1:
            gate_product(k, pe, self.s, k.ps[3])

    def act(self, k, act, n):
        a, e = self.a, self.e
        if n == 0:
            gate_hi(k, act, self.s)
        if n == 1:
            act.wait_ge(self.v, 2)
            k.nc.scalar.activation(e[:, :], self.f[:, :], ACT.Abs).then_inc(a, 1)
            act.wait_ge(a, 1)
            k.nc.scalar.activation(e[:, :], e[:, :], ACT.Exp, scale=-1.0).then_inc(a, 1)
            act.wait_ge(a, 2)
            k.nc.scalar.activation(e[:, :], e[:, :], ACT.Ln, bias=k.ones[0:FH, 0:1]).then_inc(a, 1)

    def dve(self, k, dve, n):
        f, e, v = self.f, self.e, self.v
        if n == -1:
            gate_clear(k, dve, self.s)
            dve.memset(self.one[:, :], 1.0).then_inc(v, 1)
        if n == 0:
            gate_lo(k, dve, self.s)
        if n == 1:
            dve.wait_ge(self.s.ready, 1)
            dve.wait_ge(self.bias_in, 16)
            dve.tensor_scalar(two(f[:, :]), halves(k.ps[3], FH), self.bi[:, 0:1], None, ALU.add).then_inc(v, 1)
            dve.wait_ge(self.a, 3)
            dve.wait_ge(v, 2)
            dve.tensor_scalar(f[:, :], f[:, :], 0.0, -1.0, ALU.min, ALU.mult).then_inc(v, 1)
            dve.wait_ge(v, 3)
            dve.tensor_tensor(f[:, :], f[:, :], e[:, :], ALU.add).then_inc(v, 1)
            dve.wait_ge(v, 4)
            dve.tensor_tensor_scan(self.negc[:, :], self.one[:, :], f[:, S0:T], 0.0, ALU.mult, ALU.add).then_inc(v, 1)


def fox(k, qc, kc, vc, negc):
    nc = k.nc
    with ExitStack() as ctx:
        sb = lambda nm, shape: ctx.enter_context(nc.sbuf_tensor(f"fx_{nm}", shape, F32))
        nb = sb("nb", [P, FH, SEQ])
        vt = sb("vt", [P, NCH, FH, HW])
        above = sb("above", [P, CH])
        sc, pt = sb("sc", [P, 4, SEQ]), sb("pt", [P, 2, SEQ])
        mx, sm = sb("mx", [P, NCH * FH, 2]), sb("sm", [P, NCH, FH])
        o = sb("o", [P, 2, FH, HW])
        names = ("masks", "bcast", "nb_done", "v_turned", "v_done", "scores", "maxed", "negated", "probs", "p_turned",
                 "p_done", "o_ready", "inverse", "o_done", "o_turned", "out_done")
        s = Named(**{x: k.sem(f"fx_{x}") for x in names})
        score = [k.ps[i // 2][:, i % 2, :] for i in range(4)]
        turned = [k.ps[2][:, i, :] for i in range(2)]
        o_bank, ot_bank = k.ps[3][:, 0, :], k.ps[3][:, 1, :]
        steps_ = [(c, h) for c in range(NCH) for h in range(FH)]
        block = ctx.enter_context(stage(k))

        @block.gpsimd
        def _(pool):
            pool.memset(above[:, :], 0.0).then_inc(s.masks, 1)
            pool.wait_ge(s.masks, 1)
            nc.gpsimd.affine_select(out=above[:, :], in_=above[:, :], compare_op=ALU.is_ge, fill=-1e30, base=0,
                                    pattern=[[-1, CH]], channel_multiplier=1).then_inc(s.masks, 1)

        @block.tensor
        def _(pe):
            for h in range(FH):
                if h >= 2:
                    pe.wait_ge(s.nb_done, h - 1)
                pe.matmul(turned[h % 2], k.ident[0:FH, h:h + 1].to_broadcast([FH, P]), negc[:, :], start=True,
                          stop=True).then_inc(s.bcast, 1)
            for c in range(NCH):
                if c >= 2:
                    pe.wait_ge(s.v_done, c - 1)
                for j in range(4):
                    mm = pe.transpose((o_bank, ot_bank)[c % 2][:, P * j:P * (j + 1)],
                                      vc[:, j, S0 + CH * c:S0 + CH * (c + 1)], k.ident[:, :])
                mm.then_inc(s.v_turned, 1)
            pe.wait_ge(s.masks, 2)

            def scores(i):
                c, h = steps_[i]
                r, n = slice(HW * (h % 2), HW * (h % 2) + HW), CH * (c + 1)
                if i >= 4:
                    pe.wait_ge(s.maxed, i - 3)
                pe.matmul(score[h % 4][:, 0:n], qc[r, h // 2, S0 + CH * c:S0 + n], kc[r, h // 2, S0:S0 + n],
                          start=True, stop=False)
                pe.matmul(score[h % 4][:, n - CH:n], k.ident[:, :], above[:, :], start=False, stop=True)\
                    .then_inc(s.scores, 1)

            def turn(i):
                c, h = steps_[i]
                pe.wait_ge(s.probs, i + 1)
                if i >= 2:
                    pe.wait_ge(s.p_done, i - 1)
                elif i == 0:
                    pe.wait_ge(s.nb_done, FH)
                for b in range(c + 1):
                    mm = pe.transpose(turned[i % 2][:, CH * b:CH * (b + 1)], sc[:, i % 4, CH * b:CH * (b + 1)],
                                      k.ident[:, :])
                mm.then_inc(s.p_turned, 1)

            def values(i):
                c, h = steps_[i]
                pe.wait_ge(s.p_done, i + 1)
                if h == 0:
                    pe.wait_ge(s.v_done, NCH)
                    if c > 0:
                        pe.wait_ge(s.o_done, c)
                for b in range(c + 1):
                    mm = pe.matmul(o_bank[:, HW * h:HW * (h + 1)], pt[:, i % 2, CH * b:CH * (b + 1)],
                                   vt[:, b, h, :], start=b == 0, stop=b == c)
                mm.then_inc(s.o_ready, 1)
                if h == FH - 1:
                    pe.wait_ge(s.o_done, c + 1)
                    if c > 0:
                        pe.wait_ge(s.out_done, c)
                    for j in range(4):
                        mm = pe.transpose(ot_bank[:, P * j:P * (j + 1)],
                                          o[:, c % 2, 2 * j:2 * j + 2, :].rearrange("p h d -> p (h d)"),
                                          k.ident[:, :])
                    mm.then_inc(s.o_turned, 1)

            n = len(steps_)
            for i in range(n + 3):
                if i < n:
                    scores(i)
                if 2 <= i < n + 2:
                    turn(i - 2)
                if i >= 3:
                    values(i - 3)

        @block.vector
        def _(dve):
            for c in range(NCH):
                dve.wait_ge(s.v_turned, c + 1)
                dve.tensor_copy(vt[:, c, :, :].rearrange("p h d -> p (h d)"), (o_bank, ot_bank)[c % 2])\
                    .then_inc(s.v_done, 1)
            dve.wait_ge(s.nb_done, FH)
            def top(i):
                c, h = steps_[i]
                n = CH * (c + 1)
                dve.wait_ge(s.scores, i + 1)
                if i >= 4:
                    dve.wait_ge(s.p_turned, i - 3)
                dve.tensor_tensor_reduce(out=sc[:, i % 4, 0:n], in0=score[h % 4][:, 0:n], in1=nb[:, h, 0:n], scale=1.0,
                                         scalar=-3e38, op0=ALU.add, op1=ALU.max, accum_out=mx[:, i, 0:1])\
                    .then_inc(s.maxed, 1)
                dve.wait_ge(s.maxed, i + 1)
                dve.tensor_scalar(mx[:, i, 1:2], mx[:, i, 0:1], -1.0, None, ALU.mult).then_inc(s.negated, 1)
            def out(c):
                dve.wait_ge(s.probs, FH * (c + 1))
                dve.reciprocal(sm[:, c, :], sm[:, c, :]).then_inc(s.inverse, 1)
                dve.wait_ge(s.inverse, c + 1)
                dve.wait_ge(s.o_ready, FH * (c + 1))
                if c >= 2:
                    dve.wait_ge(s.o_turned, c - 1)
                dve.tensor_tensor(o[:, c % 2, :, :], o_bank.rearrange("p (h d) -> p h d", d=HW),
                                  sm[:, c, :].unsqueeze(2).to_broadcast([P, FH, HW]), ALU.mult).then_inc(s.o_done, 1)
            n = len(steps_)
            for i in range(n + 4):
                if i < n:
                    top(i)
                if i >= 3 and i - 3 < n and (i - 3) % FH == FH - 1:
                    out((i - 3) // FH)

        @block.scalar
        def _(act):
            nc.scalar.preload_act_table_set("exp_and_others")
            for h in range(FH):
                act.wait_ge(s.bcast, h + 1)
                nc.scalar.copy(nb[:, h, :], turned[h % 2]).then_inc(s.nb_done, 1)
            def probs(i):
                c, h = steps_[i]
                n = CH * (c + 1)
                act.wait_ge(s.negated, i + 1)
                nc.scalar.activation(sc[:, i % 4, 0:n], sc[:, i % 4, 0:n], ACT.Exp, bias=mx[:, i, 1:2],
                                     accum_out=sm[:, c, h:h + 1]).then_inc(s.probs, 1)
            def take(i):
                c, h = steps_[i]
                act.wait_ge(s.p_turned, i + 1)
                nc.scalar.copy(pt[:, i % 2, 0:CH * (c + 1)], turned[i % 2][:, 0:CH * (c + 1)]).then_inc(s.p_done, 1)
            def out(c):
                act.wait_ge(s.o_turned, c + 1)
                nc.scalar.copy(qc[:, :, S0 + CH * c:S0 + CH * (c + 1)], ot_bank.rearrange("p (j n) -> p j n", j=4))\
                    .then_inc(s.out_done, 1)
            n = len(steps_)
            for i in range(n + 2):
                if i < n:
                    probs(i)
                if 1 <= i <= n:
                    take(i - 1)
                if i >= 2 and (i - 2) % FH == 3 and i - 2 >= FH:
                    out((i - 2) // FH - 1)
            out(NCH - 1)


def add_normed(k, name, y, gain_row):
    nc = k.nc
    norm = RmsNorm(name, y, gain_row)
    with ExitStack() as ctx:
        norm.open(k, ctx)
        scaled, added = k.sem(f"{name}_y_scaled"), k.sem(f"{name}_added")
        block = ctx.enter_context(stage(k))

        @block.sync
        def _(sp):
            norm.sync(k, sp)

        @block.scalar
        def _(act):
            norm.act_sum(k, act)
            norm.act_root(k, act)

        @block.tensor
        def _(pe):
            norm.pe(k, pe)

        @block.vector
        def _(dve):
            norm.dve_sum(k, dve)
            dve.wait_ge(norm.gain_in, 16)
            dve.wait_ge(norm.inv, 1)
            def add(t):
                dve.wait_ge(scaled, t + 1)
                dve.tensor_tensor(k.h[:, t, S0:T], k.h[:, t, S0:T], y[:, t, S0:T], ALU.add).then_inc(added, 1)
            for t in range(KD):
                dve.scalar_tensor_tensor(out=y[:, t, S0:T], in0=y[:, t, S0:T], scalar=norm.gain[:, t:t + 1],
                                         in1=norm.rinv[:, S0:T], op0=ALU.mult, op1=ALU.mult).then_inc(scaled, 1)
                if t >= 1:
                    add(t - 1)
            add(KD - 1)


SEC_COLS = (0, 256, 512, 1024, 1536, 1792, 2048, 2304, 2560, 2816)


def second_unit(ins):
    return lambda u: tall(ins["w_in_2"][0], SEC_COLS[u])


def second(k, ins):
    nc = k.nc
    w = ins["w_in_2"][0]
    with ExitStack() as c:
        sb = lambda nm, shape: c.enter_context(nc.sbuf_tensor(f"sec_{nm}", shape, F32))
        split_rings(k, "sec", c)
        negc = sb("negc", [FH, SEQ])
        gate_unit = lambda g, j: tall(w, ((768, 1280), (3072, 3328))[g][j])
        mix = sb("mix", [P, KD, T])
        ones2 = sb("ones2", [P, P])
        with ExitStack() as c2:
            rest = c2.enter_context(nc.sbuf_tensor("sec_rest", [P, 12, T], F32))
            place = ((rest, 0), (rest, 2), (mix, 0), (mix, 2), (mix, 4), (mix, 6), (rest, 4), (rest, 6), (rest, 8),
                     (rest, 10))
            with ExitStack() as cb:
                b = cb.enter_context(nc.sbuf_tensor("sec_b", [P, 2, T], F32))
                with ExitStack() as c3:
                    weight_ring(k, "secp", c3)
                    def dst(j):
                        buf, t = place[j // 2]
                        return buf[:, t + j % 2, :]
                    leave = Store(dst, lambda j: HW ** -0.5 if 4 <= j // 2 < 6 else 1.0)
                    project(k, "sec_p", 10, second_unit(ins), leave,
                            RmsNorm("sec_in_norm", k.h, ins["pre_norm_g_2"][0]), first_units(gate_unit),
                            Both(FoxGates(negc, w[:, 3584:3584 + FH], ins["fox_f_bias_2"][0]),
                                 HgrnGates(rest[:, 0:2, :], rest[:, 2:4, :], b, ins["lower_bounds_2"], leave)))
                hgrn(k, rest[:, 0:2, :], rest[:, 2:4, :], mix[:, 0:2, :], b)
            pooling(k, mix[:, 2:4, :], ins["pool_w_2"][0], ins["pool_scale_2"][0])
            fox(k, mix[:, 4:8, :], rest[:, 4:8, :], rest[:, 8:12, :], negc)
        block_ones(k, ones2)
        head_norm(k, "sec_hn", 2, lambda j: mix[:, j, :], ones2[:, :], 1.0 / HW, lambda g, j: g[:, j:j + 1],
                  ins["hgrn_norm_g_2"][0].rearrange("(j p) -> p j", p=P))
        k.y = sb("y", [P, KD, T])
        with ExitStack() as c3:
            weight_ring(k, "seco", c3)
            up_down(k, "sec_out", 2, gate_unit, ins["w_out_2"][0],
                    SiluTimes(lambda g, m: mix[:, g * 4 + m, :]), k.y, True)
        add_normed(k, "sec_post", k.y, ins["post_norm_g_2"][0])


def block_ones(k, ones2):
    made = k.sem("ones2_made")
    with stage(k) as block:
        @block.gpsimd
        def _(pool):
            pool.memset(ones2[:, :], 0.0).then_inc(made, 1)
            pool.wait_ge(made, 1)
            for o in range(2):
                r = slice(HW * o, HW * (o + 1))
                pool.memset(ones2[r, r], 1.0).then_inc(made, 1)



_USED = ["x", "meta_tokens", "attn_norm", "ffn_norm", "ff_up", "ff_down", "gdn_in", "gdn_conv", "gdn_a_log",
         "gdn_dt_bias", "gdn_norm", "gdn_out", "mlstm_in", "mlstm_gate_bias", "mlstm_norm", "mlstm_out",
         "lower_bounds_2", "pre_norm_g_2", "w_in_2", "hgrn_norm_g_2", "fox_f_bias_2", "pool_w_2", "pool_scale_2",
         "w_out_2", "post_norm_g_2"]


def ffn_unit(ins, layer):
    return lambda g, j: tall(ins["ff_up"][layer], g * 512 + 256 * j)


def ffn(k, ins, layer, then=()):
    with ExitStack() as c:
        split_rings(k, f"ffn{layer}", c)
        weight_ring(k, f"ffn{layer}w", c)
        up_down(k, f"ffn{layer}", 8, ffn_unit(ins, layer), ins["ff_down"][layer], SquaredRelu(), k.h, False,
                RmsNorm(f"ffn{layer}_norm", k.h, ins["ffn_norm"][layer]), then)


def STAGES(k, ctx, ins):
    gdn(k, ins, first_units(ffn_unit(ins, 0)))
    ffn(k, ins, 0, [mlstm_unit(ins)(u) for u in range(4)])
    mlstm(k, ins, first_units(ffn_unit(ins, 1)))
    ffn(k, ins, 1, [second_unit(ins)(u) for u in range(4)])
    second(k, ins)
    k.y = k.h


def build(nc, ins, out):
    with ExitStack() as ctx:
        k = persistent(nc, ctx)
        load_tokens(k, ins["x"], ins["meta_tokens"])
        STAGES(k, ctx, ins)
        store_tokens(k, k.y, out)


_OUT = ((1, SEQ, D), "float32")


def kernel(**inputs):
    import numpy as _np
    import concourse.bacc as _bacc
    from concourse import mybir as _mybir
    from concourse.bass_utils import run_bass_kernel_spmd as _run

    nc = _bacc.Bacc("TRN2", target_bir_lowering=False, num_devices=1)
    arrays, args = {}, {}
    for name in _USED:
        a = _np.ascontiguousarray(inputs[name])
        arrays[f"in_{name}_dram"] = a
        args[name] = nc.dram_tensor(f"in_{name}_dram", a.shape, _mybir.dt.from_np(a.dtype), kind="ExternalInput").ap()
    out = nc.dram_tensor("out_dram", _OUT[0], _mybir.dt.from_np(_np.dtype(_OUT[1])), kind="ExternalOutput").ap()
    build(nc, args, out)
    r = _run(nc, [arrays], core_ids=[0])
    return r.results[0]["out_dram"]
```
